# Optimizing a Trainium2 kernel written in Bass

```python
import jax, jax.numpy as jnp
from jax import lax
import numpy as np

D_MODEL = 2048
BATCH = 1
SEQ = 256
DEPTH = 2

N_MEM = 256
HEAD_DIM = 128
N_MEM_HEADS = 4
MEM_W = N_MEM_HEADS * HEAD_DIM
MIX_W = D_MODEL - MEM_W
DN_HEADS = MIX_W // HEAD_DIM
DN_CHUNK = 64
CONV_W = 5
GM_GROUPS = MIX_W // HEAD_DIM
GM_CHUNK = 128
FFN_HIDDEN = 4 * D_MODEL
N_MIXERS = 2
N_DN_LAYERS = (DEPTH + 1) // 2
N_GM_LAYERS = DEPTH // 2
DN_IN = 4 * MIX_W + 4 * DN_HEADS + MEM_W
GM_IN = 2 * MIX_W + MEM_W
RMS_EPS = 1e-6
L2_EPS = 1e-6

kernel_name = "bidir_hybrid_deltanet_gmlp_memxattn"

def rmsnorm(x, g):
    x32 = x.astype(jnp.float32)
    y = x32 * lax.rsqrt(jnp.mean(jnp.square(x32), axis=-1, keepdims=True) + RMS_EPS)
    return (y * g.astype(jnp.float32)).astype(x.dtype)

def l2norm(x):
    x32 = x.astype(jnp.float32)
    return x32 * lax.rsqrt(jnp.sum(jnp.square(x32), axis=-1, keepdims=True) + L2_EPS)

def centred_depthwise_conv(x, w):
    c = x.shape[-1]
    return lax.conv_general_dilated(
        x, w[:, None, :].astype(x.dtype), window_strides=(1,),
        padding=[(CONV_W // 2, CONV_W // 2)],
        dimension_numbers=("NWC", "WIO", "NWC"), feature_group_count=c)

def chunk_gated_delta(q, k, v, g, beta):
    b_, s_, h_, dk = q.shape
    dv = v.shape[-1]
    n_ch, c = s_ // DN_CHUNK, DN_CHUNK

    def blocks(t):
        return jnp.moveaxis(t.reshape((b_, n_ch, c, h_) + t.shape[3:]), 3, 1)

    q, k, v, g, beta = blocks(q), blocks(k), blocks(v), blocks(g), blocks(beta)
    gc = jnp.cumsum(g, axis=-1)
    incl = jnp.tril(jnp.ones((c, c), dtype=bool))
    strict = jnp.tril(jnp.ones((c, c), dtype=bool), -1)
    diff = gc[..., :, None] - gc[..., None, :]
    decay = jnp.exp(jnp.where(incl, diff, -jnp.inf))
    kb = k * beta[..., None]
    a_low = jnp.where(strict, jnp.einsum("bhnid,bhnjd->bhnij", kb, k) * decay, 0.0)
    lower = a_low + jnp.eye(c, dtype=a_low.dtype)
    rhs = jnp.concatenate([v * beta[..., None], kb * jnp.exp(gc)[..., None]], axis=-1)
    sol = lax.linalg.triangular_solve(lower, rhs, left_side=True, lower=True,
                                      unit_diagonal=True)
    u, w = sol[..., :dv], sol[..., dv:]
    attn = jnp.einsum("bhnid,bhnjd->bhnij", q, k) * decay
    q_dec = q * jnp.exp(gc)[..., None]
    g_last = gc[..., -1:]
    k_dec = k * jnp.exp(g_last - gc)[..., None]
    chunk_decay = jnp.exp(g_last)[..., None]
    xs = tuple(jnp.moveaxis(t, 2, 0) for t in (u, w, q_dec, k_dec, attn, chunk_decay))

    def step(state, inp):
        u_n, w_n, qd_n, kd_n, at_n, cd_n = inp
        v_new = u_n - jnp.einsum("bhck,bhkv->bhcv", w_n, state)
        o = (jnp.einsum("bhck,bhkv->bhcv", qd_n, state)
             + jnp.einsum("bhij,bhjv->bhiv", at_n, v_new))
        state = state * cd_n + jnp.einsum("bhck,bhcv->bhkv", kd_n, v_new)
        return state, o

    state0 = jnp.zeros((b_, h_, dk, dv), jnp.float32)
    _, o = lax.scan(step, state0, xs)
    return jnp.transpose(o, (1, 0, 3, 2, 4)).reshape(b_, s_, h_, dv)

def deltanet_mixer(xn, w_in, conv_w, a_log, dt_bias, out_g):
    b_, s_, _ = xn.shape
    h_ = DN_HEADS
    proj = xn @ w_in
    qkv, z, a, bt, q_mem = jnp.split(
        proj, [3 * MIX_W, 4 * MIX_W, 4 * MIX_W + 2 * h_, 4 * MIX_W + 4 * h_], axis=-1)
    qkv = jax.nn.silu(centred_depthwise_conv(qkv, conv_w))
    q, k, v = jnp.split(qkv, 3, axis=-1)
    q = l2norm(q.reshape(b_, s_, h_, HEAD_DIM)) * (HEAD_DIM ** -0.5)
    k = l2norm(k.reshape(b_, s_, h_, HEAD_DIM))
    v = v.reshape(b_, s_, h_, HEAD_DIM).astype(jnp.float32)
    g = -jnp.exp(a_log.reshape(-1).astype(jnp.float32)) * jax.nn.softplus(
        a.astype(jnp.float32) + dt_bias.reshape(-1).astype(jnp.float32))
    beta = jax.nn.sigmoid(bt.astype(jnp.float32))
    o_f = chunk_gated_delta(q, k, v, g[..., :h_], beta[..., :h_])
    flip = lambda t: jnp.flip(t, axis=1)
    o_b = flip(chunk_gated_delta(flip(q), flip(k), flip(v),
                                 flip(g[..., h_:]), flip(beta[..., h_:])))
    o = rmsnorm(o_f + o_b, out_g) * jax.nn.silu(
        z.reshape(b_, s_, h_, HEAD_DIM).astype(jnp.float32))
    return o.reshape(b_, s_, MIX_W).astype(xn.dtype), q_mem

def spatial_gating_mixer(xn, w_in, v_g, w_s, b_s):
    b_, s_, _ = xn.shape
    proj = xn @ w_in
    u, v, q_mem = jnp.split(proj, [MIX_W, 2 * MIX_W], axis=-1)
    u = jax.nn.gelu(u)
    v = rmsnorm(jax.nn.gelu(v), v_g)
    v = v.reshape(b_, s_ // GM_CHUNK, GM_CHUNK, GM_GROUPS, HEAD_DIM)
    sg = (jnp.einsum("gij,bnjge->bnige", w_s.astype(v.dtype), v)
          + b_s.T[None, None, :, :, None].astype(v.dtype))
    return u * sg.reshape(b_, s_, MIX_W), q_mem

def memory_attention(q_mem, mem_n, w_kv):
    b_, s_, _ = q_mem.shape
    kv = mem_n @ w_kv
    k, v = jnp.split(kv, 2, axis=-1)
    k = k.reshape(b_, -1, N_MEM_HEADS, HEAD_DIM).astype(jnp.float32)
    v = v.reshape(b_, -1, N_MEM_HEADS, HEAD_DIM).astype(jnp.float32)
    q = q_mem.reshape(b_, s_, N_MEM_HEADS, HEAD_DIM).astype(jnp.float32)
    scores = jnp.einsum("bshd,bmhd->bhsm", q, k) * (HEAD_DIM ** -0.5)
    p = jax.nn.softmax(scores, axis=-1)
    o = jnp.einsum("bhsm,bmhd->bshd", p, v)
    return o.reshape(b_, s_, MEM_W).astype(q_mem.dtype)

def setup_inputs(seed: int = 0) -> dict:
    key = jax.random.key(seed)
    ks = jax.random.split(key, 24)
    f32 = jnp.float32
    nrm = lambda k, shape, scale: jax.random.normal(k, shape, f32) * scale
    gain = lambda k, shape: 1.0 + 0.05 * jax.random.normal(k, shape, f32)
    dt = jnp.exp(jax.random.uniform(ks[5], (N_DN_LAYERS, 2, DN_HEADS), f32)
                 * (np.log(0.1) - np.log(0.001)) + np.log(0.001))
    return {
        "x": nrm(ks[0], (BATCH, SEQ, D_MODEL), 1.0),
        "mem": nrm(ks[1], (BATCH, N_MEM, D_MODEL), 1.0),
        "mem_norm_g": gain(ks[2], (D_MODEL,)),
        "tok_norm_g": gain(ks[3], (DEPTH, D_MODEL)),
        "dn_w_in": nrm(ks[4], (N_DN_LAYERS, D_MODEL, DN_IN), D_MODEL ** -0.5),
        "dn_conv_w": nrm(ks[6], (N_DN_LAYERS, CONV_W, 3 * MIX_W), CONV_W ** -0.5),
        "dn_a_log": jnp.log(jax.random.uniform(ks[7], (N_DN_LAYERS, 2, DN_HEADS), f32, 1.0, 16.0)),
        "dn_dt_bias": dt + jnp.log(-jnp.expm1(-dt)),
        "dn_out_norm_g": gain(ks[8], (N_DN_LAYERS, HEAD_DIM)),
        "gm_w_in": nrm(ks[9], (N_GM_LAYERS, D_MODEL, GM_IN), D_MODEL ** -0.5),
        "gm_v_norm_g": gain(ks[10], (N_GM_LAYERS, MIX_W)),
        "gm_w_s": nrm(ks[11], (N_GM_LAYERS, GM_GROUPS, GM_CHUNK, GM_CHUNK), 0.5 * GM_CHUNK ** -0.5),
        "gm_b_s": gain(ks[12], (N_GM_LAYERS, GM_GROUPS, GM_CHUNK)),
        "mem_w_kv": nrm(ks[13], (DEPTH, D_MODEL, 2 * MEM_W), D_MODEL ** -0.5),
        "tok_w_out": nrm(ks[14], (DEPTH, MIX_W + MEM_W, D_MODEL), (MIX_W + MEM_W) ** -0.5),
        "ffn_norm_g": gain(ks[15], (DEPTH, D_MODEL)),
        "ffn_w1": nrm(ks[16], (DEPTH, D_MODEL, FFN_HIDDEN), D_MODEL ** -0.5),
        "ffn_w2": nrm(ks[17], (DEPTH, FFN_HIDDEN, D_MODEL), FFN_HIDDEN ** -0.5),
        "final_norm_g": gain(ks[18], (D_MODEL,)),
    }

def reference(x, mem, mem_norm_g, tok_norm_g, dn_w_in, dn_conv_w, dn_a_log, dn_dt_bias,
              dn_out_norm_g, gm_w_in, gm_v_norm_g, gm_w_s, gm_b_s, mem_w_kv, tok_w_out,
              ffn_norm_g, ffn_w1, ffn_w2, final_norm_g):
    mem_n = rmsnorm(mem, mem_norm_g)
    h = x
    for layer in range(DEPTH):
        j = layer // N_MIXERS
        xn = rmsnorm(h, tok_norm_g[layer])
        if layer % N_MIXERS == 0:
            mix, q_mem = deltanet_mixer(xn, dn_w_in[j], dn_conv_w[j], dn_a_log[j],
                                        dn_dt_bias[j], dn_out_norm_g[j])
        else:
            mix, q_mem = spatial_gating_mixer(xn, gm_w_in[j], gm_v_norm_g[j],
                                              gm_w_s[j], gm_b_s[j])
        mo = memory_attention(q_mem, mem_n, mem_w_kv[layer])
        h = h + jnp.concatenate([mix, mo], axis=-1) @ tok_w_out[layer]
        hn = rmsnorm(h, ffn_norm_g[layer])
        h = h + jnp.square(jax.nn.relu(hn @ ffn_w1[layer])) @ ffn_w2[layer]
    return rmsnorm(h, final_norm_g)


_drawn_inputs = setup_inputs


def setup_inputs(seed=0):
    import zlib

    import numpy as np

    out = dict(_drawn_inputs(seed))
    spreads = {}
    factors = {'mem_norm_g': 8.0, 'gm_v_norm_g': 21.964, 'gm_b_s': 11.13, 'dn_out_norm_g': 3.748}
    for name, (base, spread) in spreads.items():
        noise = np.random.default_rng([zlib.crc32(name.encode()), seed]).standard_normal(out[name].shape)
        drawn = base * np.exp(spread * noise) if base else spread * noise
        out[name] = __import__('jax').numpy.asarray(drawn.astype(out[name].dtype))
    for name, factor in factors.items():
        out[name] = (out[name] * factor).astype(out[name].dtype)
    return out
```

```python
from contextlib import ExitStack

import numpy as np

import concourse.bass as bass
from concourse import mybir

F32 = mybir.dt.float32
F32R = mybir.dt.float32r
ACT = mybir.ActivationFunctionType
ALU = mybir.AluOpType
AX = mybir.AxisListType

P = 128
D = 2048
SEQ = 256
HD = 128
NH = 12
MIX = NH * HD
CONV = 5
CHUNK = 64
HID = 8192
NB = 512
KT = D // P
SLABS = 8
EPS = 1e-6
LEVELS = (2, 4, 8, 16, 32)
BIG = 1e30

C_ID, C_UP, C_LO, C_BLK, C_SEL, C_BIGF, C_BIGB, C_M1L, C_M1T, C_LEV, C_ONE = (
    0, 128, 256, 384, 512, 768, 896, 1024, 1152, 1280, 1600)
C_ALL = 1728

G_G, G_GC, G_EGC, G_EKD, G_BETA, G_CD = 0, 2, 4, 6, 8, 10
G_ROWS = 14


def shape_constants():
    i = np.arange(P)
    same = (i[:, None] // CHUNK) == (i[None, :] // CHUNK)
    c = np.zeros((P, C_ALL), np.float32)
    c[:, C_ID:C_ID + P] = np.eye(P)
    c[:, C_UP:C_UP + P] = same & (i[:, None] <= i[None, :])
    c[:, C_LO:C_LO + P] = same & (i[:, None] >= i[None, :])
    c[:, C_BLK:C_BLK + P] = same
    for h in range(2):
        c[:, C_SEL + h * P:C_SEL + (h + 1) * P] = (i[:, None] // CHUNK) == h
    c[:, C_BIGF:C_BIGF + P] = np.where(same & (i[:, None] <= i[None, :]), 0.0, BIG)
    c[:, C_BIGB:C_BIGB + P] = np.where(same & (i[:, None] >= i[None, :]), 0.0, BIG)
    first = (i[:, None] % 2 == 1) & (i[None, :] == i[:, None] - 1)
    c[:, C_M1L:C_M1L + P] = -first.astype(np.float32)
    c[:, C_M1T:C_M1T + P] = -first.T.astype(np.float32)
    j = np.arange(CHUNK)
    for n, s in enumerate(LEVELS):
        ok = (i[:, None] // (2 * s) == j[None, :] // s) & ((i[:, None] // s) % 2 == 1)
        c[:, C_LEV + n * CHUNK:C_LEV + (n + 1) * CHUNK] = ok
    c[:, C_ONE:C_ONE + P] = 1.0
    return c


R_KV, R_DN, R_QM, R_OUT = 0, 4, 16, (17, 52)
R_FFN = (21, 56)
R_GM = 45
R_END = 80
B_DN, B_QM, B_GM = 4, 16, 53
B_OUT = (17, 60)
B_FFN = (21, 64)
B_LAST = 95

A_SMALL, A_MEMN, A_KT, A_XN, A_GATE = 0, 2, 10, 14, 22
A_DN = 24
DN_AUX = 88
(DA, DD, DE, DF, DG, DH, DI, DJ, DK) = (0, 6, 12, 16, 20, 24, 28, 56, 68)
A_ATT0 = A_DN + 3 * DN_AUX
A_MIX0 = A_ATT0 + 12
A_FN0 = A_MIX0 + 6
A_FFN0 = A_FN0 + 8
A_TN1 = A_FFN0 + 32
A_WS = A_TN1 + 8
A_SG = A_WS + 3
A_ATT1 = A_SG + 6
A_MIX1 = A_ATT1 + 12
A_FN1 = A_MIX1 + 6
A_FFN1 = A_FN1 + 8
A_FFN = (A_FFN0, A_FFN1)

X_MEM, X_X, X_MIX0, X_FN0, X_TN1, X_MIX1, X_FN1 = range(7)

GN_MEM, GN_TOK, GN_FFN, GN_OUT, GN_BS = 0, 16, 48, 80, 81
N_SMALL = 93


def level_aux(l, direction, what):
    base = DI + 6 * l
    if l < len(LEVELS) - 1:
        return base + {("Y", 0): 0, ("Y", 1): 1, ("XY", 0): 2, ("YX", 0): 3, ("XY", 1): 4, ("YX", 1): 5}[what, direction]
    return base + {("Y", 0): 0, ("Y", 1): 1, ("YX", 0): 2, ("XY", 1): 3}[what, direction]


def step_aux(t, direction, what):
    base = DK + (0, 4, 10, 16)[t]
    if t == 0:
        return base + {("O", 0): 0, ("K", 0): 1, ("O", 1): 2, ("K", 1): 3}[what, direction]
    if t < 3:
        return base + {("W", 0): 0, ("W", 1): 1, ("O", 0): 2, ("K", 0): 3, ("O", 1): 4, ("K", 1): 5}[what, direction]
    return base + {("W", 0): 0, ("W", 1): 1, ("O", 0): 2, ("O", 1): 3}[what, direction]


def encoder_trunk(nc, x, mem, consts, mem_norm_g, tok_norm_g, dn_w_in, dn_conv_w, dn_a_log, dn_dt_bias,
                  dn_out_norm_g, gm_w_in, gm_v_norm_g, gm_w_s, gm_b_s, mem_w_kv, tok_w_out, ffn_norm_g,
                  ffn_w1, ffn_w2, final_norm_g, out):
    ctx = ExitStack()
    sem_of = {}

    def sem(name):
        if name not in sem_of:
            sem_of[name] = ctx.enter_context(nc.semaphore(name))
        return sem_of[name]

    def sb(stack, name, shape, dt=F32):
        return stack.enter_context(nc.sbuf_tensor(name, shape, dt))

    with ctx:
        cst = sb(ctx, "cst", [P, C_ALL])
        raw = sb(ctx, "raw", [P, 4, 2, NB])
        w_hi = sb(ctx, "w_hi", [P, 2, 2, NB], F32R)
        w_lo = sb(ctx, "w_lo", [P, 2, 2, NB], F32R)
        xT_hi = sb(ctx, "xT_hi", [P, KT, SEQ], F32R)
        xT_lo = sb(ctx, "xT_lo", [P, KT, SEQ], F32R)
        h = sb(ctx, "h", [P, 2, D])
        memKT = sb(ctx, "memKT", [P, 2, 4, SEQ])
        memV = sb(ctx, "memV", [P, 2, 2, NB])
        mix = sb(ctx, "mix", [P, 2, MIX])
        gains = sb(ctx, "gains", [P, N_SMALL])
        conv_w = sb(ctx, "conv_w", [P, 180])
        stat = sb(ctx, "stat", [P, 4])
        rstd = sb(ctx, "rstd", [P, 2])
        neg_half = sb(ctx, "neg_half", [P, 8])
        zeros = sb(ctx, "zeros", [P, CHUNK])
        banks = [ctx.enter_context(nc.psum_tensor(f"pair{i}", [P, NB], F32)) for i in range(4)]
        aux = [ctx.enter_context(nc.psum_tensor(f"aux{i}", [P, NB], F32)) for i in range(4)]

        dn = ExitStack()
        r1 = sb(dn, "r1", [P, 6192])
        tok = sb(dn, "tok", [P, 3, 2, NB])
        kqT = sb(dn, "kqT", [P, 2, 4, SEQ])
        Y = sb(dn, "Y", [P, 2, 8, P])
        attnT = sb(dn, "attnT", [P, 2, 2, 4, P])
        S = sb(dn, "S", [P, 2, 4, P])
        vn = sb(dn, "vn", [P, 2, 2, 4, P])
        o = sb(dn, "o", [P, 2, NB])
        gall = sb(dn, "gall", [P, 2 * G_ROWS, NH])
        gs = sb(dn, "gs", [P, 2 * G_ROWS, 4])
        gx = sb(dn, "gx", [P, 192])
        gt = sb(dn, "gt", [P, 2, 48])
        gtmp = sb(dn, "gtmp", [P, 5, 2, 24])
        rows24 = sb(dn, "rows24", [P, 2, 24])
        ss = sb(dn, "ss", [P, 3, 2, 4])
        rs = sb(dn, "rs", [P, 3, 2, 4])
        before = ExitStack()
        wg_hi = sb(before, "wg_hi", [P, KT, 48], F32R)
        wg_lo = sb(before, "wg_lo", [P, KT, 48], F32R)
        before.close()
        u = sb(dn, "u", [P, 2, 2, 4, P])
        dn.close()
        small_rows = tok[0:N_SMALL, 0, 0, 0:P]
        conv_rows = tok[0:90, 1, 0, 0:256].rearrange("p (a c) -> p a c", a=2)
        wg = kqT[:].rearrange("p a h t -> p (a h t)")[:, 0:KT * 48].rearrange("p (k n) -> p k n", n=48)
        ktok = Y[:].rearrange("p d (m h) i -> p d m (h i)", m=2)
        xpad = r1[:, 0:12 * 260].rearrange("p (c t) -> p c t", c=12)
        conv = r1[:, 3120:3120 + 12 * SEQ].rearrange("p (c t) -> p c t", c=12)
        NT = r1[:, 0:2048].rearrange("p (d m h i) -> p d m h i", d=2, m=2, h=4)
        XL = r1[:, 2048:4096].rearrange("p (d m h i) -> p d m h i", d=2, m=2, h=4)
        XT = r1[:, 4096:6144].rearrange("p (d m h i) -> p d m h i", d=2, m=2, h=4)
        negwT = r1[:, 0:2048].rearrange("p (d h t) -> p d h t", d=2, h=4)
        xl_t = r1[:, 2048:4096].rearrange("p (d h t) -> p d h t", d=2, h=4)
        xt_t = r1[:, 4096:6144].rearrange("p (d h t) -> p d h t", d=2, h=4)
        Wmat = [XT[:, 0], XL[:, 1]]
        qdT = [xl_t[:, 0], xt_t[:, 1]]
        kdec = [XT[:, 0], XL[:, 1]]
        keg = Y[:].rearrange("p d (m h) i -> p d m h i", m=2)
        qd = kqT[:].rearrange("p d h t -> p d (h t)").rearrange("p d (m h i) -> p d m h i", m=2, h=4)
        proj = h[:].rearrange("p m (x c) -> p x m c", x=4)
        g_up = Y[:, 0].rearrange("p (b h) i -> p b h i", b=2)
        g_big = Y[:, 1].rearrange("p (b h) i -> p b h i", b=2)
        sq = attnT[:].rearrange("p a b h i -> p (a b) h i")
        xn_dn = r1[:, 0:4096].rearrange("p (m d) -> p m d", m=2)

        late = ExitStack()
        xn_late = sb(late, "xn_late", [P, 2, D])
        relu = sb(late, "relu", [P, 2, 2, NB])
        mixers = ExitStack()
        q_mem = sb(mixers, "q_mem", [P, 2, NB])
        q_memT = sb(mixers, "q_memT", [P, 4, SEQ])
        vg = sb(mixers, "vg", [P, 2, MIX])
        ug = sb(mixers, "ug", [P, 2, MIX])
        ws = sb(mixers, "ws", [P, NH, P])
        wsT = sb(mixers, "wsT", [P, NH, P])
        vgain = sb(mixers, "vgain", [P, MIX])
        amax = sb(mixers, "amax", [P, 8])
        nmax = sb(mixers, "nmax", [P, 8])
        asum = sb(mixers, "asum", [P, 8])
        arec = sb(mixers, "arec", [P, 8])
        mixers.close()
        hid_hi = sb(late, "hid_hi", [P, 32, SEQ], F32R)
        hid_lo = sb(late, "hid_lo", [P, 32, SEQ], F32R)
        late.close()
        prob = xn_late[:].rearrange("p m (h t) -> p m h t", h=8)[:, :, 0:4, :]
        probT = xn_late[:].rearrange("p m (h t) -> p m h t", h=8)[:, :, 4:8, :]
        final_gain = relu[:].rearrange("p a b n -> p (a b n)")

        ident = cst[:, C_ID:C_ID + P]
        ones = cst[:, C_ONE:C_ONE + P]

        landed = [sem(f"raw_landed{i}") for i in range(4)]
        hi_ready = sem("hi_ready")
        slabs_split = sem("slabs_split")
        slab_used = sem("slab_used")
        result_drained = [sem("result_drained0"), sem("result_drained1")]
        aux_filled = [sem(f"aux_filled{i}") for i in range(4)]
        aux_drained = [sem(f"aux_drained{i}") for i in range(4)]
        mem_fill = [A_MEMN + p for p in range(8)]
        x_fill = [A_XN + p for p in range(8)]
        mix_fill = [[a + p for p in range(6)] + [t + 10, t + 11] for a, t in ((A_MIX0, A_ATT0), (A_MIX1, A_ATT1))]
        ffn_fill = [[a + p for p in range(8)] for a in (A_FN0, A_FN1)]
        tok1_fill = [A_TN1 + p for p in range(8)]

        def filled(e, n, rounds=0):
            e.wait_ge(aux_filled[n % 4], rounds + (n // 4 + 1))

        def drained(e, n, rounds=0):
            e.wait_ge(aux_drained[n % 4], rounds + (n // 4 + 2))

        def may_fill(e, n, rounds=0):
            e.wait_ge(aux_drained[n % 4], rounds + (n // 4 + 1))

        def result(e, B):
            e.wait_ge(slab_used, B * 8 + 10)

        def residual(e, R):
            for m in range(2):
                e.wait_ge(result_drained[m], R + 2)

        def freed(ins, n):
            return ins.then_inc(aux_drained[n % 4], 1)

        def free_result(ins, m):
            return ins.then_inc(result_drained[m], 1)

        block = ctx.enter_context(nc.Block())

        @block.sync
        def _(sp):
            def load(w, k0, n0, B, s):
                if not (isinstance(B, int) and 8 * B + s < 4):
                    sp.wait_ge(slabs_split, B * 8 + (s + 1))
                if isinstance(k0, int):
                    rows = w[k0 + s * 256:k0 + (s + 1) * 256]
                else:
                    rows = w[bass.ds(k0 + s * 256, 256)]
                sp.dma_start(raw[:, s % 4], rows[:, bass.ds(n0, NB)].rearrange("(k p) n -> p k n", p=P)
                             ).then_inc(landed[s % 4], 16)

            def stream(w, n0, B, count):
                if count == 1:
                    for s in range(SLABS):
                        load(w, 0, n0, B, s)
                    return
                with sp.Fori(0, count) as i:
                    for s in range(SLABS):
                        load(w, 0, i * NB + n0, i + B, s)

            def stream_ffn(layer):
                with sp.Fori(0, 2) as half:
                    with sp.Fori(0, 8) as i:
                        for s in range(SLABS):
                            load(ffn_w1[layer], 0, half * (HID // 2) + i * NB, half * 16 + i + B_FFN[layer], s)
                    with sp.Fori(0, 4) as i:
                        for s in range(2 * SLABS):
                            B = half * 16 + i * 2 + (B_FFN[layer] + 8 + s // 8)
                            load(ffn_w2[layer], half * (HID // 2) + (s // 8) * D, i * NB, B, s % 8)

            sp.dma_start(h[:], mem[0].rearrange("(m p) d -> p m d", p=P)).then_inc(sem("mem_loaded"), 16)
            sp.dma_start(cst[:], consts).then_inc(sem("consts_loaded"), 16)
            for rows, k in ((mem_norm_g.rearrange("(k p) -> k p", p=P), GN_MEM),
                            (tok_norm_g.rearrange("l (k p) -> (l k) p", p=P), GN_TOK),
                            (ffn_norm_g.rearrange("l (k p) -> (l k) p", p=P), GN_FFN),
                            (dn_out_norm_g, GN_OUT), (gm_b_s[0], GN_BS)):
                n = rows.shape[0]
                sp.dma_start(small_rows[k:k + n, :], rows).then_inc(sem("rows_loaded"), 16)
            sp.dma_start(conv_rows, dn_conv_w[0].rearrange("t (c p) -> (t c) p", p=P)
                         .rearrange("(a r) p -> r a p", a=2)).then_inc(sem("rows_loaded"), 16)
            for n, row in enumerate((dn_a_log, dn_dt_bias)):
                sp.dma_start(rows24[:, n], row[0:1].rearrange("l a b -> l (a b)").broadcast_to([P, 24])
                             ).then_inc(sem("gate_rows_loaded"), 16)
            sp.dma_start(wg, dn_w_in[0][:, 4 * MIX:4 * MIX + 48].rearrange("(k p) n -> p k n", p=P)
                         ).then_inc(sem("gate_weights_loaded"), 16)
            stream(mem_w_kv[0], 0, 0, 1)
            stream(mem_w_kv[0], NB, 1, 1)
            sp.wait_ge(sem("normalised"), 2)
            sp.dma_start(h[:], x[0].rearrange("(m p) d -> p m d", p=P)).then_inc(sem("x_loaded"), 16)
            stream(mem_w_kv[1], 0, 2, 2)
            with sp.Fori(0, 3) as g:
                for c in range(4):
                    for s in range(SLABS):
                        load(dn_w_in[0], 0, g * NB + c * MIX, g * 4 + (B_DN + c), s)
            stream(dn_w_in[0], 4 * MIX + 48, B_QM, 1)
            sp.wait_ge(sem("mixed"), 6)
            sp.dma_start(h[:], x[0].rearrange("(m p) d -> p m d", p=P)).then_inc(sem("x_loaded"), 16)
            stream(tok_w_out[0], 0, B_OUT[0], 4)
            stream_ffn(0)
            result(sp, B_GM - 1)
            sp.dma_start(ws[:], gm_w_s[0].rearrange("g i j -> i g j")).then_inc(sem("ws_loaded"), 16)
            sp.dma_start(vgain[:], gm_v_norm_g[0:1].broadcast_to([P, MIX])).then_inc(sem("vgain_loaded"), 16)
            stream(gm_w_in[0], MIX, B_GM, 3)
            stream(gm_w_in[0], 0, B_GM + 3, 3)
            stream(gm_w_in[0], 2 * MIX, B_GM + 6, 1)
            stream(tok_w_out[1], 0, B_OUT[1], 4)
            stream_ffn(1)
            result(sp, B_LAST - 2)
            sp.dma_start(final_gain, final_norm_g.rearrange("(a d) -> a d", a=1)
                         .broadcast_to([P, D])).then_inc(sem("final_gain_loaded"), 16)
            for m in range(2):
                sp.wait_ge(sem(f"output_ready{m}"), 1)
                sp.dma_start(out[0, m * P:(m + 1) * P, :], xn_late[:, m]).then_inc(sem("stored"), 16)
            sp.wait_ge(sem("stored"), 32)

        @block.tensor
        def _(pe):
            pe.sem_inc(slab_used, 2)

            def slab(B, s, R, parity, kt0, act_hi, act_lo, last):
                pe.wait_ge(slabs_split, B * 8 + (s + 5))
                for k in range(2):
                    kt = kt0 + k
                    for m in range(2):
                        if kt == 0:
                            pe.wait_ge(result_drained[m], R + 1)
                        acc = banks[2 * parity + m][:]
                        tokens = slice(m * P, (m + 1) * P)
                        pe.matmul(acc, act_hi[:, kt, tokens], w_hi[:, s % 2, k], start=kt == 0, stop=False)
                        pe.matmul(acc, act_hi[:, kt, tokens], w_lo[:, s % 2, k], start=False, stop=False)
                        mm = pe.matmul(acc, act_lo[:, kt, tokens], w_hi[:, s % 2, k], start=False,
                                       stop=last and k == 1)
                mm.then_inc(slab_used, 1)

            def proj_block(B, R, parity, fill=None, between=None):
                for s in range(SLABS):
                    if fill is not None:
                        drained(pe, fill[s])
                    if s == 4 and between is not None:
                        between()
                    slab(B, s, R, parity, 2 * s, xT_hi, xT_lo, s == SLABS - 1)

            def transposes(n, pieces, rounds=0):
                may_fill(pe, n, rounds)
                for col, src in pieces:
                    w = src.shape[0]
                    t = pe.transpose(aux[n % 4][0:src.shape[1], col:col + w], src, cst[0:w, C_ID:C_ID + w])
                t.then_inc(aux_filled[n % 4], 1)

            def pair_transposes(n, src, p, rounds=0):
                transposes(n, [((k * 2 + m) * P, src[:, m, (2 * p + k) * P:(2 * p + k + 1) * P])
                               for k in range(2) for m in range(2)], rounds)

            def norm_transposes(fill, src, count):
                pe.wait_ge(sem("normalised"), count)
                for p in range(8):
                    pair_transposes(fill[p], src, p)

            pe.wait_ge(sem("consts_loaded"), 16)
            pe.wait_ge(sem("rows_loaded"), 96)
            transposes(A_SMALL, [(0, small_rows)])
            transposes(A_SMALL + 1, [(0, conv_rows[:, 0, :]), (90, conv_rows[:, 1, :])])
            norm_transposes(mem_fill, xn_dn, 2)
            for b in range(4):
                proj_block(b, b, b % 2, fill=mem_fill)
            for layer in range(2):
                for m in range(2):
                    pe.wait_ge(result_drained[m], R_KV + 2 * layer + 3)
                for hp in range(2):
                    pair_transposes(A_KT + 2 * layer + hp, ktok[:, layer], hp)
            norm_transposes(x_fill, xn_dn, 4)

            n = A_GATE
            may_fill(pe, n)
            pe.wait_ge(sem("gate_weights_split"), 1)
            for f in x_fill:
                drained(pe, f)
            for m in range(2):
                for kt in range(KT):
                    for j, (a, b) in enumerate(((xT_hi, wg_hi), (xT_hi, wg_lo), (xT_lo, wg_hi))):
                        mm = pe.matmul(aux[n % 4][:, m * 48:(m + 1) * 48], a[:, kt, m * P:(m + 1) * P], b[:, kt],
                                       start=kt == 0 and j == 0, stop=kt == KT - 1 and j == 2)
            mm.then_inc(aux_filled[n % 4], 1)
            n = A_GATE + 1
            may_fill(pe, n)
            pe.wait_ge(sem("gate_steps"), 9)
            b = aux[n % 4]
            for m in range(2):
                row = 2 * (G_G + m)
                for d, c in ((0, C_UP), (1, C_LO)):
                    pe.matmul(b[:, m * 24 + d * 12:m * 24 + d * 12 + 12], cst[:, c:c + P],
                              gall[:, row + d, :], start=True, stop=True)
                pe.matmul(b[:, 48 + m * 24:72 + m * 24], cst[:, C_BLK:C_BLK + P],
                          gall[:, row:row + 2, :], start=True, stop=True)
                for half in range(2):
                    c = 2 * m + half
                    mm = pe.matmul(b[:, 96 + c * 24:120 + c * 24], cst[:, C_SEL + half * P:C_SEL + (half + 1) * P],
                                   gall[:, row:row + 2, :], start=True, stop=True)
            mm.then_inc(aux_filled[n % 4], 1)

            def deltanet(g):
                rnd = g * (DN_AUX // 4)
                bank = lambda n: aux[(A_DN + n) % 4]
                fill = lambda n: may_fill(pe, A_DN + n, rnd)
                have = lambda n: drained(pe, A_DN + n, rnd)
                done = lambda mm, n: mm.then_inc(aux_filled[(A_DN + n) % 4], 1)

                def product(n, lhs, rhs, width, mats):
                    fill(n)
                    for i in range(mats):
                        mm = pe.matmul(bank(n)[:, i * width:(i + 1) * width], lhs(i), rhs(i), start=True, stop=True)
                    done(mm, n)

                for X in range(3):
                    for m in range(2):
                        pe.wait_ge(result_drained[m], g * 4 + (R_DN + X + 3))
                    for hp in range(2):
                        pair_transposes(A_DN + DA + 2 * X + hp, proj[:, X], hp, rnd)
                yield
                for X in range(3):
                    pe.wait_ge(sem("silu_done"), g * 4 + (X + 1))
                    for m in range(2):
                        transposes(A_DN + DD + 2 * X + m,
                                   [(k * P, conv[:, 4 * X + k, m * P:(m + 1) * P]) for k in range(4)], rnd)
                yield
                for X in range(2):
                    for m in range(2):
                        have(DD + 2 * X + m)
                    for hp in range(2):
                        pair_transposes(A_DN + DE + 2 * X + hp, tok[:, X], hp, rnd)
                yield
                for f in range(4):
                    fill(DF + f)
                    pe.wait_ge(sem("decay_operands"), g * 8 + (2 * f + 1))
                    done(pe.matmul(bank(DF + f)[:], ones, g_up[:, f % 2].rearrange("p h i -> p (h i)"),
                                   start=True, stop=True), DF + f)
                yield
                for n in range(4):
                    have(DE + n)
                for m in range(2):
                    for hp in range(2):
                        n = DG + 2 * m + hp
                        fill(n)
                        for k in range(2):
                            hh = 2 * hp + k
                            mm = pe.matmul(bank(n)[:, k * 256:(k + 1) * 256], kqT[:, 1, hh, m * P:(m + 1) * P],
                                           kqT[:, 0:2, hh, m * P:(m + 1) * P], start=True, stop=True)
                        done(mm, n)
                yield
                for d in range(2):
                    for m in range(2):
                        have(DG + 2 * m)
                        have(DG + 2 * m + 1)
                        transposes(A_DN + DH + 2 * d + m, [(k * P, NT[:, d, m, k, :]) for k in range(4)], rnd)
                yield
                for l, s in enumerate(LEVELS):
                    last = l == len(LEVELS) - 1
                    halves = lambda t: t.rearrange("p (b two s) -> p b two s", two=2, s=s)
                    for d in range(2):
                        if l == 0:
                            if d == 0:
                                pe.wait_ge(sem("x0_vector"), g * 6 + 2)
                            pe.wait_ge(sem("x0_pool"), g * 8 + 4 * (d + 1))
                            for m in range(2):
                                have(DH + 2 * d + m)
                        else:
                            have(level_aux(l - 1, d, "XY"))
                        product(level_aux(l, d, "Y"), lambda i: NT[:, d, i // 4, i % 4, :],
                                lambda i: halves(XL[:, d, i // 4, i % 4, :])[:, :, 0, :], CHUNK, 8)
                    yield
                    for d in range(2):
                        if l == 0 and d == 1:
                            pe.wait_ge(sem("x0_vector"), g * 6 + 6)
                        if l > 0:
                            have(level_aux(l - 1, d, "YX"))
                        have(level_aux(l, d, "Y"))
                        if not (last and d == 0):
                            product(level_aux(l, d, "XY"), lambda i: XT[:, d, i // 4, i % 4, :],
                                    lambda i: halves(Y[:, d, i, :])[:, :, 0, :], CHUNK, 8)
                        if not (last and d == 1):
                            product(level_aux(l, d, "YX"), lambda i: Y[:, d, i, :],
                                    lambda i: halves(XT[:, d, i // 4, i % 4, :])[:, :, 1, :], CHUNK, 8)
                    yield
                have(level_aux(4, 0, "YX"))
                have(level_aux(4, 1, "XY"))
                for d in range(2):
                    pe.wait_ge(sem("keg_done"), g * 4 + 2 * (d + 1))
                    for hp in range(2):
                        n = DJ + 2 * d + hp
                        fill(n)
                        for k in range(2):
                            for m in range(2):
                                mm = pe.matmul(bank(n)[:, (2 * k + m) * P:(2 * k + m + 1) * P],
                                               keg[:, d, m, 2 * hp + k, :], Wmat[d][:, m, 2 * hp + k, :],
                                               start=True, stop=True)
                        done(mm, n)
                yield
                for m in range(2):
                    have(DD + 4 + m)
                for d in range(2):
                    for m in range(2):
                        product(DJ + 4 + 2 * d + m, lambda i: Wmat[d][:, m, i, :],
                                lambda i: tok[:, 2, m, i * P:(i + 1) * P], P, 4)
                yield
                for d in range(2):
                    pe.wait_ge(sem("qd_done"), g * 4 + 2 * (d + 1))
                    for hp in range(2):
                        transposes(A_DN + DJ + 8 + 2 * d + hp,
                                   [((2 * k + m) * P, qd[:, d, m, 2 * hp + k, :]) for k in range(2) for m in range(2)],
                                   rnd)
                yield
                for t in range(4):
                    place = [(t // 2, t % 2), ((3 - t) // 2, (3 - t) % 2)]
                    if t:
                        for d in range(2):
                            m, half = place[d]
                            have(step_aux(t - 1, d, "K"))
                            if t == 1 and d == 1:
                                have(DJ + 10)
                            product(step_aux(t, d, "W"), lambda i: negwT[:, d, i, m * P:(m + 1) * P],
                                    lambda i: S[:, d, i, :], P, 4)
                        yield
                    for d in range(2):
                        m, half = place[d]
                        n = step_aux(t, d, "O")
                        if t:
                            have(step_aux(t, d, "W"))
                        else:
                            pe.wait_ge(sem("v_new"), g * 20 + (d + 1))
                        fill(n)
                        for i in range(4):
                            if t:
                                pe.matmul(bank(n)[:, i * P:(i + 1) * P], qdT[d][:, i, m * P:(m + 1) * P], S[:, d, i, :],
                                          start=True, stop=False)
                            mm = pe.matmul(bank(n)[:, i * P:(i + 1) * P], attnT[:, d, m, i, :], vn[:, d, half, i, :],
                                           start=t == 0, stop=True)
                        done(mm, n)
                        if t < 3:
                            if t == 0:
                                pe.wait_ge(sem("kdec_done"), g * 4 + 2 * (d + 1))
                            product(step_aux(t, d, "K"), lambda i: kdec[d][:, m, i, :],
                                    lambda i: vn[:, d, half, i, :], P, 4)
                    yield

            with pe.Fori(0, 3) as g:
                for c in range(4):
                    proj_block(g * 4 + (B_DN + c), g * 4 + (R_DN + c), c % 2)
                for _ in deltanet(g):
                    pass
            proj_block(B_QM, R_QM, R_QM % 2)

            def attention(layer, n0, R):
                for m in range(2):
                    pe.wait_ge(result_drained[m], R + 3)
                for hp in range(2):
                    pair_transposes(n0 + hp, q_mem, hp)
                for m in range(2):
                    for hp in range(2):
                        n = n0 + 2 + 2 * m + hp
                        drained(pe, n0 + hp)
                        may_fill(pe, n)
                        for k in range(2):
                            mm = pe.matmul(aux[n % 4][:, k * 256:(k + 1) * 256], q_memT[:, 2 * hp + k, m * P:(m + 1) * P],
                                           memKT[:, layer, 2 * hp + k, :], start=True, stop=True)
                        mm.then_inc(aux_filled[n % 4], 1)
                pe.wait_ge(sem("prob_ready"), 4 * layer + 4)
                for i in range(4):
                    transposes(n0 + 6 + i, [((mt * 2 + m) * P, prob[:, m, i, mt * P:(mt + 1) * P])
                                            for mt in range(2) for m in range(2)])
                for hp in range(2):
                    n = n0 + 10 + hp
                    drained(pe, n0 + 6 + 2 * hp)
                    drained(pe, n0 + 7 + 2 * hp)
                    may_fill(pe, n)
                    for k in range(2):
                        for mt in range(2):
                            mm = pe.matmul(aux[n % 4][:, k * 256:(k + 1) * 256],
                                           memV[:, layer, mt, (2 * hp + k) * P:(2 * hp + k + 1) * P],
                                           probT[:, mt, 2 * hp + k, :], start=mt == 0, stop=mt == 1)
                    mm.then_inc(aux_filled[n % 4], 1)

            def out_projection(layer):
                with pe.Fori(0, 2) as i:
                    for c in range(2):
                        R = R_OUT[layer] + c
                        proj_block(i * 2 + (B_OUT[layer] + c), i * 2 + R, R % 2, fill=mix_fill[layer])

            def hidden_transposes(layer, half, it, j):
                pe.wait_ge(sem("squared"), half * 8 + it * 2 + (16 * layer + j + 1))
                for q in range(2):
                    pair_transposes(A_FFN[layer] + 2 * j + q, relu[:, j], q, half * 4 + it)

            def ffn(layer):
                with pe.Fori(0, 2) as half:
                    def up(it, j, between):
                        b = it * 2 + j
                        proj_block(half * 16 + b + B_FFN[layer], half * 12 + b + R_FFN[layer],
                                   (R_FFN[layer] + j) % 2, fill=ffn_fill[layer], between=between)
                    up(0, 0, None)
                    with pe.Fori(0, 3) as it:
                        up(it, 1, lambda: hidden_transposes(layer, half, it, 0))
                        up(it + 1, 0, lambda: hidden_transposes(layer, half, it, 1))
                    up(3, 1, lambda: hidden_transposes(layer, half, 3, 0))

                    def down(i, c, between):
                        for s in range(16):
                            if s == 4 and between is not None:
                                between()
                            drained(pe, A_FFN[layer] + s, half * 4)
                            slab(half * 16 + i * 2 + (B_FFN[layer] + 8 + 2 * c + s // 8), s % 8,
                                 half * 12 + i + (R_FFN[layer] + 8 + c), (R_FFN[layer] + c) % 2, 2 * s,
                                 hid_hi, hid_lo, s == 15)
                    down(0, 0, lambda: hidden_transposes(layer, half, 3, 1))
                    down(0, 1, None)
                    down(2, 0, None)
                    down(2, 1, None)

            attention(0, A_ATT0, R_QM)
            pe.wait_ge(sem("mixed"), 6)
            for p in range(6):
                pair_transposes(A_MIX0 + p, mix, p)
            out_projection(0)
            norm_transposes(ffn_fill[0], xn_late, 6)
            ffn(0)

            norm_transposes(tok1_fill, xn_late, 8)
            with pe.Fori(0, 3) as i:
                for c in range(2):
                    proj_block(i * 2 + (B_GM + c), i * 2 + (R_GM + c), (R_GM + c) % 2, fill=tok1_fill)
            proj_block(B_GM + 6, R_GM + 6, (R_GM + 6) % 2)
            pe.wait_ge(sem("ws_loaded"), 16)
            for q in range(3):
                transposes(A_WS + q, [(k * P, ws[:, 4 * q + k, :]) for k in range(4)])
            for q in range(3):
                drained(pe, A_WS + q)
            for m in range(2):
                pe.wait_ge(sem("v_normalised"), m + 1)
                for q in range(3):
                    n = A_SG + 3 * m + q
                    may_fill(pe, n)
                    for k in range(4):
                        i = 4 * q + k
                        mm = pe.matmul(aux[n % 4][:, k * P:(k + 1) * P], wsT[:, i, :], vg[:, m, i * P:(i + 1) * P],
                                       start=True, stop=True)
                    mm.then_inc(aux_filled[n % 4], 1)
            attention(1, A_ATT1, R_GM + 6)
            for n in range(6):
                drained(pe, A_SG + n)
            for p in range(6):
                pair_transposes(A_MIX1 + p, mix, p)
            out_projection(1)
            norm_transposes(ffn_fill[1], xn_late, 10)
            ffn(1)

        @block.scalar
        def _(act):
            def split(B, s):
                act.wait_ge(landed[s % 4], B * 32 + 16 * (s // 4 + 1))
                act.wait_ge(slab_used, B * 8 + (s + 1))
                act.activation(w_hi[:, s % 2], raw[:, s % 4], ACT.Copy).then_inc(hi_ready, 1)

            def head(B):
                for s in range(2):
                    split(B, s)

            def tail(B, between=None, at=5):
                for s in range(2, SLABS):
                    split(B, s)
                    if s == at and between is not None:
                        between()

            def copy_result(B, parity, m, dst, func=ACT.Copy):
                result(act, B)
                free_result(act.activation(dst, banks[2 * parity + m][:], func), m)

            def sum_squares(src, junk, m):
                act.activation(junk, src, ACT.Square, accum_out=stat[:, m:m + 1]).then_inc(sem(f"squares_summed{m}"), 1)

            def norm(r, xn):
                sum_squares(h[:, 0], xn[:, 0], 0)
                act.wait_ge(sem("rstd_ready"), 2 * r + 2)
                act.activation(xn[:, 0], h[:, 0], ACT.Copy, scale=rstd[:, 0:1]).then_inc(sem("normalised"), 1)

            def operand_hi(n, p, gain):
                filled(act, n)
                if gain is None:
                    act.activation(xT_hi[:, 2 * p:2 * p + 2, :], pair(n), ACT.Copy).then_inc(sem("xT_hi_ready"), 2)
                else:
                    for k in range(2):
                        c = gain + (2 * p + k) * (gain != GN_OUT)
                        act.activation(xT_hi[:, 2 * p + k, :], aux[n % 4][:, k * SEQ:(k + 1) * SEQ], ACT.Copy,
                                       scale=gains[:, c:c + 1]).then_inc(sem("xT_hi_ready"), 1)

            def copy_aux(n, dst, src):
                filled(act, n)
                freed(act.activation(dst, src, ACT.Copy), n)

            pair = lambda n: aux[n % 4][:].rearrange("p (k t) -> p k t", k=2)

            copy_aux(A_SMALL, gains[:], src=aux[A_SMALL % 4][:, 0:N_SMALL])
            copy_aux(A_SMALL + 1, conv_w[:], src=aux[(A_SMALL + 1) % 4][:, 0:180])
            head(0)
            act.wait_ge(sem("mem_loaded"), 16)
            norm(0, xn_dn)
            drained(act, A_SMALL)
            for p in range(8):
                operand_hi(mem_fill[p], p, GN_MEM)
            for b in range(4):
                tail(b)
                head(b + 1)
                dst = ktok[:, b // 2, 0, :] if b % 2 == 0 else memV[:, b // 2, 0, :]
                copy_result(b, b % 2, 0, dst)
                if b == 0:
                    act.wait_ge(sem("gate_weights_loaded"), 16)
                    act.activation(wg_hi[:], wg, ACT.Copy).then_inc(sem("gate_hi"), 1)
            for layer in range(2):
                for hp in range(2):
                    n = A_KT + 2 * layer + hp
                    copy_aux(n, memKT[:, layer, 2 * hp:2 * hp + 2, :], src=pair(n))
            filled(act, mem_fill[7])
            act.wait_ge(sem("x_loaded"), 16)
            norm(1, xn_dn)
            for p in range(8):
                operand_hi(x_fill[p], p, GN_TOK)
            act.wait_ge(sem("gate_rows_loaded"), 32)
            act.activation(rows24[:, 0], rows24[:, 0], ACT.Exp).then_inc(sem("gate_exps"), 1)
            act.wait_ge(sem("gate_steps"), 4)
            act.activation(gtmp[:, 2], gtmp[:, 1], ACT.Exp).then_inc(sem("gate_exps"), 1)
            act.activation(gtmp[:, 3], gt[:, :, 24:48], ACT.Exp, scale=-1.0).then_inc(sem("gate_exps"), 1)
            act.wait_ge(sem("gate_exps"), 2)
            act.activation(gtmp[:, 4], gtmp[:, 2], ACT.Ln, bias=1.0).then_inc(sem("gate_exps"), 1)
            act.wait_ge(sem("gate_steps"), 12)
            act.activation(gall[:, 2 * G_EGC:2 * G_EGC + 4, :].rearrange("p r h -> p (r h)"),
                           gx[:, 0:48], ACT.Exp).then_inc(sem("gate_exps"), 1)
            act.activation(gall[:, 2 * G_EKD:2 * G_EKD + 4, :].rearrange("p r h -> p (r h)"),
                           gtmp[:, 0].rearrange("p m c -> p (m c)"), ACT.Exp).then_inc(sem("gate_exps"), 1)
            act.activation(gall[:, 2 * G_CD:2 * G_CD + 8, :].rearrange("p r h -> p (r h)"),
                           gx[:, 96:192], ACT.Exp).then_inc(sem("gate_exps"), 1)

            def deltanet(g):
                rnd = g * (DN_AUX // 4)
                fil = lambda n: filled(act, A_DN + n, rnd)
                bank = lambda n: aux[(A_DN + n) % 4]
                halves = lambda n: bank(n)[:].rearrange("p (k t) -> p k t", k=2)
                free = lambda ins, n: freed(ins, A_DN + n)
                for n in range(6):
                    fil(DA + n)
                    free(act.activation(xpad[:, 2 * n:2 * n + 2, 2:2 + SEQ], halves(DA + n), ACT.Copy), DA + n)
                yield
                for X in range(3):
                    act.wait_ge(sem("conv_tap"), g * 60 + 20 * (X + 1))
                    act.activation(conv[:, 4 * X:4 * X + 4, :], conv[:, 4 * X:4 * X + 4, :], ACT.Silu
                                   ).then_inc(sem("silu_done"), 1)
                for m in range(2):
                    act.wait_ge(result_drained[m], g * 4 + (R_DN + 6))
                act.activation(proj[:, 3], proj[:, 3], ACT.Silu).then_inc(sem("silu_done"), 1)
                yield
                for n in range(4):
                    fil(DD + n)
                    if n >= 2:
                        act.wait_ge(sem("head_sums"), g * 6 + (n - 1))
                    act.activation(sq[:, n % 2], bank(DD + n)[:].rearrange("p (h i) -> p h i", h=4), ACT.Square
                                   ).then_inc(sem("head_squares"), 1)
                for m in range(2):
                    fil(DD + 4 + m)
                    free(act.activation(tok[:, 2, m], bank(DD + 4 + m)[:], ACT.Copy), DD + 4 + m)
                yield
                for X in range(2):
                    for hp in range(2):
                        n = DE + 2 * X + hp
                        fil(n)
                        free(act.activation(kqT[:, X, 2 * hp:2 * hp + 2, :], halves(n), ACT.Copy), n)
                yield
                for f in range(4):
                    drained(act, A_DN + DF + f, rnd)
                    act.activation(NT[:, f // 2, f % 2], NT[:, f // 2, f % 2], ACT.Exp).then_inc(sem("decay_ready"), 1)
                yield
                for m in range(2):
                    n = DH + 2 + m
                    act.wait_ge(sem("x0_vector"), g * 6 + (3 + 2 * m))
                    act.wait_ge(sem("x0_pool"), g * 8 + (6 + 2 * m))
                    free(act.activation(NT[:, 1, m].rearrange("p h i -> p (h i)"), bank(n)[:], ACT.Copy), n)
                yield
                for d in range(2):
                    for hp in range(2):
                        n = DJ + 2 * d + hp
                        fil(n)
                        free(act.activation(negwT[:, d, 2 * hp:2 * hp + 2, :], halves(n), ACT.Copy, scale=-1.0), n)
                yield
                for d in range(2):
                    for hp in range(2):
                        n = DJ + 8 + 2 * d + hp
                        fil(n)
                        free(act.activation(qdT[d][:, 2 * hp:2 * hp + 2, :], halves(n), ACT.Copy), n)
                yield
                for n in (step_aux(2, 0, "O"), step_aux(2, 1, "O"), step_aux(3, 0, "O"), step_aux(3, 1, "O")):
                    drained(act, A_DN + n, rnd)
                for m in range(2):
                    act.activation(sq[:, m], o[:, m].rearrange("p (h i) -> p h i", h=4), ACT.Square
                                   ).then_inc(sem("out_squares"), 1)
                act.wait_ge(sem("mixed"), g * 2 + 2)

            with act.Fori(0, 3) as g:
                for c in range(4):
                    B = g * 4 + (B_DN + c)
                    tail(B)
                    head(g * 4 + (B_DN + c + 1))
                    copy_result(B, c % 2, 0, proj[:, c, 0, :])
                for _ in deltanet(g):
                    pass

            def attention(layer, n0, B, parity):
                copy_result(B, parity, 0, q_mem[:, 0, :])
                for hp in range(2):
                    copy_aux(n0 + hp, q_memT[:, 2 * hp:2 * hp + 2, :], src=pair(n0 + hp))
                for j in range(4):
                    n = n0 + 2 + j
                    act.wait_ge(sem("score_max"), 8 * layer + 2 * (j + 1))
                    for k in range(2):
                        c = 2 * j + k
                        e = act.activation(prob[:, j // 2, 2 * (j % 2) + k, :], aux[n % 4][:, k * SEQ:(k + 1) * SEQ],
                                           ACT.Exp, bias=nmax[:, c:c + 1], scale=HD ** -0.5, accum_out=asum[:, c:c + 1])
                        if k == 0:
                            e.then_inc(sem("exp_half"), 1)
                        else:
                            freed(e, n)
                for i in range(4):
                    n = n0 + 6 + i
                    copy_aux(n, probT[:, :, i, :], src=pair(n))
                for hp in range(2):
                    operand_hi(n0 + 10 + hp, 6 + hp, None)

            def out_projection(layer):
                with act.Fori(0, 4) as i:
                    tail(i + B_OUT[layer])
                    head(i + (B_OUT[layer] + 1))

            def hidden(layer, half, it, j):
                for q in range(2):
                    n = A_FFN[layer] + 2 * j + q
                    filled(act, n, half * 4 + it)
                    act.activation(hid_hi[:, bass.ds(it * 8 + (4 * j + 2 * q), 2), :], pair(n), ACT.Copy
                                   ).then_inc(sem("hidden_hi"), 1)

            def ffn_half(layer, half, last=False):
                def up(it, j, between):
                    tail(half * 16 + it * 2 + (B_FFN[layer] + j), between)
                    head(half * 16 + it * 2 + (B_FFN[layer] + j + 1))
                    copy_result(half * 16 + it * 2 + (B_FFN[layer] + j), (R_FFN[layer] + j) % 2, 0,
                                relu[:, j, 0, :], ACT.Relu)
                up(0, 0, None)
                with act.Fori(0, 3) as it:
                    up(it, 1, lambda: hidden(layer, half, it, 0))
                    up(it + 1, 0, lambda: hidden(layer, half, it, 1))
                up(3, 1, lambda: hidden(layer, half, 3, 0))
                tail(half * 16 + (B_FFN[layer] + 8), lambda: hidden(layer, half, 3, 1))
                with act.Fori(0, 7) as i:
                    head(half * 16 + i + (B_FFN[layer] + 9))
                    tail(half * 16 + i + (B_FFN[layer] + 9))
                if not last:
                    head(half * 16 + (B_FFN[layer] + 16))

            tail(B_QM)
            head(B_QM + 1)
            attention(0, A_ATT0, B_QM, R_QM % 2)
            for p in range(6):
                operand_hi(A_MIX0 + p, p, GN_OUT)
            out_projection(0)
            residual(act, R_FFN[0])
            norm(2, xn_late)
            for p in range(8):
                operand_hi(ffn_fill[0][p], p, GN_FFN)
            with act.Fori(0, 2) as half:
                ffn_half(0, half)

            residual(act, R_GM)
            norm(3, xn_late)
            for p in range(8):
                operand_hi(tok1_fill[p], p, GN_TOK + 16)
            for dst, b0 in ((vg, 0), (ug, 3)):
                for i in range(3):
                    B = B_GM + b0 + i
                    tail(B)
                    head(B + 1)
                    for m in range(2):
                        copy_result(B, (R_GM + b0 + i) % 2, m, dst[:, m, i * NB:(i + 1) * NB], ACT.Gelu_apprx_tanh)
                if b0 == 0:
                    for m in range(2):
                        act.wait_ge(result_drained[m], R_GM + 5)
                        sum_squares(vg[:, m], xn_late[:, m, 0:MIX], m)
            tail(B_GM + 6)
            head(B_GM + 7)
            for q in range(3):
                copy_aux(A_WS + q, wsT[:, 4 * q:4 * q + 4, :], src=aux[(A_WS + q) % 4][:].rearrange("p (k t) -> p k t", k=4))
            attention(1, A_ATT1, B_GM + 6, (R_GM + 6) % 2)
            for p in range(6):
                operand_hi(A_MIX1 + p, p, None)
            out_projection(1)
            residual(act, R_FFN[1])
            norm(5, xn_late)
            for p in range(8):
                operand_hi(ffn_fill[1][p], p, GN_FFN + 16)
            ffn_half(1, 0)
            ffn_half(1, 1, last=True)
            residual(act, R_END)
            sum_squares(h[:, 0], xn_late[:, 0], 0)
            act.wait_ge(sem("rstd_ready"), 14)
            act.activation(xn_late[:, 0], h[:, 0], ACT.Copy, scale=rstd[:, 0:1]).then_inc(sem("scaled"), 1)
            act.wait_ge(sem("scaled"), 1)

        @block.vector
        def _(dve):
            dve.sem_inc(slabs_split, 4)
            for m in range(2):
                dve.sem_inc(result_drained[m], 2)
            for b in range(4):
                dve.sem_inc(aux_drained[b], 1)

            def split(B, s):
                dve.wait_ge(hi_ready, B * 8 + (s + 1))
                dve.wait_ge(slab_used, B * 8 + (s + 1))
                dve.tensor_tensor(w_lo[:, s % 2], raw[:, s % 4], w_hi[:, s % 2].bitcast(F32), ALU.subtract
                                  ).then_inc(slabs_split, 1)

            def head(B):
                for s in range(2):
                    split(B, s)

            def tail(B, between=None, at=5):
                for s in range(2, SLABS):
                    split(B, s)
                    if s == at and between is not None:
                        between()

            def copy_result(B, parity, m, dst):
                result(dve, B)
                free_result(dve.tensor_copy(dst, banks[2 * parity + m][:]), m)

            def norm(r, xn):
                dve.tensor_tensor_reduce(out=xn[:, 1], in0=h[:, 1], in1=h[:, 1], scale=1.0, scalar=0.0, op0=ALU.mult,
                                         op1=ALU.add, accum_out=stat[:, 1:2]).then_inc(sem("squares_summed1"), 1)
                dve.wait_ge(sem("rstd_ready"), 2 * r + 2)
                dve.tensor_scalar(xn[:, 1], h[:, 1], rstd[:, 1:2], None, ALU.mult).then_inc(sem("normalised"), 1)

            def operand_lo(n, p, gain, hi_count):
                dve.wait_ge(sem("xT_hi_ready"), hi_count)
                if gain is None:
                    freed(dve.tensor_tensor(xT_lo[:, 2 * p:2 * p + 2, :], aux[n % 4][:].rearrange("p (k t) -> p k t", k=2),
                                            xT_hi[:, 2 * p:2 * p + 2, :].bitcast(F32), ALU.subtract), n)
                else:
                    for k in range(2):
                        c = gain + (2 * p + k) * (gain != GN_OUT)
                        e = dve.scalar_tensor_tensor(out=xT_lo[:, 2 * p + k, :], in0=aux[n % 4][:, k * SEQ:(k + 1) * SEQ],
                                                     scalar=gains[:, c:c + 1], in1=xT_hi[:, 2 * p + k, :].bitcast(F32),
                                                     op0=ALU.mult, op1=ALU.subtract)
                        if k == 0:
                            e.then_inc(sem("xT_lo_half"), 1)
                    freed(e, n)

            def rows(v, n):
                return v.unsqueeze(2).broadcast_to([P, 4, n])

            def over(v, n):
                return v.unsqueeze(1).broadcast_to([P, n, v.shape[1]])

            head(0)
            dve.wait_ge(sem("mem_loaded"), 16)
            norm(0, xn_dn)
            drained(dve, A_SMALL)
            for p in range(8):
                operand_lo(mem_fill[p], p, GN_MEM, 2 * (p + 1))
            for b in range(4):
                tail(b)
                head(b + 1)
                dst = ktok[:, b // 2, 1, :] if b % 2 == 0 else memV[:, b // 2, 1, :]
                copy_result(b, b % 2, 1, dst)
                if b == 0:
                    dve.wait_ge(sem("gate_hi"), 1)
                    dve.tensor_tensor(wg_lo[:], wg, wg_hi[:].bitcast(F32), ALU.subtract
                                      ).then_inc(sem("gate_weights_split"), 1)
            filled(dve, mem_fill[7])
            dve.wait_ge(sem("x_loaded"), 16)
            norm(1, xn_dn)
            for p in range(8):
                operand_lo(x_fill[p], p, GN_TOK, 16 + 2 * (p + 1))

            steps = sem("gate_steps")
            n = A_GATE
            filled(dve, n)
            freed(dve.tensor_copy(gt[:].rearrange("p m c -> p (m c)"), aux[n % 4][:, 0:96]), n)
            drained(dve, n)
            dve.wait_ge(sem("gate_rows_loaded"), 32)
            dve.tensor_tensor(gtmp[:, 0], gt[:, :, 0:24], over(rows24[:, 1], 2), ALU.add).then_inc(steps, 1)
            dve.wait_ge(steps, 1)
            dve.tensor_scalar(gtmp[:, 1], gtmp[:, 0], -1.0, None, ALU.mult).then_inc(steps, 1)
            dve.wait_ge(steps, 2)
            dve.tensor_tensor(gtmp[:, 1], gtmp[:, 1], gtmp[:, 0], ALU.min).then_inc(steps, 1)
            dve.wait_ge(steps, 3)
            dve.tensor_scalar(gtmp[:, 0], gtmp[:, 0], 0.0, None, ALU.max).then_inc(steps, 1)
            dve.wait_ge(sem("gate_exps"), 4)
            dve.tensor_tensor(gtmp[:, 0], gtmp[:, 0], gtmp[:, 4], ALU.add).then_inc(steps, 1)
            dve.wait_ge(steps, 5)
            dve.tensor_tensor(gtmp[:, 0], gtmp[:, 0], over(rows24[:, 0], 2), ALU.mult).then_inc(steps, 1)
            dve.wait_ge(steps, 6)
            gm = lambda a: gall[:, 2 * a:2 * a + 4, :].rearrange("p (m d) h -> p m (d h)", m=2)
            dve.tensor_scalar(gm(G_G), gtmp[:, 0], -1.0, None, ALU.mult).then_inc(steps, 1)
            dve.tensor_scalar(gtmp[:, 3], gtmp[:, 3], 1.0, None, ALU.add).then_inc(steps, 1)
            dve.wait_ge(steps, 8)
            dve.reciprocal(gm(G_BETA), gtmp[:, 3]).then_inc(steps, 1)
            n = A_GATE + 1
            filled(dve, n)
            freed(dve.tensor_copy(gx[:], aux[n % 4][:, 0:192]), n)
            drained(dve, n)
            dve.tensor_copy(gm(G_GC), gx[:, 0:48].rearrange("p (m c) -> p m c", m=2)).then_inc(steps, 1)
            dve.tensor_tensor(gtmp[:, 0].rearrange("p m c -> p (m c)"), gx[:, 48:96], gx[:, 0:48], ALU.subtract
                              ).then_inc(steps, 1)
            dve.tensor_copy(gtmp[:, 1].rearrange("p m c -> p (m c)"), gx[:, 0:48]).then_inc(steps, 1)

            def deltanet(g):
                rnd = g * (DN_AUX // 4)
                fil = lambda n: filled(dve, A_DN + n, rnd)
                have = lambda n: drained(dve, A_DN + n, rnd)
                bank = lambda n: aux[(A_DN + n) % 4]
                heads = lambda n: bank(n)[:].rearrange("p (h i) -> p h i", h=4)
                free = lambda ins, n: freed(ins, A_DN + n)
                beta = lambda m, d, hh: gs[:, 2 * (G_BETA + m) + d, hh:hh + 1]
                dve.wait_ge(sem("padded"), g * 2 + 2)
                taps = sem("conv_tap")
                for X in range(3):
                    have(DA + 2 * X)
                    have(DA + 2 * X + 1)
                    for tap in range(CONV):
                        for c in range(4):
                            ct = 4 * X + c
                            w = conv_w[:, bass.ds(g * 4 + (tap * 36 + X * 12 + c), 1)]
                            src = xpad[:, ct, tap:tap + SEQ]
                            if tap == 0:
                                e = dve.tensor_scalar(conv[:, ct], src, w, None, ALU.mult)
                            else:
                                dve.wait_ge(taps, g * 60 + (20 * X + 4 * (tap - 1) + c + 1))
                                e = dve.scalar_tensor_tensor(out=conv[:, ct], in0=src, scalar=w, in1=conv[:, ct],
                                                             op0=ALU.mult, op1=ALU.add)
                            e.then_inc(taps, 1)
                yield
                for n in range(4):
                    dve.wait_ge(sem("head_squares"), g * 4 + (n + 1))
                    dve.tensor_reduce(ss[:, n // 2, n % 2], sq[:, n % 2], AX.X, ALU.add).then_inc(sem("head_sums"), 1)
                    if n % 2:
                        X = n // 2
                        f = float(HD) if X == 0 else 1.0
                        dve.wait_ge(sem("head_sums"), g * 6 + (3 * X + 2))
                        dve.tensor_scalar(ss[:, X], ss[:, X], f, f * EPS, ALU.mult, ALU.add
                                          ).then_inc(sem("head_sums"), 1)
                for n in range(4):
                    dve.wait_ge(sem("head_rstd"), g * 2 + (n // 2 + 1))
                    free(dve.tensor_tensor(tok[:, n // 2, n % 2].rearrange("p (h i) -> p h i", h=4), heads(DD + n),
                                           rows(rs[:, n // 2, n % 2], P), ALU.mult), DD + n)
                yield
                for f in range(4):
                    fil(DF + f)
                    dve.wait_ge(sem("decay_operands"), g * 8 + (2 * f + 2))
                    free(dve.tensor_tensor(NT[:, f // 2, f % 2], heads(DF + f), g_big[:, f % 2], ALU.subtract), DF + f)
                yield
                dve.wait_ge(sem("decay_ready"), g * 4 + 4)
                dve.wait_ge(sem("head_sums"), g * 6 + 6)
                for m in range(2):
                    for hp in range(2):
                        n = DG + 2 * m + hp
                        fil(n)
                        view = bank(n)[:].rearrange("p (k two i) -> p k two i", k=2, two=2)
                        for d in range(2):
                            dve.tensor_tensor(attnT[:, d, m, 2 * hp:2 * hp + 2, :], view[:, :, 0, :],
                                              NT[:, d, m, 2 * hp:2 * hp + 2, :], ALU.mult).then_inc(sem("attn_ready"), 1)
                        dve.wait_ge(sem("attn_ready"), g * 8 + (2 * (2 * m + hp) + 2))
                        for d in range(2):
                            for k in range(2):
                                hh = 2 * hp + k
                                e = dve.scalar_tensor_tensor(out=NT[:, d, m, hh, :], in0=view[:, k, 1, :],
                                                             scalar=beta(m, d, hh), in1=NT[:, d, m, hh, :],
                                                             op0=ALU.mult, op1=ALU.mult)
                                if (d, k) != (1, 1):
                                    e.then_inc(sem("n_part"), 1)
                        free(e, n)
                yield
                x0 = sem("x0_vector")
                for d in range(2):
                    for m in range(2):
                        n = DH + 2 * d + m
                        fil(n)
                        if d == 0:
                            free(dve.tensor_tensor(XL[:, 0, m], heads(n), over(cst[:, C_M1L:C_M1L + P], 4), ALU.mult), n)
                            have(n)
                            dve.tensor_tensor(XL[:, 0, m], XL[:, 0, m], over(ident, 4), ALU.add).then_inc(x0, 1)
                        else:
                            dve.tensor_tensor(XT[:, 1, m], heads(n), over(cst[:, C_M1T:C_M1T + P], 4), ALU.mult
                                              ).then_inc(x0, 1)
                            dve.wait_ge(x0, g * 6 + (3 + 2 * m))
                            dve.tensor_tensor(XT[:, 1, m], XT[:, 1, m], over(ident, 4), ALU.add).then_inc(x0, 1)
                yield
                for l, s in enumerate(LEVELS):
                    last = l == len(LEVELS) - 1
                    halves = lambda t: t.rearrange("p x (b two s) -> p x b two s", two=2, s=s)
                    mats = lambda t: t.rearrange("p m h i -> p (m h) i")
                    got = lambda n: bank(n)[:].rearrange("p (x b s) -> p x b s", x=8, s=s)
                    mask = cst[:, C_LEV + l * CHUNK:C_LEV + (l + 1) * CHUNK].rearrange("p (b s) -> p b s", s=s)
                    mask = mask.unsqueeze(1).broadcast_to([P, 8, CHUNK // s, s])
                    for d in range(2):
                        n = level_aux(l, d, "Y")
                        fil(n)
                        dve.wait_ge(sem("y_zeroed"), g * 10 + (2 * l + d + 1))
                        free(dve.tensor_tensor(halves(Y[:, d])[:, :, :, 0, :], got(n), mask, ALU.mult), n)
                    yield
                    for d in range(2):
                        if not (last and d == 0):
                            n = level_aux(l, d, "XY")
                            fil(n)
                            t = halves(mats(XL[:, d]))[:, :, :, 0, :]
                            free(dve.tensor_tensor(t, t, got(n), ALU.subtract), n)
                        if not (last and d == 1):
                            n = level_aux(l, d, "YX")
                            fil(n)
                            t = halves(mats(XT[:, d]))[:, :, :, 1, :]
                            free(dve.tensor_tensor(t, t, got(n), ALU.subtract), n)
                    yield
                for d in range(2):
                    for m in range(2):
                        n = DJ + 4 + 2 * d + m
                        fil(n)
                        free(dve.tensor_tensor(u[:, d, m], heads(n), rows(gs[:, 2 * (G_BETA + m) + d, :], P), ALU.mult), n)
                yield
                for t in range(4):
                    place = [(t // 2, t % 2), ((3 - t) // 2, (3 - t) % 2)]
                    for d in range(2):
                        m, half = place[d]
                        R = slice(half * CHUNK, (half + 1) * CHUNK)
                        if t == 0:
                            have(DJ + 4 + 2 * d + m)
                            dve.tensor_copy(vn[R, d, half], u[R, d, m]).then_inc(sem("v_new"), 1)
                        else:
                            n = step_aux(t, d, "W")
                            fil(n)
                            for i in range(4):
                                e = dve.scalar_tensor_tensor(out=vn[R, d, half, i, :], in0=heads(n)[R, i, :],
                                                             scalar=gs[R, 2 * (G_BETA + m) + d, i:i + 1],
                                                             in1=u[R, d, m, i, :], op0=ALU.mult, op1=ALU.add)
                                if i < 3:
                                    e.then_inc(sem("v_new"), 1)
                            free(e, n)
                    yield
                    for d in range(2):
                        m, half = place[d]
                        R = slice(half * CHUNK, (half + 1) * CHUNK)
                        n = step_aux(t, d, "O")
                        fil(n)
                        if t < 2:
                            free(dve.tensor_copy(o[R, m], bank(n)[R, :]), n)
                        else:
                            have(step_aux(3 - t, 1 - d, "O"))
                            free(dve.tensor_tensor(o[R, m], o[R, m], bank(n)[R, :], ALU.add), n)
                        if t == 3:
                            continue
                        n = step_aux(t, d, "K")
                        fil(n)
                        if t == 0:
                            free(dve.tensor_copy(S[:, d], heads(n)), n)
                        else:
                            for i in range(4):
                                e = dve.scalar_tensor_tensor(out=S[:, d, i], in0=S[:, d, i],
                                                             scalar=gs[:, 2 * (G_CD + 2 * m + half) + d, i:i + 1],
                                                             in1=heads(n)[:, i, :], op0=ALU.mult, op1=ALU.add)
                                if i < 3:
                                    e.then_inc(sem("state_part"), 1)
                            free(e, n)
                    yield
                for m in range(2):
                    dve.wait_ge(sem("out_squares"), g * 2 + (m + 1))
                    dve.tensor_reduce(ss[:, 2, m], sq[:, m], AX.X, ALU.add).then_inc(sem("out_sums"), 1)
                dve.wait_ge(sem("out_sums"), g * 3 + 2)
                dve.tensor_scalar(ss[:, 2], ss[:, 2], 1.0 / HD, EPS, ALU.mult, ALU.add).then_inc(sem("out_sums"), 1)
                dve.wait_ge(sem("out_rstd"), g + 1)
                for m in range(2):
                    om = o[:, m].rearrange("p (h i) -> p h i", h=4)
                    dve.tensor_tensor(om, om, rows(rs[:, 2, m], P), ALU.mult).then_inc(sem("out_normed"), 1)
                dve.wait_ge(sem("silu_done"), g * 4 + 4)
                for m in range(2):
                    dve.wait_ge(sem("out_normed"), g * 2 + (m + 1))
                    dve.tensor_tensor(mix[:, m, bass.ds(g * NB, NB)], o[:, m], proj[:, 3, m], ALU.mult
                                      ).then_inc(sem("mixed"), 1)
                dve.wait_ge(sem("mixed"), g * 2 + 2)

            with dve.Fori(0, 3) as g:
                for c in range(4):
                    B = g * 4 + (B_DN + c)
                    tail(B)
                    head(g * 4 + (B_DN + c + 1))
                    copy_result(B, c % 2, 1, proj[:, c, 1, :])
                for _ in deltanet(g):
                    pass

            def attention(layer, n0, B, parity, hi_count):
                copy_result(B, parity, 1, q_mem[:, 1, :])
                for j in range(4):
                    n = n0 + 2 + j
                    filled(dve, n)
                    dve.tensor_reduce(amax[:, 2 * j:2 * j + 2], aux[n % 4][:].rearrange("p (k t) -> p k t", k=2),
                                      AX.X, ALU.max).then_inc(sem("score_max"), 1)
                    dve.wait_ge(sem("score_max"), 8 * layer + 2 * j + 1)
                    dve.tensor_scalar(nmax[:, 2 * j:2 * j + 2], amax[:, 2 * j:2 * j + 2], -(HD ** -0.5), None, ALU.mult
                                      ).then_inc(sem("score_max"), 1)
                for j in range(4):
                    drained(dve, n0 + 2 + j)
                dve.reciprocal(arec[:], asum[:]).then_inc(sem("sum_inverse"), 1)
                dve.wait_ge(sem("sum_inverse"), layer + 1)
                for j in range(4):
                    t = prob[:, j // 2, 2 * (j % 2):2 * (j % 2) + 2, :]
                    dve.tensor_tensor(t, t, arec[:, 2 * j:2 * j + 2].unsqueeze(2).broadcast_to([P, 2, SEQ]), ALU.mult
                                      ).then_inc(sem("prob_ready"), 1)
                for hp in range(2):
                    operand_lo(n0 + 10 + hp, 6 + hp, None, hi_count + 2 * (hp + 1))

            def add_result(B, parity, i):
                result(dve, B)
                for m in range(2):
                    t = h[:, m, bass.ds(i * NB, NB)]
                    free_result(dve.tensor_tensor(t, t, banks[2 * parity + m][:], ALU.add), m)

            def out_projection(layer):
                with dve.Fori(0, 2) as i:
                    for c in range(2):
                        tail(i * 2 + (B_OUT[layer] + c))
                        head(i * 2 + (B_OUT[layer] + c + 1))
                        add_result(i * 2 + (B_OUT[layer] + c), (R_OUT[layer] + c) % 2, i * 2 + c)

            def hidden(layer, half, it, j):
                for q in range(2):
                    n = A_FFN[layer] + 2 * j + q
                    dve.wait_ge(sem("hidden_hi"), half * 16 + it * 4 + (32 * layer + 2 * j + q + 1))
                    t = bass.ds(it * 8 + (4 * j + 2 * q), 2)
                    freed(dve.tensor_tensor(hid_lo[:, t, :], aux[n % 4][:].rearrange("p (k t) -> p k t", k=2),
                                            hid_hi[:, t, :].bitcast(F32), ALU.subtract), n)

            def ffn_half(layer, half, last=False):
                def up(it, j, between):
                    B = half * 16 + it * 2 + (B_FFN[layer] + j)
                    tail(B, between)
                    head(half * 16 + it * 2 + (B_FFN[layer] + j + 1))
                    result(dve, B)
                    free_result(dve.tensor_scalar(relu[:, j, 1, :], banks[2 * ((R_FFN[layer] + j) % 2) + 1][:], 0.0, None,
                                                  ALU.max), 1)
                up(0, 0, None)
                with dve.Fori(0, 3) as it:
                    up(it, 1, lambda: hidden(layer, half, it, 0))
                    up(it + 1, 0, lambda: hidden(layer, half, it, 1))
                up(3, 1, lambda: hidden(layer, half, 3, 0))

                def down(i, c, between=None, end=False):
                    B = half * 16 + i * 2 + (B_FFN[layer] + 8 + 2 * c)
                    tail(B, between)
                    head(half * 16 + i * 2 + (B_FFN[layer] + 9 + 2 * c))
                    tail(half * 16 + i * 2 + (B_FFN[layer] + 9 + 2 * c))
                    if not end:
                        head(half * 16 + i * 2 + (B_FFN[layer] + 10 + 2 * c))
                    add_result(half * 16 + i * 2 + (B_FFN[layer] + 9 + 2 * c), (R_FFN[layer] + c) % 2, i + c)
                down(0, 0, lambda: hidden(layer, half, 3, 1))
                down(0, 1)
                down(2, 0)
                down(2, 1, end=last)

            dve.wait_ge(sem("mixed"), 6)
            tail(B_QM)
            head(B_QM + 1)
            attention(0, A_ATT0, B_QM, R_QM % 2, 32)
            for p in range(6):
                operand_lo(A_MIX0 + p, p, GN_OUT, 36 + 2 * (p + 1))
            dve.wait_ge(sem("x_loaded"), 32)
            out_projection(0)
            residual(dve, R_FFN[0])
            norm(2, xn_late)
            for p in range(8):
                operand_lo(ffn_fill[0][p], p, GN_FFN, 48 + 2 * (p + 1))
            with dve.Fori(0, 2) as half:
                ffn_half(0, half)

            residual(dve, R_GM)
            norm(3, xn_late)
            for p in range(8):
                operand_lo(tok1_fill[p], p, GN_TOK + 16, 64 + 2 * (p + 1))
            for i in range(7):
                tail(B_GM + i)
                head(B_GM + i + 1)
                if i == 3:
                    dve.wait_ge(sem("vgain_loaded"), 16)
                    dve.wait_ge(sem("rstd_ready"), 10)
                    for m in range(2):
                        dve.scalar_tensor_tensor(out=vg[:, m], in0=vg[:, m], scalar=rstd[:, m:m + 1], in1=vgain[:],
                                                 op0=ALU.mult, op1=ALU.mult).then_inc(sem("v_normalised"), 1)
            for m in range(2):
                dve.wait_ge(result_drained[m], R_GM + 8)
            for m in range(2):
                for q in range(3):
                    n = A_SG + 3 * m + q
                    filled(dve, n)
                    for k in range(4):
                        i = 4 * q + k
                        e = dve.scalar_tensor_tensor(out=mix[:, m, i * P:(i + 1) * P], in0=aux[n % 4][:, k * P:(k + 1) * P],
                                                     scalar=gains[:, GN_BS + i:GN_BS + i + 1],
                                                     in1=ug[:, m, i * P:(i + 1) * P], op0=ALU.add, op1=ALU.mult)
                        if k < 3:
                            e.then_inc(sem("gate_part"), 1)
                    freed(e, n)
            attention(1, A_ATT1, B_GM + 6, (R_GM + 6) % 2, 80)
            for p in range(6):
                operand_lo(A_MIX1 + p, p, None, 84 + 2 * (p + 1))
            out_projection(1)
            residual(dve, R_FFN[1])
            norm(5, xn_late)
            for p in range(8):
                operand_lo(ffn_fill[1][p], p, GN_FFN + 16, 96 + 2 * (p + 1))
            ffn_half(1, 0)
            ffn_half(1, 1, last=True)

            residual(dve, R_END)
            dve.tensor_tensor_reduce(out=xn_late[:, 1], in0=h[:, 1], in1=h[:, 1], scale=1.0, scalar=0.0, op0=ALU.mult,
                                     op1=ALU.add, accum_out=stat[:, 1:2]).then_inc(sem("squares_summed1"), 1)
            dve.wait_ge(sem("final_gain_loaded"), 16)
            dve.wait_ge(sem("rstd_ready"), 14)
            dve.scalar_tensor_tensor(out=xn_late[:, 1], in0=h[:, 1], scalar=rstd[:, 1:2], in1=final_gain,
                                     op0=ALU.mult, op1=ALU.mult).then_inc(sem("output_ready1"), 1)

        @block.gpsimd
        def _(pool):
            def inverse_root(dst, src, width, mult, eps, name, first):
                pool.tensor_scalar(dst, src, mult, eps, ALU.mult, ALU.add).then_inc(sem(name), 1)
                pool.wait_ge(sem(name), first + 1)
                pool.tensor_tensor(dst, dst, neg_half[:, 0:width], ALU.pow).then_inc(sem(name), 1)

            def norm(r, width=D):
                for m in range(2):
                    pool.wait_ge(sem(f"squares_summed{m}"), r + 1)
                inverse_root(rstd[:], stat[:, 0:2], 2, 1.0 / width, EPS, "rstd_ready", 2 * r)

            pool.memset(neg_half[:], -0.5).then_inc(sem("filled_constants"), 1)
            for d in range(2):
                for half in range(2):
                    pool.wait_ge(sem("filled_constants"), 2 * d + half + 1)
                    other = slice((1 - half) * CHUNK, (2 - half) * CHUNK)
                    pool.memset(vn[other, d, half], 0.0).then_inc(sem("filled_constants"), 1)
            pool.wait_ge(sem("filled_constants"), 5)
            pool.memset(zeros[:], 0.0).then_inc(sem("filled_constants"), 1)
            pool.wait_ge(sem("filled_constants"), 6)
            norm(0)
            norm(1)
            pool.wait_ge(sem("gate_steps"), 12)
            pool.wait_ge(sem("gate_exps"), 7)

            def deltanet(g):
                rnd = g * (DN_AUX // 4)
                fil = lambda n: filled(pool, A_DN + n, rnd)
                have = lambda n: drained(pool, A_DN + n, rnd)
                heads = lambda v: v.unsqueeze(2).broadcast_to([P, 4, P])
                over = lambda v: v.unsqueeze(1).broadcast_to([P, 4, P])

                def zero(dst):
                    z = zeros[:, 0:dst.shape[2]].unsqueeze(1).broadcast_to([P, dst.shape[1], dst.shape[2]])
                    pool.tensor_tensor(dst, z, z, ALU.add).then_inc(sem("y_zeroed"), 1)

                for c in (0, 2 + SEQ):
                    pool.memset(xpad[:, :, c:c + 2], 0.0).then_inc(sem("padded"), 1)
                pool.tensor_copy(gs[:], gall[:, :, bass.ds(g * 4, 4)]).then_inc(sem("group_gates"), 1)
                pool.wait_ge(sem("group_gates"), g + 1)
                yield
                for X in range(2):
                    pool.wait_ge(sem("head_sums"), g * 6 + (3 * X + 3))
                    pool.tensor_tensor(rs[:, X].rearrange("p m h -> p (m h)"), ss[:, X].rearrange("p m h -> p (m h)"),
                                       neg_half[:], ALU.pow).then_inc(sem("head_rstd"), 1)
                yield
                for f in range(4):
                    d, m = f // 2, f % 2
                    if f >= 2:
                        have(DF + f - 2)
                    c = (C_UP, C_LO)[d]
                    pool.tensor_tensor(g_up[:, f % 2], over(cst[:, c:c + P]), heads(gs[:, 2 * (G_G + m) + d, :]), ALU.mult
                                       ).then_inc(sem("decay_operands"), 1)
                    c = (C_BIGF, C_BIGB)[d]
                    pool.tensor_tensor(g_big[:, f % 2], over(cst[:, c:c + P]), heads(gs[:, 2 * (G_GC + m) + d, :]), ALU.add
                                       ).then_inc(sem("decay_operands"), 1)
                yield
                fil(DG + 3)
                for d in range(2):
                    for m in range(2):
                        pool.tensor_tensor(qd[:, d, m], tok[:, 0, m].rearrange("p (h i) -> p h i", h=4),
                                           heads(gs[:, 2 * (G_EGC + m) + d, :]), ALU.mult).then_inc(sem("qd_done"), 1)
                for d in range(2):
                    for m in range(2):
                        have(DG + 2 * m)
                        have(DG + 2 * m + 1)
                        dst, c = ((XT[:, 0, m], C_M1T), (XL[:, 1, m], C_M1L))[d]
                        n = g * 8 + (4 * d + 2 * m + 1)
                        pool.tensor_tensor(dst, NT[:, d, m], over(cst[:, c:c + P]), ALU.mult).then_inc(sem("x0_pool"), 1)
                        pool.wait_ge(sem("x0_pool"), n)
                        pool.tensor_tensor(dst, dst, over(ident), ALU.add).then_inc(sem("x0_pool"), 1)
                yield
                for l, s in enumerate(LEVELS):
                    for d in range(2):
                        if l == 0:
                            have(DF + 3)
                            zero(Y[:, d].rearrange("p x (two s) -> p (x two) s", s=CHUNK))
                        else:
                            fil(level_aux(l - 1, d, "YX"))
                            zero(Y[:, d].rearrange("p x (b two s) -> p (x b) two s", two=2, s=s)[:, :, 1, :])
                    yield
                for d in range(2):
                    fil(level_aux(4, d, ("YX", "XY")[d]))
                    for m in range(2):
                        pool.tensor_tensor(keg[:, d, m], tok[:, 1, m].rearrange("p (h i) -> p h i", h=4),
                                           heads(gs[:, 2 * (G_EGC + m) + d, :]), ALU.mult).then_inc(sem("keg_done"), 1)
                yield
                fil(DJ + 7)
                for d in range(2):
                    for m in range(2):
                        pool.tensor_tensor(kdec[d][:, m], tok[:, 1, m].rearrange("p (h i) -> p h i", h=4),
                                           heads(gs[:, 2 * (G_EKD + m) + d, :]), ALU.mult).then_inc(sem("kdec_done"), 1)
                yield
                pool.wait_ge(sem("out_sums"), g * 3 + 3)
                pool.tensor_tensor(rs[:, 2].rearrange("p m h -> p (m h)"), ss[:, 2].rearrange("p m h -> p (m h)"),
                                   neg_half[:], ALU.pow).then_inc(sem("out_rstd"), 1)
                pool.wait_ge(sem("mixed"), g * 2 + 2)

            with pool.Fori(0, 3) as g:
                for _ in deltanet(g):
                    pass

            def square_hidden(layer, half, it, j):
                for m in range(2):
                    pool.wait_ge(result_drained[m], half * 12 + it * 2 + (R_FFN[layer] + j + 3))
                t = relu[:, j].rearrange("p m n -> p (m n)")
                pool.tensor_tensor(t, t, t, ALU.mult).then_inc(sem("squared"), 1)

            def ffn(layer):
                with pool.Fori(0, 2) as half:
                    with pool.Fori(0, 4) as it:
                        for j in range(2):
                            square_hidden(layer, half, it, j)

            norm(2)
            ffn(0)
            norm(3)
            norm(4, MIX)
            norm(5)
            ffn(1)
            norm(6)
            pool.wait_ge(sem("final_gain_loaded"), 16)
            pool.wait_ge(sem("scaled"), 1)
            pool.tensor_tensor(xn_late[:, 0], xn_late[:, 0], final_gain, ALU.mult).then_inc(sem("output_ready0"), 1)


_INS = ["x", "mem", "mem_norm_g", "tok_norm_g", "dn_w_in", "dn_conv_w", "dn_a_log", "dn_dt_bias", "dn_out_norm_g",
        "gm_w_in", "gm_v_norm_g", "gm_w_s", "gm_b_s", "mem_w_kv", "tok_w_out", "ffn_norm_g", "ffn_w1", "ffn_w2",
        "final_norm_g"]


def kernel(**inputs):
    import concourse.bacc as bacc
    from concourse.bass_utils import run_bass_kernel_spmd

    nc = bacc.Bacc("TRN2", target_bir_lowering=False, num_devices=1)
    arrays, args = {}, {}
    for name in _INS:
        a = np.ascontiguousarray(inputs[name])
        arrays[f"in_{name}"] = a
        args[name] = nc.dram_tensor(f"in_{name}", a.shape, mybir.dt.from_np(a.dtype), kind="ExternalInput").ap()
    arrays["in_consts"] = shape_constants()
    args["consts"] = nc.dram_tensor("in_consts", (P, C_ALL), F32, kind="ExternalInput").ap()
    out = nc.dram_tensor("out_0", (1, SEQ, D), F32, kind="ExternalOutput").ap()
    encoder_trunk(nc, out=out, **args)
    r = run_bass_kernel_spmd(nc, [arrays], core_ids=[0])
    return r.results[0]["out_0"]
```

```python
from contextlib import ExitStack
from itertools import chain

import numpy as np

import concourse.bass as bass
from concourse import mybir

F32 = mybir.dt.float32
F32R = mybir.dt.float32r
ACT = mybir.ActivationFunctionType
ALU = mybir.AluOpType
AX = mybir.AxisListType

P = 128
D = 2048
SEQ = 256
HD = 128
NH = 12
MIX = NH * HD
CONV = 5
HID = 8192
NB = 512
KT = D // P
SLABS = 8
EPS = 1e-6
LEVELS = (2, 4, 8, 16, 32, 64)
HALF = P // 2
BIG = 1e30

C_ID, C_UP, C_LO, C_BIGF, C_BIGB, C_M1L, C_M1T, C_ONE, C_LEV = (0, 128, 256, 384, 512, 640, 768, 896, 1024)
C_ALL = C_LEV + len(LEVELS) * HALF

G_G, G_GC, G_EGC, G_EKD, G_BETA, G_NEG = 0, 2, 4, 6, 8, 10
G_ROWS = 12


def shape_constants():
    i = np.arange(P)
    upper = i[:, None] <= i[None, :]
    c = np.zeros((P, C_ALL), np.float32)
    c[:, C_ID:C_ID + P] = np.eye(P)
    c[:, C_UP:C_UP + P] = upper
    c[:, C_LO:C_LO + P] = upper.T
    c[:, C_BIGF:C_BIGF + P] = np.where(upper, 0.0, BIG)
    c[:, C_BIGB:C_BIGB + P] = np.where(upper.T, 0.0, BIG)
    first = (i[:, None] % 2 == 1) & (i[None, :] == i[:, None] - 1)
    c[:, C_M1L:C_M1L + P] = -first.astype(np.float32)
    c[:, C_M1T:C_M1T + P] = -first.T.astype(np.float32)
    c[:, C_ONE:C_ONE + P] = 1.0
    j = np.arange(HALF)
    for n, s in enumerate(LEVELS):
        ok = (i[:, None] // (2 * s) == j[None, :] // s) & ((i[:, None] // s) % 2 == 1)
        c[:, C_LEV + n * HALF:C_LEV + (n + 1) * HALF] = ok
    return c


R_KV, R_QM, R_DN = 0, 4, 5
R_OUT = (17, 56)
R_FFN = (25, 60)
R_GM = 49
R_END = 84
B_QM, B_DN, B_GM = 4, 5, 53
B_OUT = (17, 60)
B_FFN = (21, 64)
B_LAST = 95
PART_A = (0, 1, 2, 3, 6, 7)
PART_B = (4, 5)

A_SMALL, A_MEMN, A_KT, A_XN, A_GATE, A_ATT0, A_DN = 0, 2, 10, 14, 22, 24, 36
DA, DD, DE, DV, DF, DG, DH, DI = 0, 6, 10, 14, 16, 20, 24, 28
DWV = DI + 6 * len(LEVELS) - 2
DST, DO1, DKS, DQS, DWR, DO2 = DWV + 2, DWV + 4, DWV + 6, DWV + 8, DWV + 10, DWV + 12
DN_AUX = DO2 + 2
A_MIX0 = A_DN + 2 * DN_AUX
A_DN2 = A_MIX0 + 4
A_MIX0B = A_DN2 + DN_AUX
A_FN0 = A_MIX0B + 2
A_FFN0 = A_FN0 + 8
A_TN1 = A_FFN0 + 32
A_WS = A_TN1 + 8
A_SG = A_WS + 3
A_ATT1 = A_SG + 6
A_MIX1 = A_ATT1 + 12
A_FN1 = A_MIX1 + 6
A_FFN1 = A_FN1 + 8
A_FFN = (A_FFN0, A_FFN1)
assert DN_AUX % 4 == 0

GN_MEM, GN_TOK, GN_FFN, GN_OUT, GN_BS = 0, 16, 48, 80, 81
N_SMALL = 93


def level_aux(l, direction, what):
    base = DI + 6 * l
    if l < len(LEVELS) - 1:
        return base + {("Y", 0): 0, ("Y", 1): 1, ("XY", 0): 2, ("YX", 0): 3, ("XY", 1): 4, ("YX", 1): 5}[what, direction]
    return base + {("Y", 0): 0, ("Y", 1): 1, ("YX", 0): 2, ("XY", 1): 3}[what, direction]


def encoder_trunk(nc, x, mem, consts, mem_norm_g, tok_norm_g, dn_w_in, dn_conv_w, dn_a_log, dn_dt_bias,
                  dn_out_norm_g, gm_w_in, gm_v_norm_g, gm_w_s, gm_b_s, mem_w_kv, tok_w_out, ffn_norm_g,
                  ffn_w1, ffn_w2, final_norm_g, out):
    ctx = ExitStack()
    sem_of = {}

    def sem(name):
        if name not in sem_of:
            sem_of[name] = ctx.enter_context(nc.semaphore(name))
        return sem_of[name]

    def sb(stack, name, shape, dt=F32):
        return stack.enter_context(nc.sbuf_tensor(name, shape, dt))

    with ctx:
        cst = sb(ctx, "cst", [P, C_ALL])
        raw = sb(ctx, "raw", [P, 4, 2, NB])
        w_hi = sb(ctx, "w_hi", [P, 2, 2, NB], F32R)
        w_lo = sb(ctx, "w_lo", [P, 2, 2, NB], F32R)
        xT_hi = sb(ctx, "xT_hi", [P, KT, SEQ], F32R)
        xT_lo = sb(ctx, "xT_lo", [P, KT, SEQ], F32R)
        h = sb(ctx, "h", [P, 2, D])
        memKT = sb(ctx, "memKT", [P, 2, 4, SEQ])
        memV = sb(ctx, "memV", [P, 2, 2, NB])
        mix = sb(ctx, "mix", [P, 2, MIX])
        gains = sb(ctx, "gains", [P, N_SMALL])
        conv_w = sb(ctx, "conv_w", [P, 180])
        stat = sb(ctx, "stat", [P, 4])
        rstd = sb(ctx, "rstd", [P, 2])
        neg_half = sb(ctx, "neg_half", [P, 8])
        amax = sb(ctx, "amax", [P, 8])
        nmax = sb(ctx, "nmax", [P, 8])
        asum = sb(ctx, "asum", [P, 8])
        arec = sb(ctx, "arec", [P, 8])
        zeros = sb(ctx, "zeros", [P, HALF])
        banks = [ctx.enter_context(nc.psum_tensor(f"pair{i}", [P, NB], F32)) for i in range(4)]
        aux = [ctx.enter_context(nc.psum_tensor(f"aux{i}", [P, NB], F32)) for i in range(4)]

        dn = ExitStack()
        r1 = sb(dn, "r1", [P, 6192])
        tok = sb(dn, "tok", [P, 3, 2, NB])
        kqT = sb(dn, "kqT", [P, 2, 4, SEQ])
        Y = sb(dn, "Y", [P, 2, 8, P])
        attnT = sb(dn, "attnT", [P, 2, 2, 4, P])
        state_out = sb(dn, "state_out", [P, 2, 2, NB])
        gall = sb(dn, "gall", [P, 2 * G_ROWS, NH])
        gs = sb(dn, "gs", [P, 2 * G_ROWS, 4])
        gx = sb(dn, "gx", [P, 96])
        gt = sb(dn, "gt", [P, 2, 48])
        gtmp = sb(dn, "gtmp", [P, 5, 2, 24])
        rows24 = sb(dn, "rows24", [P, 2, 24])
        ss = sb(dn, "ss", [P, 3, 2, 4])
        rs = sb(dn, "rs", [P, 3, 2, 4])
        before = ExitStack()
        wg_hi = sb(before, "wg_hi", [P, KT, 48], F32R)
        wg_lo = sb(before, "wg_lo", [P, KT, 48], F32R)
        before.close()
        proj = sb(dn, "proj", [P, 3, 2, NB])
        dn.close()
        small_rows = tok[0:N_SMALL, 0, 0, 0:P]
        conv_rows = tok[0:90, 1, 0, 0:256].rearrange("p (a c) -> p a c", a=2)
        wg = kqT[:].rearrange("p a h t -> p (a h t)")[:, 0:KT * 48].rearrange("p (k n) -> p k n", n=48)
        ktok = Y[:].rearrange("p d (m h) i -> p d m (h i)", m=2)
        xpad = r1[:, 0:12 * 260].rearrange("p (c t) -> p c t", c=12)
        conv = r1[:, 3120:3120 + 12 * SEQ].rearrange("p (c t) -> p c t", c=12)
        NT = r1[:, 0:2048].rearrange("p (d m h i) -> p d m h i", d=2, m=2, h=4)
        XL = r1[:, 2048:4096].rearrange("p (d m h i) -> p d m h i", d=2, m=2, h=4)
        XT = r1[:, 4096:6144].rearrange("p (d m h i) -> p d m h i", d=2, m=2, h=4)
        Wmat = [XT[:, 0], XL[:, 1]]
        S = state_out[:, 0].rearrange("p d (h i) -> p d h i", h=4)
        o = state_out[:, 1]
        g_up = Y[:].rearrange("p d (b h) i -> p (d b) h i", b=2)
        g_big = state_out[:].rearrange("p a b (h i) -> p (a b) h i", h=4)
        sq = attnT[:].rearrange("p a b h i -> p (a b) h i")
        by_head = lambda t: t.rearrange("p (h i) -> p h i", h=4)
        v_new = [by_head(tok[:, 0, d]) for d in range(2)]
        kdec = [by_head(tok[:, 1, d]) for d in range(2)]
        v_tok = [by_head(tok[:, 2, m]) for m in range(2)]
        xn_dn = r1[:, 0:4096].rearrange("p (m d) -> p m d", m=2)
        early = dict(q=r1[:, 4096:5120].rearrange("p (m c) -> p m c", m=2),
                     qT=r1[:, 5120:6144].rearrange("p (h t) -> p h t", h=4),
                     prob=r1[:, 0:2048].rearrange("p (m h t) -> p m h t", m=2, h=4),
                     probT=r1[:, 2048:4096].rearrange("p (m h t) -> p m h t", m=2, h=4))
        moT = memKT[:, 0]

        late = ExitStack()
        xn_late = sb(late, "xn_late", [P, 2, D])
        relu = sb(late, "relu", [P, 2, 2, NB])
        mixers = ExitStack()
        q_mem = sb(mixers, "q_mem", [P, 2, NB])
        q_memT = sb(mixers, "q_memT", [P, 4, SEQ])
        vg = sb(mixers, "vg", [P, 2, MIX])
        ug = sb(mixers, "ug", [P, 2, MIX])
        ws = sb(mixers, "ws", [P, NH, P])
        wsT = sb(mixers, "wsT", [P, NH, P])
        vgain = sb(mixers, "vgain", [P, MIX])
        mixers.close()
        hid_hi = sb(late, "hid_hi", [P, 32, SEQ], F32R)
        hid_lo = sb(late, "hid_lo", [P, 32, SEQ], F32R)
        late.close()
        late_heads = xn_late[:].rearrange("p m (h t) -> p m h t", h=8)
        buffers = (early, dict(q=q_mem[:], qT=q_memT[:], prob=late_heads[:, :, 0:4, :], probT=late_heads[:, :, 4:8, :]))
        final_gain = relu[:].rearrange("p a b n -> p (a b n)")

        ident = cst[:, C_ID:C_ID + P]
        ones = cst[:, C_ONE:C_ONE + P]

        landed = [sem(f"raw_landed{i}") for i in range(4)]
        hi_ready = sem("hi_ready")
        slabs_split = sem("slabs_split")
        slab_used = sem("slab_used")
        result_drained = [sem("result_drained0"), sem("result_drained1")]
        aux_filled = [sem(f"aux_filled{i}") for i in range(4)]
        aux_drained = [sem(f"aux_drained{i}") for i in range(4)]
        mem_fill = [A_MEMN + p for p in range(8)]
        x_fill = [A_XN + p for p in range(8)]
        mix_fill = [[A_MIX0 + p for p in range(4)] + [A_MIX0B, A_MIX0B + 1],
                    [A_MIX1 + p for p in range(6)] + [A_ATT1 + 10, A_ATT1 + 11]]
        ffn_fill = [[a + p for p in range(8)] for a in (A_FN0, A_FN1)]
        tok1_fill = [A_TN1 + p for p in range(8)]

        def filled(e, n, rounds=0):
            e.wait_ge(aux_filled[n % 4], rounds + (n // 4 + 1))

        def drained(e, n, rounds=0):
            e.wait_ge(aux_drained[n % 4], rounds + (n // 4 + 2))

        def may_fill(e, n, rounds=0):
            e.wait_ge(aux_drained[n % 4], rounds + (n // 4 + 1))

        def result(e, B):
            e.wait_ge(slab_used, B * 8 + 10)

        def slab_done(e, t):
            e.wait_ge(slab_used, t + 3)

        def residual(e, R):
            for m in range(2):
                e.wait_ge(result_drained[m], R + 2)

        def freed(ins, n):
            return ins.then_inc(aux_drained[n % 4], 1)

        def free_result(ins, m):
            return ins.then_inc(result_drained[m], 1)

        def beside(stages, steps):
            for _ in steps:
                next(stages, None)
            for _ in stages:
                pass

        block = ctx.enter_context(nc.Block())

        @block.sync
        def _(sp):
            def load(w, k0, n0, B, s):
                if isinstance(k0, int):
                    rows = w[k0 + s * 256:k0 + (s + 1) * 256]
                else:
                    rows = w[bass.ds(k0 + s * 256, 256)]
                src = rows[:, bass.ds(n0, NB)].rearrange("(k p) n -> p k n", p=P)
                if not (isinstance(B, int) and 8 * B + s < 4):
                    sp.wait_ge(slabs_split, B * 8 + (s + 1))
                sp.dma_start(raw[:, s % 4], src).then_inc(landed[s % 4], 16)

            def stream(w, n0, B, count):
                if count == 1:
                    for s in range(SLABS):
                        load(w, 0, n0, B, s)
                    return
                with sp.Fori(0, count) as i:
                    for s in range(SLABS):
                        load(w, 0, i * NB + n0, i + B, s)

            def stream_ffn(layer):
                with sp.Fori(0, 2) as half:
                    with sp.Fori(0, 8) as i:
                        for s in range(SLABS):
                            load(ffn_w1[layer], 0, half * (HID // 2) + i * NB, half * 16 + i + B_FFN[layer], s)
                    with sp.Fori(0, 4) as i:
                        for s in range(2 * SLABS):
                            B = half * 16 + i * 2 + (B_FFN[layer] + 8 + s // 8)
                            load(ffn_w2[layer], half * (HID // 2) + (s // 8) * D, i * NB, B, s % 8)

            sp.dma_start(h[:], mem[0].rearrange("(m p) d -> p m d", p=P)).then_inc(sem("mem_loaded"), 16)
            sp.dma_start(cst[:], consts).then_inc(sem("consts_loaded"), 16)
            for rows, k in ((mem_norm_g.rearrange("(k p) -> k p", p=P), GN_MEM),
                            (tok_norm_g.rearrange("l (k p) -> (l k) p", p=P), GN_TOK),
                            (ffn_norm_g.rearrange("l (k p) -> (l k) p", p=P), GN_FFN),
                            (dn_out_norm_g, GN_OUT), (gm_b_s[0], GN_BS)):
                n = rows.shape[0]
                sp.dma_start(small_rows[k:k + n, :], rows).then_inc(sem("rows_loaded"), 16)
            sp.dma_start(conv_rows, dn_conv_w[0].rearrange("t (c p) -> (t c) p", p=P)
                         .rearrange("(a r) p -> r a p", a=2)).then_inc(sem("rows_loaded"), 16)
            for n, row in enumerate((dn_a_log, dn_dt_bias)):
                sp.dma_start(rows24[:, n], row[0:1].rearrange("l a b -> l (a b)").broadcast_to([P, 24])
                             ).then_inc(sem("gate_rows_loaded"), 16)
            sp.dma_start(wg, dn_w_in[0][:, 4 * MIX:4 * MIX + 48].rearrange("(k p) n -> p k n", p=P)
                         ).then_inc(sem("gate_weights_loaded"), 16)
            stream(mem_w_kv[0], 0, 0, 1)
            stream(mem_w_kv[0], NB, 1, 1)
            sp.wait_ge(sem("normalised"), 2)
            sp.dma_start(h[:], x[0].rearrange("(m p) d -> p m d", p=P)).then_inc(sem("x_loaded"), 16)
            stream(mem_w_kv[1], 0, 2, 2)
            stream(dn_w_in[0], 4 * MIX + 48, B_QM, 1)
            with sp.Fori(1, 4) as g:
                for c, X in enumerate((3, 0, 1, 2)):
                    for s in range(SLABS):
                        load(dn_w_in[0], 0, g * NB + (X * MIX - NB), g * 4 + (B_DN - 4 + c), s)
            t = 8 * B_OUT[0]
            for part in (PART_A, PART_B):
                for n in range(4):
                    for p in part:
                        sp.wait_ge(slabs_split, t + 1)
                        sp.dma_start(raw[:, t % 4], tok_w_out[0][p * 256:(p + 1) * 256, n * NB:(n + 1) * NB]
                                     .rearrange("(k p) n -> p k n", p=P)).then_inc(landed[t % 4], 16)
                        t += 1
            stream_ffn(0)
            result(sp, B_GM - 1)
            sp.dma_start(ws[:], gm_w_s[0].rearrange("g i j -> i g j")).then_inc(sem("ws_loaded"), 16)
            sp.dma_start(vgain[:], gm_v_norm_g[0:1].broadcast_to([P, MIX])).then_inc(sem("vgain_loaded"), 16)
            stream(gm_w_in[0], MIX, B_GM, 3)
            stream(gm_w_in[0], 0, B_GM + 3, 3)
            stream(gm_w_in[0], 2 * MIX, B_GM + 6, 1)
            stream(tok_w_out[1], 0, B_OUT[1], 4)
            stream_ffn(1)
            result(sp, B_LAST - 2)
            sp.dma_start(final_gain, final_norm_g.rearrange("(a d) -> a d", a=1)
                         .broadcast_to([P, D])).then_inc(sem("final_gain_loaded"), 16)
            for m in range(2):
                sp.wait_ge(sem(f"output_ready{m}"), 1)
                sp.dma_start(out[0, m * P:(m + 1) * P, :], xn_late[:, m]).then_inc(sem("stored"), 16)
            sp.wait_ge(sem("stored"), 32)

        @block.tensor
        def _(pe):
            pe.sem_inc(slab_used, 2)

            def slab(B, s, R, parity, kt0, act_hi, act_lo, first, last):
                pe.wait_ge(slabs_split, B * 8 + (s + 5))
                for k in range(2):
                    kt = kt0 + k
                    start = first and k == 0
                    for m in range(2):
                        if start:
                            pe.wait_ge(result_drained[m], R + 1)
                        acc = banks[2 * parity + m][:]
                        tokens = slice(m * P, (m + 1) * P)
                        pe.matmul(acc, act_hi[:, kt, tokens], w_hi[:, s % 2, k], start=start, stop=False)
                        pe.matmul(acc, act_hi[:, kt, tokens], w_lo[:, s % 2, k], start=False, stop=False)
                        mm = pe.matmul(acc, act_lo[:, kt, tokens], w_hi[:, s % 2, k], start=False,
                                       stop=last and k == 1)
                mm.then_inc(slab_used, 1)

            def proj_block(B, R, parity, fill=None, between=None):
                for s in range(SLABS):
                    if fill is not None:
                        drained(pe, fill[s])
                    if s == 4 and between is not None:
                        between()
                    slab(B, s, R, parity, 2 * s, xT_hi, xT_lo, s == 0, s == SLABS - 1)

            def transposes(n, pieces, rounds=0):
                may_fill(pe, n, rounds)
                for col, src in pieces:
                    w = src.shape[0]
                    t = pe.transpose(aux[n % 4][0:src.shape[1], col:col + w], src, cst[0:w, C_ID:C_ID + w])
                t.then_inc(aux_filled[n % 4], 1)

            def pair_transposes(n, src, p, rounds=0):
                transposes(n, [((k * 2 + m) * P, src[:, m, (2 * p + k) * P:(2 * p + k + 1) * P])
                               for k in range(2) for m in range(2)], rounds)

            def norm_transposes(fill, src, count):
                pe.wait_ge(sem("normalised"), count)
                for p in range(8):
                    pair_transposes(fill[p], src, p)

            pe.wait_ge(sem("consts_loaded"), 16)
            pe.wait_ge(sem("rows_loaded"), 96)
            transposes(A_SMALL, [(0, small_rows)])
            transposes(A_SMALL + 1, [(0, conv_rows[:, 0, :]), (90, conv_rows[:, 1, :])])
            norm_transposes(mem_fill, xn_dn, 2)
            for b in range(4):
                proj_block(b, b, b % 2, fill=mem_fill)
            for layer in range(2):
                for m in range(2):
                    pe.wait_ge(result_drained[m], R_KV + 2 * layer + 3)
                for hp in range(2):
                    pair_transposes(A_KT + 2 * layer + hp, ktok[:, layer], hp)
            norm_transposes(x_fill, xn_dn, 4)

            proj_block(B_QM, R_QM, R_QM % 2, fill=x_fill)

            def gates():
                n = A_GATE
                may_fill(pe, n)
                pe.wait_ge(sem("gate_weights_split"), 1)
                for m in range(2):
                    for kt in range(KT):
                        for j, (a, b) in enumerate(((xT_hi, wg_hi), (xT_hi, wg_lo), (xT_lo, wg_hi))):
                            mm = pe.matmul(aux[n % 4][:, m * 48:(m + 1) * 48], a[:, kt, m * P:(m + 1) * P], b[:, kt],
                                           start=kt == 0 and j == 0, stop=kt == KT - 1 and j == 2)
                mm.then_inc(aux_filled[n % 4], 1)
                yield
                yield
                n = A_GATE + 1
                may_fill(pe, n)
                pe.wait_ge(sem("gate_steps"), 9)
                b = aux[n % 4]
                for m in range(2):
                    row = 2 * (G_G + m)
                    for d, c in ((0, C_UP), (1, C_LO)):
                        pe.matmul(b[:, m * 24 + d * 12:m * 24 + d * 12 + 12], cst[:, c:c + P],
                                  gall[:, row + d, :], start=True, stop=True)
                    mm = pe.matmul(b[:, 48 + m * 24:72 + m * 24], ones, gall[:, row:row + 2, :], start=True, stop=True)
                mm.then_inc(aux_filled[n % 4], 1)
                yield

            def attention(layer, n0, R):
                q, qT, prob, probT = (buffers[layer][k] for k in ("q", "qT", "prob", "probT"))
                for m in range(2):
                    pe.wait_ge(result_drained[m], R + 3)
                for hp in range(2):
                    pair_transposes(n0 + hp, q, hp)
                yield
                for m in range(2):
                    for hp in range(2):
                        n = n0 + 2 + 2 * m + hp
                        drained(pe, n0 + hp)
                        may_fill(pe, n)
                        for k in range(2):
                            mm = pe.matmul(aux[n % 4][:, k * 256:(k + 1) * 256], qT[:, 2 * hp + k, m * P:(m + 1) * P],
                                           memKT[:, layer, 2 * hp + k, :], start=True, stop=True)
                        mm.then_inc(aux_filled[n % 4], 1)
                    yield
                yield
                pe.wait_ge(sem("prob_ready"), 4 * layer + 4)
                for i in range(4):
                    transposes(n0 + 6 + i, [((mt * 2 + m) * P, prob[:, m, i, mt * P:(mt + 1) * P])
                                            for mt in range(2) for m in range(2)])
                yield
                for hp in range(2):
                    n = n0 + 10 + hp
                    drained(pe, n0 + 6 + 2 * hp)
                    drained(pe, n0 + 7 + 2 * hp)
                    may_fill(pe, n)
                    for k in range(2):
                        for mt in range(2):
                            mm = pe.matmul(aux[n % 4][:, k * 256:(k + 1) * 256],
                                           memV[:, layer, mt, (2 * hp + k) * P:(2 * hp + k + 1) * P],
                                           probT[:, mt, 2 * hp + k, :], start=mt == 0, stop=mt == 1)
                    mm.then_inc(aux_filled[n % 4], 1)
                yield

            def deltanet(g, base, rnd):
                bank = lambda n: aux[(base + n) % 4]
                fill = lambda n: may_fill(pe, base + n, rnd)
                have = lambda n: drained(pe, base + n, rnd)
                done = lambda mm, n: mm.then_inc(aux_filled[(base + n) % 4], 1)

                def product(n, lhs, rhs, width, mats):
                    fill(n)
                    for i in range(mats):
                        mm = pe.matmul(bank(n)[:, i * width:(i + 1) * width], lhs(i), rhs(i), start=True, stop=True)
                    done(mm, n)

                def by_tokens(X, n0):
                    pe.wait_ge(sem("silu_done"), g * 3 + (X + 1))
                    for m in range(2):
                        transposes(base + n0 + m,
                                   [(k * P, conv[:, 4 * X + k, m * P:(m + 1) * P]) for k in range(4)], rnd)

                for X in range(3):
                    for m in range(2):
                        pe.wait_ge(result_drained[m], g * 4 + (R_DN + X + 4))
                    for hp in range(2):
                        pair_transposes(base + DA + 2 * X + hp, proj[:, X], hp, rnd)
                    yield
                yield
                by_tokens(0, DD)
                yield
                yield
                by_tokens(1, DD + 2)
                yield
                yield
                for X in range(2):
                    for m in range(2):
                        have(DD + 2 * X + m)
                    for hp in range(2):
                        pair_transposes(base + DE + 2 * X + hp, tok[:, X], hp, rnd)
                yield
                by_tokens(2, DV)
                yield
                for f in range(4):
                    fill(DF + f)
                    pe.wait_ge(sem("decay_operands"), g * 8 + (2 * f + 1))
                    done(pe.matmul(bank(DF + f)[:], ones, g_up[:, f].rearrange("p h i -> p (h i)"),
                                   start=True, stop=True), DF + f)
                yield
                for n in range(4):
                    have(DE + n)
                for m in range(2):
                    for hp in range(2):
                        n = DG + 2 * m + hp
                        fill(n)
                        for k in range(2):
                            hh = 2 * hp + k
                            mm = pe.matmul(bank(n)[:, k * 256:(k + 1) * 256], kqT[:, 1, hh, m * P:(m + 1) * P],
                                           kqT[:, 0:2, hh, m * P:(m + 1) * P], start=True, stop=True)
                        done(mm, n)
                yield
                yield
                for d in range(2):
                    for m in range(2):
                        have(DG + 2 * m)
                        have(DG + 2 * m + 1)
                        transposes(base + DH + 2 * d + m, [(k * P, NT[:, d, m, k, :]) for k in range(4)], rnd)
                yield
                for l, s in enumerate(LEVELS):
                    last = l == len(LEVELS) - 1
                    halves = lambda t: t.rearrange("p (b two s) -> p b two s", two=2, s=s)
                    for d in range(2):
                        if l == 0:
                            if d == 0:
                                pe.wait_ge(sem("x0_vector"), g * 6 + 2)
                            pe.wait_ge(sem("x0_pool"), g * 8 + 4 * (d + 1))
                            for m in range(2):
                                have(DH + 2 * d + m)
                        else:
                            have(level_aux(l - 1, d, "XY"))
                        product(level_aux(l, d, "Y"), lambda i: NT[:, d, i // 4, i % 4, :],
                                lambda i: halves(XL[:, d, i // 4, i % 4, :])[:, :, 0, :], HALF, 8)
                    yield
                    for d in range(2):
                        if l == 0 and d == 1:
                            pe.wait_ge(sem("x0_vector"), g * 6 + 6)
                        if l > 0:
                            have(level_aux(l - 1, d, "YX"))
                        have(level_aux(l, d, "Y"))
                        if not (last and d == 0):
                            product(level_aux(l, d, "XY"), lambda i: XT[:, d, i // 4, i % 4, :],
                                    lambda i: halves(Y[:, d, i, :])[:, :, 0, :], HALF, 8)
                        if not (last and d == 1):
                            product(level_aux(l, d, "YX"), lambda i: Y[:, d, i, :],
                                    lambda i: halves(XT[:, d, i // 4, i % 4, :])[:, :, 1, :], HALF, 8)
                    yield
                have(level_aux(len(LEVELS) - 1, 0, "YX"))
                have(level_aux(len(LEVELS) - 1, 1, "XY"))
                for m in range(2):
                    have(DV + m)
                for d in range(2):
                    product(DWV + d, lambda i: Wmat[d][:, d, i, :], lambda i: v_tok[d][:, i, :], P, 4)
                yield
                for d in range(2):
                    have(DWV + d)
                    pe.wait_ge(sem("kdec_done"), g * 2 + (d + 1))
                    product(DST + d, lambda i: kdec[d][:, i, :], lambda i: v_new[d][:, i, :], P, 4)
                for d in range(2):
                    product(DO1 + d, lambda i: attnT[:, d, d, i, :], lambda i: v_new[d][:, i, :], P, 4)
                yield
                for X, n in ((1, DKS), (0, DQS)):
                    for d in range(2):
                        if X == 1:
                            have(DST + d)
                        product(n + d, lambda i: kqT[:, X, i, (1 - d) * P:(2 - d) * P], lambda i: S[:, d, i, :], P, 4)
                yield
                for d in range(2):
                    have(DKS + d)
                    product(DWR + d, lambda i: Wmat[d][:, 1 - d, i, :], lambda i: v_tok[1 - d][:, i, :], P, 4)
                yield
                for d in range(2):
                    have(DWR + d)
                    product(DO2 + d, lambda i: attnT[:, d, 1 - d, i, :], lambda i: v_new[d][:, i, :], P, 4)
                yield
                yield

            def heads_stream(g):
                for c in range(4):
                    for s in range(SLABS):
                        slab(g * 4 + (B_DN + c), s, g * 4 + (R_DN + c), (R_DN + c) % 2, 2 * s, xT_hi, xT_lo,
                             s == 0, s == SLABS - 1)
                        yield

            beside(chain(gates(), attention(0, A_ATT0, R_QM)), heads_stream(0))
            with pe.Fori(0, 2) as g:
                beside(deltanet(g, A_DN, g * (DN_AUX // 4)), heads_stream(g + 1))

            def projection_part(part, t, R):
                for n in range(4):
                    for j, p in enumerate(part):
                        if p < 6:
                            drained(pe, mix_fill[0][p])
                        else:
                            pe.wait_ge(sem("attention_split"), 1)
                        slab(t // 8, t % 8, R + n, (R + n) % 2, 2 * p, xT_hi, xT_lo, j == 0, j == len(part) - 1)
                        t += 1
                        yield

            pe.wait_ge(sem("mixed"), 4)
            for p in range(4):
                pair_transposes(A_MIX0 + p, mix, p)
            beside(deltanet(2, A_DN2, 0), projection_part(PART_A, 8 * B_OUT[0], R_OUT[0]))
            pe.wait_ge(sem("mixed"), 6)
            for p in range(4, 6):
                pair_transposes(mix_fill[0][p], mix, p)
            for _ in projection_part(PART_B, 8 * B_OUT[0] + 24, R_OUT[0] + 4):
                pass

            def out_projection():
                with pe.Fori(0, 2) as i:
                    for c in range(2):
                        R = R_OUT[1] + c
                        proj_block(i * 2 + (B_OUT[1] + c), i * 2 + R, R % 2, fill=mix_fill[1])

            def hidden_transposes(layer, half, it, j):
                pe.wait_ge(sem("squared"), half * 8 + it * 2 + (16 * layer + j + 1))
                for q in range(2):
                    pair_transposes(A_FFN[layer] + 2 * j + q, relu[:, j], q, half * 4 + it)

            def ffn(layer):
                with pe.Fori(0, 2) as half:
                    def up(it, j, between):
                        b = it * 2 + j
                        proj_block(half * 16 + b + B_FFN[layer], half * 12 + b + R_FFN[layer],
                                   (R_FFN[layer] + j) % 2, fill=ffn_fill[layer], between=between)
                    up(0, 0, None)
                    with pe.Fori(0, 3) as it:
                        up(it, 1, lambda: hidden_transposes(layer, half, it, 0))
                        up(it + 1, 0, lambda: hidden_transposes(layer, half, it, 1))
                    up(3, 1, lambda: hidden_transposes(layer, half, 3, 0))

                    def down(i, c, between):
                        for s in range(16):
                            if s == 4 and between is not None:
                                between()
                            drained(pe, A_FFN[layer] + s, half * 4)
                            slab(half * 16 + i * 2 + (B_FFN[layer] + 8 + 2 * c + s // 8), s % 8,
                                 half * 12 + i + (R_FFN[layer] + 8 + c), (R_FFN[layer] + c) % 2, 2 * s,
                                 hid_hi, hid_lo, s == 0, s == 15)
                    down(0, 0, lambda: hidden_transposes(layer, half, 3, 1))
                    down(0, 1, None)
                    down(2, 0, None)
                    down(2, 1, None)

            norm_transposes(ffn_fill[0], xn_late, 6)
            ffn(0)

            norm_transposes(tok1_fill, xn_late, 8)
            with pe.Fori(0, 3) as i:
                for c in range(2):
                    proj_block(i * 2 + (B_GM + c), i * 2 + (R_GM + c), (R_GM + c) % 2, fill=tok1_fill)
            proj_block(B_GM + 6, R_GM + 6, (R_GM + 6) % 2)
            pe.wait_ge(sem("ws_loaded"), 16)
            for q in range(3):
                transposes(A_WS + q, [(k * P, ws[:, 4 * q + k, :]) for k in range(4)])
            for q in range(3):
                drained(pe, A_WS + q)
            for m in range(2):
                pe.wait_ge(sem("v_normalised"), m + 1)
                for q in range(3):
                    n = A_SG + 3 * m + q
                    may_fill(pe, n)
                    for k in range(4):
                        i = 4 * q + k
                        mm = pe.matmul(aux[n % 4][:, k * P:(k + 1) * P], wsT[:, i, :], vg[:, m, i * P:(i + 1) * P],
                                       start=True, stop=True)
                    mm.then_inc(aux_filled[n % 4], 1)
            for _ in attention(1, A_ATT1, R_GM + 6):
                pass
            for n in range(6):
                drained(pe, A_SG + n)
            for p in range(6):
                pair_transposes(A_MIX1 + p, mix, p)
            out_projection()
            norm_transposes(ffn_fill[1], xn_late, 10)
            ffn(1)

        @block.scalar
        def _(act):
            def split(B, s):
                act.wait_ge(landed[s % 4], B * 32 + 16 * (s // 4 + 1))
                act.wait_ge(slab_used, B * 8 + (s + 1))
                act.activation(w_hi[:, s % 2], raw[:, s % 4], ACT.Copy).then_inc(hi_ready, 1)

            def head(B):
                for s in range(2):
                    split(B, s)

            def tail(B, between=None, at=5):
                for s in range(2, SLABS):
                    split(B, s)
                    if s == at and between is not None:
                        between()

            def copy_result(B, parity, m, dst, func=ACT.Copy):
                result(act, B)
                free_result(act.activation(dst, banks[2 * parity + m][:], func), m)

            def sum_squares(src, junk, m):
                act.activation(junk, src, ACT.Square, accum_out=stat[:, m:m + 1]).then_inc(sem(f"squares_summed{m}"), 1)

            def norm(r, xn):
                sum_squares(h[:, 0], xn[:, 0], 0)
                act.wait_ge(sem("rstd_ready"), 2 * r + 2)
                act.activation(xn[:, 0], h[:, 0], ACT.Copy, scale=rstd[:, 0:1]).then_inc(sem("normalised"), 1)

            def operand_hi(n, p, gain):
                filled(act, n)
                if gain is None:
                    act.activation(xT_hi[:, 2 * p:2 * p + 2, :], pair(n), ACT.Copy).then_inc(sem("xT_hi_ready"), 2)
                else:
                    for k in range(2):
                        c = gain + (2 * p + k) * (gain != GN_OUT)
                        act.activation(xT_hi[:, 2 * p + k, :], aux[n % 4][:, k * SEQ:(k + 1) * SEQ], ACT.Copy,
                                       scale=gains[:, c:c + 1]).then_inc(sem("xT_hi_ready"), 1)

            def copy_aux(n, dst, src):
                filled(act, n)
                freed(act.activation(dst, src, ACT.Copy), n)

            pair = lambda n: aux[n % 4][:].rearrange("p (k t) -> p k t", k=2)

            copy_aux(A_SMALL, gains[:], src=aux[A_SMALL % 4][:, 0:N_SMALL])
            copy_aux(A_SMALL + 1, conv_w[:], src=aux[(A_SMALL + 1) % 4][:, 0:180])
            head(0)
            act.wait_ge(sem("mem_loaded"), 16)
            norm(0, xn_dn)
            drained(act, A_SMALL)
            for p in range(8):
                operand_hi(mem_fill[p], p, GN_MEM)
            for b in range(4):
                tail(b)
                head(b + 1)
                dst = ktok[:, b // 2, 0, :] if b % 2 == 0 else memV[:, b // 2, 0, :]
                copy_result(b, b % 2, 0, dst)
                if b == 0:
                    act.wait_ge(sem("gate_weights_loaded"), 16)
                    act.activation(wg_hi[:], wg, ACT.Copy).then_inc(sem("gate_hi"), 1)
            for layer in range(2):
                for hp in range(2):
                    n = A_KT + 2 * layer + hp
                    copy_aux(n, memKT[:, layer, 2 * hp:2 * hp + 2, :], src=pair(n))
            filled(act, mem_fill[7])
            act.wait_ge(sem("x_loaded"), 16)
            norm(1, xn_dn)
            for p in range(8):
                operand_hi(x_fill[p], p, GN_TOK)
            tail(B_QM)
            head(B_QM + 1)
            copy_result(B_QM, R_QM % 2, 0, early["q"][:, 0])

            def gates():
                act.wait_ge(sem("gate_rows_loaded"), 32)
                act.activation(rows24[:, 0], rows24[:, 0], ACT.Exp).then_inc(sem("gate_exps"), 1)
                act.wait_ge(sem("gate_steps"), 4)
                act.activation(gtmp[:, 2], gtmp[:, 1], ACT.Exp).then_inc(sem("gate_exps"), 1)
                act.activation(gtmp[:, 3], gt[:, :, 24:48], ACT.Exp, scale=-1.0).then_inc(sem("gate_exps"), 1)
                act.wait_ge(sem("gate_exps"), 2)
                act.activation(gtmp[:, 4], gtmp[:, 2], ACT.Ln, bias=1.0).then_inc(sem("gate_exps"), 1)
                yield
                yield
                act.wait_ge(sem("gate_steps"), 12)
                act.activation(gall[:, 2 * G_EGC:2 * G_EGC + 4, :].rearrange("p r h -> p (r h)"),
                               gx[:, 0:48], ACT.Exp).then_inc(sem("gate_exps"), 1)
                act.activation(gall[:, 2 * G_EKD:2 * G_EKD + 4, :].rearrange("p r h -> p (r h)"),
                               gtmp[:, 0].rearrange("p m c -> p (m c)"), ACT.Exp).then_inc(sem("gate_exps"), 1)
                yield

            def attention(layer, n0):
                qT, prob, probT = (buffers[layer][k] for k in ("qT", "prob", "probT"))
                for hp in range(2):
                    copy_aux(n0 + hp, qT[:, 2 * hp:2 * hp + 2, :], src=pair(n0 + hp))
                yield
                for j in range(4):
                    n = n0 + 2 + j
                    act.wait_ge(sem("score_max"), 8 * layer + 2 * (j + 1))
                    for k in range(2):
                        c = 2 * j + k
                        e = act.activation(prob[:, j // 2, 2 * (j % 2) + k, :], aux[n % 4][:, k * SEQ:(k + 1) * SEQ],
                                           ACT.Exp, bias=nmax[:, c:c + 1], scale=HD ** -0.5, accum_out=asum[:, c:c + 1])
                        if k == 0:
                            e.then_inc(sem("exp_half"), 1)
                        else:
                            freed(e, n)
                    if j % 2:
                        yield
                yield
                for i in range(4):
                    n = n0 + 6 + i
                    copy_aux(n, probT[:, :, i, :], src=pair(n))
                yield
                for hp in range(2):
                    if layer == 0:
                        copy_aux(n0 + 10 + hp, moT[:, 2 * hp:2 * hp + 2, :], src=pair(n0 + 10 + hp))
                    else:
                        operand_hi(n0 + 10 + hp, 6 + hp, None)
                yield

            def deltanet(g, base, rnd):
                fil = lambda n: filled(act, base + n, rnd)
                bank = lambda n: aux[(base + n) % 4]
                halves = lambda n: bank(n)[:].rearrange("p (k t) -> p k t", k=2)
                free = lambda ins, n: freed(ins, base + n)

                def silu(X):
                    act.wait_ge(sem("conv_tap"), g * 60 + 20 * (X + 1))
                    act.activation(conv[:, 4 * X:4 * X + 4, :], conv[:, 4 * X:4 * X + 4, :], ACT.Silu
                                   ).then_inc(sem("silu_done"), 1)

                def squares(X):
                    for m in range(2):
                        n = DD + 2 * X + m
                        fil(n)
                        act.activation(sq[:, 2 * X + m], bank(n)[:].rearrange("p (h i) -> p h i", h=4), ACT.Square
                                       ).then_inc(sem("head_squares"), 1)

                for X in range(3):
                    for n in (2 * X, 2 * X + 1):
                        fil(DA + n)
                        free(act.activation(xpad[:, 2 * n:2 * n + 2, 2:2 + SEQ], halves(DA + n), ACT.Copy), DA + n)
                    yield
                silu(0)
                yield
                squares(0)
                yield
                silu(1)
                yield
                squares(1)
                yield
                yield
                silu(2)
                for X in range(2):
                    for hp in range(2):
                        n = DE + 2 * X + hp
                        fil(n)
                        free(act.activation(kqT[:, X, 2 * hp:2 * hp + 2, :], halves(n), ACT.Copy), n)
                yield
                for m in range(2):
                    fil(DV + m)
                    free(act.activation(tok[:, 2, m], bank(DV + m)[:], ACT.Copy), DV + m)
                yield
                for f in range(4):
                    drained(act, base + DF + f, rnd)
                    act.activation(NT[:, f // 2, f % 2], NT[:, f // 2, f % 2], ACT.Exp).then_inc(sem("decay_ready"), 1)
                yield
                yield
                yield
                for m in range(2):
                    n = DH + 2 + m
                    act.wait_ge(sem("x0_vector"), g * 6 + (3 + 2 * m))
                    act.wait_ge(sem("x0_pool"), g * 8 + (6 + 2 * m))
                    free(act.activation(NT[:, 1, m].rearrange("p h i -> p (h i)"), bank(n)[:], ACT.Copy), n)
                yield
                for _ in range(2 * len(LEVELS) + 1):
                    yield
                for d in range(2):
                    fil(DST + d)
                    free(act.activation(S[:, d], by_head(bank(DST + d)[:]), ACT.Copy), DST + d)
                yield
                yield
                yield
                yield
                for d in range(2):
                    drained(act, base + DO2 + d, rnd)
                for m in range(2):
                    act.activation(sq[:, m], by_head(o[:, m]), ACT.Square).then_inc(sem("out_squares"), 1)
                act.wait_ge(sem("mixed"), g * 2 + 2)
                yield

            def heads_stream(g):
                for c in range(4):
                    for s in range(SLABS):
                        B = g * 4 + (B_DN + c + (s + 2) // 8)
                        split(B, (s + 2) % 8)
                        if s == SLABS - 1:
                            B = g * 4 + (B_DN + c)
                            parity = (R_DN + c) % 2
                            if c == 0:
                                for m in range(2):
                                    copy_result(B, parity, m, mix[:, m, bass.ds(g * NB, NB)], ACT.Silu)
                            else:
                                copy_result(B, parity, 0, proj[:, c - 1, 0, :])
                        yield

            beside(chain(gates(), attention(0, A_ATT0)), heads_stream(0))
            with act.Fori(0, 2) as g:
                beside(deltanet(g, A_DN, g * (DN_AUX // 4)), heads_stream(g + 1))

            def out_part(t, count):
                for t in range(t, t + count):
                    split((t + 2) // 8, (t + 2) % 8)
                    yield

            for p in range(4):
                operand_hi(A_MIX0 + p, p, GN_OUT)
            act.activation(xT_hi[:, 12:16, :], moT, ACT.Copy).then_inc(sem("xT_hi_ready"), 4)
            beside(deltanet(2, A_DN2, 0), out_part(8 * B_OUT[0], 24))
            for p in range(4, 6):
                operand_hi(mix_fill[0][p], p, GN_OUT)
            for _ in out_part(8 * B_OUT[0] + 24, 8):
                pass

            def out_projection():
                with act.Fori(0, 4) as i:
                    tail(i + B_OUT[1])
                    head(i + (B_OUT[1] + 1))

            def hidden(layer, half, it, j):
                for q in range(2):
                    n = A_FFN[layer] + 2 * j + q
                    filled(act, n, half * 4 + it)
                    act.activation(hid_hi[:, bass.ds(it * 8 + (4 * j + 2 * q), 2), :], pair(n), ACT.Copy
                                   ).then_inc(sem("hidden_hi"), 1)

            def ffn_half(layer, half, last=False):
                def up(it, j, between):
                    tail(half * 16 + it * 2 + (B_FFN[layer] + j), between)
                    head(half * 16 + it * 2 + (B_FFN[layer] + j + 1))
                    copy_result(half * 16 + it * 2 + (B_FFN[layer] + j), (R_FFN[layer] + j) % 2, 0,
                                relu[:, j, 0, :], ACT.Relu)
                up(0, 0, None)
                with act.Fori(0, 3) as it:
                    up(it, 1, lambda: hidden(layer, half, it, 0))
                    up(it + 1, 0, lambda: hidden(layer, half, it, 1))
                up(3, 1, lambda: hidden(layer, half, 3, 0))
                tail(half * 16 + (B_FFN[layer] + 8), lambda: hidden(layer, half, 3, 1))
                with act.Fori(0, 7) as i:
                    head(half * 16 + i + (B_FFN[layer] + 9))
                    tail(half * 16 + i + (B_FFN[layer] + 9))
                if not last:
                    head(half * 16 + (B_FFN[layer] + 16))

            residual(act, R_FFN[0])
            norm(2, xn_late)
            for p in range(8):
                operand_hi(ffn_fill[0][p], p, GN_FFN)
            with act.Fori(0, 2) as half:
                ffn_half(0, half)

            residual(act, R_GM)
            norm(3, xn_late)
            for p in range(8):
                operand_hi(tok1_fill[p], p, GN_TOK + 16)
            for dst, b0 in ((vg, 0), (ug, 3)):
                for i in range(3):
                    B = B_GM + b0 + i
                    tail(B)
                    head(B + 1)
                    for m in range(2):
                        copy_result(B, (R_GM + b0 + i) % 2, m, dst[:, m, i * NB:(i + 1) * NB], ACT.Gelu_apprx_tanh)
                if b0 == 0:
                    for m in range(2):
                        act.wait_ge(result_drained[m], R_GM + 5)
                        sum_squares(vg[:, m], xn_late[:, m, 0:MIX], m)
            tail(B_GM + 6)
            head(B_GM + 7)
            for q in range(3):
                copy_aux(A_WS + q, wsT[:, 4 * q:4 * q + 4, :], src=aux[(A_WS + q) % 4][:].rearrange("p (k t) -> p k t", k=4))
            copy_result(B_GM + 6, (R_GM + 6) % 2, 0, q_mem[:, 0, :])
            for _ in attention(1, A_ATT1):
                pass
            for p in range(6):
                operand_hi(A_MIX1 + p, p, None)
            out_projection()
            residual(act, R_FFN[1])
            norm(5, xn_late)
            for p in range(8):
                operand_hi(ffn_fill[1][p], p, GN_FFN + 16)
            ffn_half(1, 0)
            ffn_half(1, 1, last=True)
            residual(act, R_END)
            sum_squares(h[:, 0], xn_late[:, 0], 0)
            act.wait_ge(sem("rstd_ready"), 14)
            act.activation(xn_late[:, 0], h[:, 0], ACT.Copy, scale=rstd[:, 0:1]).then_inc(sem("scaled"), 1)
            act.wait_ge(sem("scaled"), 1)

        @block.vector
        def _(dve):
            dve.sem_inc(slabs_split, 4)
            for m in range(2):
                dve.sem_inc(result_drained[m], 2)
            for b in range(4):
                dve.sem_inc(aux_drained[b], 1)

            def split(B, s):
                dve.wait_ge(hi_ready, B * 8 + (s + 1))
                dve.wait_ge(slab_used, B * 8 + (s + 1))
                dve.tensor_tensor(w_lo[:, s % 2], raw[:, s % 4], w_hi[:, s % 2].bitcast(F32), ALU.subtract
                                  ).then_inc(slabs_split, 1)

            def head(B):
                for s in range(2):
                    split(B, s)

            def tail(B, between=None, at=5):
                for s in range(2, SLABS):
                    split(B, s)
                    if s == at and between is not None:
                        between()

            def copy_result(B, parity, m, dst):
                result(dve, B)
                free_result(dve.tensor_copy(dst, banks[2 * parity + m][:]), m)

            def norm(r, xn):
                dve.tensor_tensor_reduce(out=xn[:, 1], in0=h[:, 1], in1=h[:, 1], scale=1.0, scalar=0.0, op0=ALU.mult,
                                         op1=ALU.add, accum_out=stat[:, 1:2]).then_inc(sem("squares_summed1"), 1)
                dve.wait_ge(sem("rstd_ready"), 2 * r + 2)
                dve.tensor_scalar(xn[:, 1], h[:, 1], rstd[:, 1:2], None, ALU.mult).then_inc(sem("normalised"), 1)

            def operand_lo(n, p, gain, hi_count):
                dve.wait_ge(sem("xT_hi_ready"), hi_count)
                if gain is None:
                    freed(dve.tensor_tensor(xT_lo[:, 2 * p:2 * p + 2, :], aux[n % 4][:].rearrange("p (k t) -> p k t", k=2),
                                            xT_hi[:, 2 * p:2 * p + 2, :].bitcast(F32), ALU.subtract), n)
                else:
                    for k in range(2):
                        c = gain + (2 * p + k) * (gain != GN_OUT)
                        e = dve.scalar_tensor_tensor(out=xT_lo[:, 2 * p + k, :], in0=aux[n % 4][:, k * SEQ:(k + 1) * SEQ],
                                                     scalar=gains[:, c:c + 1], in1=xT_hi[:, 2 * p + k, :].bitcast(F32),
                                                     op0=ALU.mult, op1=ALU.subtract)
                        if k == 0:
                            e.then_inc(sem("xT_lo_half"), 1)
                    freed(e, n)

            def rows(v, n):
                return v.unsqueeze(2).broadcast_to([P, 4, n])

            def over(v, n):
                return v.unsqueeze(1).broadcast_to([P, n, v.shape[1]])

            head(0)
            dve.wait_ge(sem("mem_loaded"), 16)
            norm(0, xn_dn)
            drained(dve, A_SMALL)
            for p in range(8):
                operand_lo(mem_fill[p], p, GN_MEM, 2 * (p + 1))
            for b in range(4):
                tail(b)
                head(b + 1)
                dst = ktok[:, b // 2, 1, :] if b % 2 == 0 else memV[:, b // 2, 1, :]
                copy_result(b, b % 2, 1, dst)
                if b == 0:
                    dve.wait_ge(sem("gate_hi"), 1)
                    dve.tensor_tensor(wg_lo[:], wg, wg_hi[:].bitcast(F32), ALU.subtract
                                      ).then_inc(sem("gate_weights_split"), 1)
            filled(dve, mem_fill[7])
            dve.wait_ge(sem("x_loaded"), 16)
            norm(1, xn_dn)
            for p in range(8):
                operand_lo(x_fill[p], p, GN_TOK, 16 + 2 * (p + 1))

            tail(B_QM)
            head(B_QM + 1)
            copy_result(B_QM, R_QM % 2, 1, early["q"][:, 1])

            def gates():
                steps = sem("gate_steps")
                n = A_GATE
                filled(dve, n)
                freed(dve.tensor_copy(gt[:].rearrange("p m c -> p (m c)"), aux[n % 4][:, 0:96]), n)
                drained(dve, n)
                dve.wait_ge(sem("gate_rows_loaded"), 32)
                dve.tensor_tensor(gtmp[:, 0], gt[:, :, 0:24], over(rows24[:, 1], 2), ALU.add).then_inc(steps, 1)
                dve.wait_ge(steps, 1)
                dve.tensor_scalar(gtmp[:, 1], gtmp[:, 0], -1.0, None, ALU.mult).then_inc(steps, 1)
                dve.wait_ge(steps, 2)
                dve.tensor_tensor(gtmp[:, 1], gtmp[:, 1], gtmp[:, 0], ALU.min).then_inc(steps, 1)
                dve.wait_ge(steps, 3)
                dve.tensor_scalar(gtmp[:, 0], gtmp[:, 0], 0.0, None, ALU.max).then_inc(steps, 1)
                yield
                dve.wait_ge(sem("gate_exps"), 4)
                dve.tensor_tensor(gtmp[:, 0], gtmp[:, 0], gtmp[:, 4], ALU.add).then_inc(steps, 1)
                dve.wait_ge(steps, 5)
                dve.tensor_tensor(gtmp[:, 0], gtmp[:, 0], over(rows24[:, 0], 2), ALU.mult).then_inc(steps, 1)
                dve.wait_ge(steps, 6)
                gm = lambda a: gall[:, 2 * a:2 * a + 4, :].rearrange("p (m d) h -> p m (d h)", m=2)
                dve.tensor_scalar(gm(G_G), gtmp[:, 0], -1.0, None, ALU.mult).then_inc(steps, 1)
                dve.tensor_scalar(gtmp[:, 3], gtmp[:, 3], 1.0, None, ALU.add).then_inc(steps, 1)
                dve.wait_ge(steps, 8)
                dve.reciprocal(gm(G_BETA), gtmp[:, 3]).then_inc(steps, 1)
                yield
                n = A_GATE + 1
                filled(dve, n)
                freed(dve.tensor_copy(gx[:], aux[n % 4][:, 0:96]), n)
                drained(dve, n)
                dve.tensor_copy(gm(G_GC), gx[:, 0:48].rearrange("p (m c) -> p m c", m=2)).then_inc(steps, 1)
                dve.tensor_tensor(gtmp[:, 0].rearrange("p m c -> p (m c)"), gx[:, 48:96], gx[:, 0:48], ALU.subtract
                                  ).then_inc(steps, 1)
                dve.tensor_copy(gtmp[:, 1].rearrange("p m c -> p (m c)"), gx[:, 0:48]).then_inc(steps, 1)
                dve.wait_ge(sem("gate_exps"), 5)
                dve.tensor_scalar(gm(G_NEG), gm(G_EGC), -1.0, None, ALU.mult).then_inc(steps, 1)
                yield

            def attention(layer, n0, hi_count=None):
                prob = buffers[layer]["prob"]
                yield
                for j in range(4):
                    n = n0 + 2 + j
                    filled(dve, n)
                    dve.tensor_reduce(amax[:, 2 * j:2 * j + 2], aux[n % 4][:].rearrange("p (k t) -> p k t", k=2),
                                      AX.X, ALU.max).then_inc(sem("score_max"), 1)
                    dve.wait_ge(sem("score_max"), 8 * layer + 2 * j + 1)
                    dve.tensor_scalar(nmax[:, 2 * j:2 * j + 2], amax[:, 2 * j:2 * j + 2], -(HD ** -0.5), None, ALU.mult
                                      ).then_inc(sem("score_max"), 1)
                    if j == 1:
                        yield
                for j in range(4):
                    drained(dve, n0 + 2 + j)
                dve.reciprocal(arec[:], asum[:]).then_inc(sem("sum_inverse"), 1)
                dve.wait_ge(sem("sum_inverse"), layer + 1)
                for j in range(4):
                    t = prob[:, j // 2, 2 * (j % 2):2 * (j % 2) + 2, :]
                    dve.tensor_tensor(t, t, arec[:, 2 * j:2 * j + 2].unsqueeze(2).broadcast_to([P, 2, SEQ]), ALU.mult
                                      ).then_inc(sem("prob_ready"), 1)
                yield
                yield
                yield
                if layer == 1:
                    for hp in range(2):
                        operand_lo(n0 + 10 + hp, 6 + hp, None, hi_count + 2 * (hp + 1))
                yield

            def deltanet(g, base, rnd):
                fil = lambda n: filled(dve, base + n, rnd)
                have = lambda n: drained(dve, base + n, rnd)
                bank = lambda n: aux[(base + n) % 4]
                heads = lambda n: by_head(bank(n)[:])
                free = lambda ins, n: freed(ins, base + n)
                beta = lambda m, d, hh: gs[:, 2 * (G_BETA + m) + d, hh:hh + 1]
                taps = sem("conv_tap")

                def convolve(part):
                    for X, tap in [divmod(i, CONV) for i in (2 * part, 2 * part + 1) if i < 3 * CONV]:
                        if tap == 0:
                            have(DA + 2 * X)
                            have(DA + 2 * X + 1)
                        for c in range(4):
                            ct = 4 * X + c
                            w = conv_w[:, bass.ds(g * 4 + (tap * 36 + X * 12 + c), 1)]
                            src = xpad[:, ct, tap:tap + SEQ]
                            if tap == 0:
                                e = dve.tensor_scalar(conv[:, ct], src, w, None, ALU.mult)
                            else:
                                dve.wait_ge(taps, g * 60 + (20 * X + 4 * (tap - 1) + c + 1))
                                e = dve.scalar_tensor_tensor(out=conv[:, ct], in0=src, scalar=w, in1=conv[:, ct],
                                                             op0=ALU.mult, op1=ALU.add)
                            e.then_inc(taps, 1)

                def square_sums(X):
                    for m in range(2):
                        dve.wait_ge(sem("head_squares"), g * 4 + (2 * X + m + 1))
                        dve.tensor_reduce(ss[:, X, m], sq[:, 2 * X + m], AX.X, ALU.add).then_inc(sem("head_sums"), 1)
                    f = float(HD) if X == 0 else 1.0
                    dve.wait_ge(sem("head_sums"), g * 6 + (3 * X + 2))
                    dve.tensor_scalar(ss[:, X], ss[:, X], f, f * EPS, ALU.mult, ALU.add).then_inc(sem("head_sums"), 1)

                def normalise(X):
                    for m in range(2):
                        n = DD + 2 * X + m
                        dve.wait_ge(sem("head_rstd"), g * 2 + (X + 1))
                        free(dve.tensor_tensor(by_head(tok[:, X, m]), heads(n), rows(rs[:, X, m], P), ALU.mult), n)

                dve.wait_ge(sem("padded"), g * 2 + 2)
                for part in range(8):
                    if part in (5, 7):
                        normalise((part - 5) // 2)
                    convolve(part)
                    if part in (4, 6):
                        square_sums((part - 4) // 2)
                    yield
                yield
                yield
                for f in range(4):
                    fil(DF + f)
                    dve.wait_ge(sem("decay_operands"), g * 8 + (2 * f + 2))
                    free(dve.tensor_tensor(NT[:, f // 2, f % 2], heads(DF + f), g_big[:, f], ALU.subtract), DF + f)
                yield
                dve.wait_ge(sem("decay_ready"), g * 4 + 4)
                dve.wait_ge(sem("head_sums"), g * 6 + 6)
                for m in range(2):
                    for hp in range(2):
                        n = DG + 2 * m + hp
                        fil(n)
                        view = bank(n)[:].rearrange("p (k two i) -> p k two i", k=2, two=2)
                        for d in range(2):
                            dve.tensor_tensor(attnT[:, d, m, 2 * hp:2 * hp + 2, :], view[:, :, 0, :],
                                              NT[:, d, m, 2 * hp:2 * hp + 2, :], ALU.mult).then_inc(sem("attn_ready"), 1)
                        dve.wait_ge(sem("attn_ready"), g * 8 + (2 * (2 * m + hp) + 2))
                        for d in range(2):
                            for k in range(2):
                                hh = 2 * hp + k
                                e = dve.scalar_tensor_tensor(out=NT[:, d, m, hh, :], in0=view[:, k, 1, :],
                                                             scalar=beta(m, d, hh), in1=NT[:, d, m, hh, :],
                                                             op0=ALU.mult, op1=ALU.mult)
                                if (d, k) != (1, 1):
                                    e.then_inc(sem("n_part"), 1)
                        free(e, n)
                    yield
                x0 = sem("x0_vector")
                for d in range(2):
                    for m in range(2):
                        n = DH + 2 * d + m
                        fil(n)
                        if d == 0:
                            free(dve.tensor_tensor(XL[:, 0, m], heads(n), over(cst[:, C_M1L:C_M1L + P], 4), ALU.mult), n)
                            have(n)
                            dve.tensor_tensor(XL[:, 0, m], XL[:, 0, m], over(ident, 4), ALU.add).then_inc(x0, 1)
                        else:
                            dve.tensor_tensor(XT[:, 1, m], heads(n), over(cst[:, C_M1T:C_M1T + P], 4), ALU.mult
                                              ).then_inc(x0, 1)
                            dve.wait_ge(x0, g * 6 + (3 + 2 * m))
                            dve.tensor_tensor(XT[:, 1, m], XT[:, 1, m], over(ident, 4), ALU.add).then_inc(x0, 1)
                yield
                for l, s in enumerate(LEVELS):
                    last = l == len(LEVELS) - 1
                    halves = lambda t: t.rearrange("p x (b two s) -> p x b two s", two=2, s=s)
                    mats = lambda t: t.rearrange("p m h i -> p (m h) i")
                    got = lambda n: bank(n)[:].rearrange("p (x b s) -> p x b s", x=8, s=s)
                    mask = cst[:, C_LEV + l * HALF:C_LEV + (l + 1) * HALF].rearrange("p (b s) -> p b s", s=s)
                    mask = mask.unsqueeze(1).broadcast_to([P, 8, HALF // s, s])
                    for d in range(2):
                        n = level_aux(l, d, "Y")
                        fil(n)
                        dve.wait_ge(sem("y_zeroed"), g * (2 * len(LEVELS)) + (2 * l + d + 1))
                        free(dve.tensor_tensor(halves(Y[:, d])[:, :, :, 0, :], got(n), mask, ALU.mult), n)
                    yield
                    for d in range(2):
                        if not (last and d == 0):
                            n = level_aux(l, d, "XY")
                            fil(n)
                            t = halves(mats(XL[:, d]))[:, :, :, 0, :]
                            free(dve.tensor_tensor(t, t, got(n), ALU.subtract), n)
                        if not (last and d == 1):
                            n = level_aux(l, d, "YX")
                            fil(n)
                            t = halves(mats(XT[:, d]))[:, :, :, 1, :]
                            free(dve.tensor_tensor(t, t, got(n), ALU.subtract), n)
                    yield

                def new_values(d, m, n):
                    fil(n)
                    free(dve.tensor_tensor(v_new[d], heads(n), rows(gs[:, 2 * (G_BETA + m) + d, :], P), ALU.mult), n)

                for d in range(2):
                    new_values(d, d, DWV + d)
                yield
                for d in range(2):
                    fil(DO1 + d)
                    free(dve.tensor_copy(o[:, d], bank(DO1 + d)[:]), DO1 + d)
                yield
                for n, kind in ((DKS, G_NEG), (DQS, G_EGC)):
                    for d in range(2):
                        m = 1 - d
                        fil(n + d)
                        if n == DQS:
                            have(DO1 + m)
                        dst = v_tok[m] if n == DKS else by_head(o[:, m])
                        for i in range(4):
                            e = dve.scalar_tensor_tensor(out=dst[:, i], in0=heads(n + d)[:, i],
                                                         scalar=gs[:, 2 * (kind + m) + d, i:i + 1],
                                                         in1=dst[:, i], op0=ALU.mult, op1=ALU.add)
                            if i < 3:
                                e.then_inc(sem("head_part"), 1)
                        free(e, n + d)
                yield
                for d in range(2):
                    new_values(d, 1 - d, DWR + d)
                yield
                for d in range(2):
                    m = 1 - d
                    fil(DO2 + d)
                    have(DQS + d)
                    free(dve.tensor_tensor(o[:, m], o[:, m], bank(DO2 + d)[:], ALU.add), DO2 + d)
                yield
                for m in range(2):
                    dve.wait_ge(sem("out_squares"), g * 2 + (m + 1))
                    dve.tensor_reduce(ss[:, 2, m], sq[:, m], AX.X, ALU.add).then_inc(sem("out_sums"), 1)
                dve.wait_ge(sem("out_sums"), g * 3 + 2)
                dve.tensor_scalar(ss[:, 2], ss[:, 2], 1.0 / HD, EPS, ALU.mult, ALU.add).then_inc(sem("out_sums"), 1)
                dve.wait_ge(sem("out_rstd"), g + 1)
                for m in range(2):
                    om = by_head(o[:, m])
                    dve.tensor_tensor(om, om, rows(rs[:, 2, m], P), ALU.mult).then_inc(sem("out_normed"), 1)
                for m in range(2):
                    dve.wait_ge(result_drained[m], g * 4 + (R_DN + 3))
                for m in range(2):
                    dve.wait_ge(sem("out_normed"), g * 2 + (m + 1))
                    t = mix[:, m, bass.ds(g * NB, NB)]
                    dve.tensor_tensor(t, o[:, m], t, ALU.mult).then_inc(sem("mixed"), 1)
                dve.wait_ge(sem("mixed"), g * 2 + 2)
                yield

            def heads_stream(g):
                for c in range(4):
                    for s in range(SLABS):
                        split(g * 4 + (B_DN + c + (s + 2) // 8), (s + 2) % 8)
                        if s == SLABS - 1 and c > 0:
                            copy_result(g * 4 + (B_DN + c), (R_DN + c) % 2, 1, proj[:, c - 1, 1, :])
                        yield

            beside(chain(gates(), attention(0, A_ATT0)), heads_stream(0))
            with dve.Fori(0, 2) as g:
                beside(deltanet(g, A_DN, g * (DN_AUX // 4)), heads_stream(g + 1))

            def out_part(part, t, R):
                for n in range(4):
                    for j in range(len(part)):
                        split((t + 2) // 8, (t + 2) % 8)
                        if j == len(part) - 1:
                            slab_done(dve, t)
                            for m in range(2):
                                v = h[:, m, n * NB:(n + 1) * NB]
                                free_result(dve.tensor_tensor(v, v, banks[2 * ((R + n) % 2) + m][:], ALU.add), m)
                        t += 1
                        yield

            for p in range(4):
                operand_lo(A_MIX0 + p, p, GN_OUT, 32 + 2 * (p + 1))
            dve.wait_ge(sem("xT_hi_ready"), 44)
            dve.tensor_tensor(xT_lo[:, 12:16, :], moT, xT_hi[:, 12:16, :].bitcast(F32), ALU.subtract
                              ).then_inc(sem("attention_split"), 1)
            beside(deltanet(2, A_DN2, 0), out_part(PART_A, 8 * B_OUT[0], R_OUT[0]))
            for p in range(4, 6):
                operand_lo(mix_fill[0][p], p, GN_OUT, 44 + 2 * (p - 3))
            residual(dve, R_OUT[0] + 4)
            for _ in out_part(PART_B, 8 * B_OUT[0] + 24, R_OUT[0] + 4):
                pass

            def add_result(B, parity, i):
                result(dve, B)
                for m in range(2):
                    t = h[:, m, bass.ds(i * NB, NB)]
                    free_result(dve.tensor_tensor(t, t, banks[2 * parity + m][:], ALU.add), m)

            def out_projection():
                with dve.Fori(0, 2) as i:
                    for c in range(2):
                        tail(i * 2 + (B_OUT[1] + c))
                        head(i * 2 + (B_OUT[1] + c + 1))
                        add_result(i * 2 + (B_OUT[1] + c), (R_OUT[1] + c) % 2, i * 2 + c)

            def hidden(layer, half, it, j):
                for q in range(2):
                    n = A_FFN[layer] + 2 * j + q
                    dve.wait_ge(sem("hidden_hi"), half * 16 + it * 4 + (32 * layer + 2 * j + q + 1))
                    t = bass.ds(it * 8 + (4 * j + 2 * q), 2)
                    freed(dve.tensor_tensor(hid_lo[:, t, :], aux[n % 4][:].rearrange("p (k t) -> p k t", k=2),
                                            hid_hi[:, t, :].bitcast(F32), ALU.subtract), n)

            def ffn_half(layer, half, last=False):
                def up(it, j, between):
                    B = half * 16 + it * 2 + (B_FFN[layer] + j)
                    tail(B, between)
                    head(half * 16 + it * 2 + (B_FFN[layer] + j + 1))
                    result(dve, B)
                    free_result(dve.tensor_scalar(relu[:, j, 1, :], banks[2 * ((R_FFN[layer] + j) % 2) + 1][:], 0.0, None,
                                                  ALU.max), 1)
                up(0, 0, None)
                with dve.Fori(0, 3) as it:
                    up(it, 1, lambda: hidden(layer, half, it, 0))
                    up(it + 1, 0, lambda: hidden(layer, half, it, 1))
                up(3, 1, lambda: hidden(layer, half, 3, 0))

                def down(i, c, between=None, end=False):
                    B = half * 16 + i * 2 + (B_FFN[layer] + 8 + 2 * c)
                    tail(B, between)
                    head(half * 16 + i * 2 + (B_FFN[layer] + 9 + 2 * c))
                    tail(half * 16 + i * 2 + (B_FFN[layer] + 9 + 2 * c))
                    if not end:
                        head(half * 16 + i * 2 + (B_FFN[layer] + 10 + 2 * c))
                    add_result(half * 16 + i * 2 + (B_FFN[layer] + 9 + 2 * c), (R_FFN[layer] + c) % 2, i + c)
                down(0, 0, lambda: hidden(layer, half, 3, 1))
                down(0, 1)
                down(2, 0)
                down(2, 1, end=last)

            residual(dve, R_FFN[0])
            norm(2, xn_late)
            for p in range(8):
                operand_lo(ffn_fill[0][p], p, GN_FFN, 48 + 2 * (p + 1))
            with dve.Fori(0, 2) as half:
                ffn_half(0, half)

            residual(dve, R_GM)
            norm(3, xn_late)
            for p in range(8):
                operand_lo(tok1_fill[p], p, GN_TOK + 16, 64 + 2 * (p + 1))
            for i in range(7):
                tail(B_GM + i)
                head(B_GM + i + 1)
                if i == 3:
                    dve.wait_ge(sem("vgain_loaded"), 16)
                    dve.wait_ge(sem("rstd_ready"), 10)
                    for m in range(2):
                        dve.scalar_tensor_tensor(out=vg[:, m], in0=vg[:, m], scalar=rstd[:, m:m + 1], in1=vgain[:],
                                                 op0=ALU.mult, op1=ALU.mult).then_inc(sem("v_normalised"), 1)
            for m in range(2):
                dve.wait_ge(result_drained[m], R_GM + 8)
            for m in range(2):
                for q in range(3):
                    n = A_SG + 3 * m + q
                    filled(dve, n)
                    for k in range(4):
                        i = 4 * q + k
                        e = dve.scalar_tensor_tensor(out=mix[:, m, i * P:(i + 1) * P], in0=aux[n % 4][:, k * P:(k + 1) * P],
                                                     scalar=gains[:, GN_BS + i:GN_BS + i + 1],
                                                     in1=ug[:, m, i * P:(i + 1) * P], op0=ALU.add, op1=ALU.mult)
                        if k < 3:
                            e.then_inc(sem("gate_part"), 1)
                    freed(e, n)
            copy_result(B_GM + 6, (R_GM + 6) % 2, 1, q_mem[:, 1, :])
            for _ in attention(1, A_ATT1, 80):
                pass
            for p in range(6):
                operand_lo(A_MIX1 + p, p, None, 84 + 2 * (p + 1))
            out_projection()
            residual(dve, R_FFN[1])
            norm(5, xn_late)
            for p in range(8):
                operand_lo(ffn_fill[1][p], p, GN_FFN + 16, 96 + 2 * (p + 1))
            ffn_half(1, 0)
            ffn_half(1, 1, last=True)

            residual(dve, R_END)
            dve.tensor_tensor_reduce(out=xn_late[:, 1], in0=h[:, 1], in1=h[:, 1], scale=1.0, scalar=0.0, op0=ALU.mult,
                                     op1=ALU.add, accum_out=stat[:, 1:2]).then_inc(sem("squares_summed1"), 1)
            dve.wait_ge(sem("final_gain_loaded"), 16)
            dve.wait_ge(sem("rstd_ready"), 14)
            dve.scalar_tensor_tensor(out=xn_late[:, 1], in0=h[:, 1], scalar=rstd[:, 1:2], in1=final_gain,
                                     op0=ALU.mult, op1=ALU.mult).then_inc(sem("output_ready1"), 1)

        @block.gpsimd
        def _(pool):
            def inverse_root(dst, src, width, mult, eps, name, first):
                pool.tensor_scalar(dst, src, mult, eps, ALU.mult, ALU.add).then_inc(sem(name), 1)
                pool.wait_ge(sem(name), first + 1)
                pool.tensor_tensor(dst, dst, neg_half[:, 0:width], ALU.pow).then_inc(sem(name), 1)

            def norm(r, width=D):
                for m in range(2):
                    pool.wait_ge(sem(f"squares_summed{m}"), r + 1)
                inverse_root(rstd[:], stat[:, 0:2], 2, 1.0 / width, EPS, "rstd_ready", 2 * r)

            pool.memset(neg_half[:], -0.5).then_inc(sem("filled_constants"), 1)
            pool.memset(zeros[:], 0.0).then_inc(sem("filled_constants"), 1)
            pool.wait_ge(sem("filled_constants"), 2)
            norm(0)
            norm(1)
            pool.wait_ge(sem("gate_steps"), 13)
            pool.wait_ge(sem("gate_exps"), 6)
            for hp in range(2):
                drained(pool, A_ATT0 + 10 + hp)

            def deltanet(g, base, rnd):
                fil = lambda n: filled(pool, base + n, rnd)
                have = lambda n: drained(pool, base + n, rnd)
                heads = lambda v: v.unsqueeze(2).broadcast_to([P, 4, P])
                over = lambda v: v.unsqueeze(1).broadcast_to([P, 4, P])
                flat = lambda t: t.rearrange("p m h -> p (m h)")

                def zero(dst):
                    z = zeros[:, 0:dst.shape[2]].unsqueeze(1).broadcast_to([P, dst.shape[1], dst.shape[2]])
                    pool.tensor_tensor(dst, z, z, ALU.add).then_inc(sem("y_zeroed"), 1)

                def decay_operands(f):
                    d, m = f // 2, f % 2
                    c = (C_UP, C_LO)[d]
                    pool.tensor_tensor(g_up[:, f], over(cst[:, c:c + P]), heads(gs[:, 2 * (G_G + m) + d, :]), ALU.mult
                                       ).then_inc(sem("decay_operands"), 1)
                    c = (C_BIGF, C_BIGB)[d]
                    pool.tensor_tensor(g_big[:, f], over(cst[:, c:c + P]), heads(gs[:, 2 * (G_GC + m) + d, :]), ALU.add
                                       ).then_inc(sem("decay_operands"), 1)

                for c in (0, 2 + SEQ):
                    pool.memset(xpad[:, :, c:c + 2], 0.0).then_inc(sem("padded"), 1)
                pool.tensor_copy(gs[:], gall[:, :, bass.ds(g * 4, 4)]).then_inc(sem("group_gates"), 1)
                pool.wait_ge(sem("group_gates"), g + 1)
                for f in range(4):
                    decay_operands(f)
                for X in range(2):
                    pool.wait_ge(sem("head_sums"), g * 6 + (3 * X + 3))
                    pool.tensor_tensor(flat(rs[:, X]), flat(ss[:, X]), neg_half[:], ALU.pow).then_inc(sem("head_rstd"), 1)
                for d in range(2):
                    for m in range(2):
                        have(DG + 2 * m)
                        have(DG + 2 * m + 1)
                        dst, c = ((XT[:, 0, m], C_M1T), (XL[:, 1, m], C_M1L))[d]
                        n = g * 8 + (4 * d + 2 * m + 1)
                        pool.tensor_tensor(dst, NT[:, d, m], over(cst[:, c:c + P]), ALU.mult).then_inc(sem("x0_pool"), 1)
                        pool.wait_ge(sem("x0_pool"), n)
                        pool.tensor_tensor(dst, dst, over(ident), ALU.add).then_inc(sem("x0_pool"), 1)
                for l, s in enumerate(LEVELS):
                    for d in range(2):
                        if l == 0:
                            zero(Y[:, d].rearrange("p x (two s) -> p (x two) s", s=HALF))
                        else:
                            fil(level_aux(l - 1, d, "YX"))
                            zero(Y[:, d].rearrange("p x (b two s) -> p (x b) two s", two=2, s=s)[:, :, 1, :])
                    if l == 0:
                        for d in range(2):
                            pool.tensor_tensor(kdec[d], kdec[d], heads(gs[:, 2 * (G_EKD + d) + d, :]), ALU.mult
                                               ).then_inc(sem("kdec_done"), 1)
                pool.wait_ge(sem("out_sums"), g * 3 + 3)
                pool.tensor_tensor(flat(rs[:, 2]), flat(ss[:, 2]), neg_half[:], ALU.pow).then_inc(sem("out_rstd"), 1)
                pool.wait_ge(sem("mixed"), g * 2 + 2)

            with pool.Fori(0, 2) as g:
                deltanet(g, A_DN, g * (DN_AUX // 4))
            deltanet(2, A_DN2, 0)

            def square_hidden(layer, half, it, j):
                for m in range(2):
                    pool.wait_ge(result_drained[m], half * 12 + it * 2 + (R_FFN[layer] + j + 3))
                t = relu[:, j].rearrange("p m n -> p (m n)")
                pool.tensor_tensor(t, t, t, ALU.mult).then_inc(sem("squared"), 1)

            def ffn(layer):
                with pool.Fori(0, 2) as half:
                    with pool.Fori(0, 4) as it:
                        for j in range(2):
                            square_hidden(layer, half, it, j)

            norm(2)
            ffn(0)
            norm(3)
            norm(4, MIX)
            norm(5)
            ffn(1)
            norm(6)
            pool.wait_ge(sem("final_gain_loaded"), 16)
            pool.wait_ge(sem("scaled"), 1)
            pool.tensor_tensor(xn_late[:, 0], xn_late[:, 0], final_gain, ALU.mult).then_inc(sem("output_ready0"), 1)


_INS = ["x", "mem", "mem_norm_g", "tok_norm_g", "dn_w_in", "dn_conv_w", "dn_a_log", "dn_dt_bias", "dn_out_norm_g",
        "gm_w_in", "gm_v_norm_g", "gm_w_s", "gm_b_s", "mem_w_kv", "tok_w_out", "ffn_norm_g", "ffn_w1", "ffn_w2",
        "final_norm_g"]


def kernel(**inputs):
    import concourse.bacc as bacc
    from concourse.bass_utils import run_bass_kernel_spmd

    nc = bacc.Bacc("TRN2", target_bir_lowering=False, num_devices=1)
    arrays, args = {}, {}
    for name in _INS:
        a = np.ascontiguousarray(inputs[name])
        arrays[f"in_{name}"] = a
        args[name] = nc.dram_tensor(f"in_{name}", a.shape, mybir.dt.from_np(a.dtype), kind="ExternalInput").ap()
    arrays["in_consts"] = shape_constants()
    args["consts"] = nc.dram_tensor("in_consts", (P, C_ALL), F32, kind="ExternalInput").ap()
    out = nc.dram_tensor("out_0", (1, SEQ, D), F32, kind="ExternalOutput").ap()
    encoder_trunk(nc, out=out, **args)
    r = run_bass_kernel_spmd(nc, [arrays], core_ids=[0])
    return r.results[0]["out_0"]
```

```python
from contextlib import ExitStack
from itertools import chain

import numpy as np

import concourse.bass as bass
from concourse import mybir

F32 = mybir.dt.float32
F32R = mybir.dt.float32r
ACT = mybir.ActivationFunctionType
ALU = mybir.AluOpType
AX = mybir.AxisListType

P = 128
D = 2048
SEQ = 256
HD = 128
NH = 12
MIX = NH * HD
CONV = 5
HID = 8192
NB = 512
KT = D // P
SLABS = 8
EPS = 1e-6
LEVELS = (2, 4, 8, 16, 32, 64)
HALF = P // 2
BIG = 1e30

C_ID, C_UP, C_LO, C_BIGF, C_BIGB, C_M1L, C_M1T, C_ONE, C_LEV = (0, 128, 256, 384, 512, 640, 768, 896, 1024)
C_ALL = C_LEV + len(LEVELS) * HALF

G_G, G_GC, G_EGC, G_EKD, G_BETA, G_NEG = 0, 2, 4, 6, 8, 10
G_ROWS = 12


def shape_constants():
    i = np.arange(P)
    upper = i[:, None] <= i[None, :]
    c = np.zeros((P, C_ALL), np.float32)
    c[:, C_ID:C_ID + P] = np.eye(P)
    c[:, C_UP:C_UP + P] = upper
    c[:, C_LO:C_LO + P] = upper.T
    c[:, C_BIGF:C_BIGF + P] = np.where(upper, 0.0, BIG)
    c[:, C_BIGB:C_BIGB + P] = np.where(upper.T, 0.0, BIG)
    first = (i[:, None] % 2 == 1) & (i[None, :] == i[:, None] - 1)
    c[:, C_M1L:C_M1L + P] = -first.astype(np.float32)
    c[:, C_M1T:C_M1T + P] = -first.T.astype(np.float32)
    c[:, C_ONE:C_ONE + P] = 1.0
    j = np.arange(HALF)
    for n, s in enumerate(LEVELS):
        ok = (i[:, None] // (2 * s) == j[None, :] // s) & ((i[:, None] // s) % 2 == 1)
        c[:, C_LEV + n * HALF:C_LEV + (n + 1) * HALF] = ok
    return c


R_KV, R_QM, R_DN = 0, 4, 5
R_OUT = (17, 56)
R_FFN = (25, 60)
R_GM = 49
R_END = 84
B_QM, B_DN, B_GM = 4, 5, 53
B_OUT = (17, 60)
B_FFN = (21, 64)
B_LAST = 95
PART_A = (0, 1, 2, 3, 6, 7)
PART_B = (4, 5)

A_SMALL, A_MEMN, A_KT, A_XN, A_GATE, A_ATT0, A_DN = 0, 2, 10, 14, 22, 24, 36
DA, DD, DE, DF, DG, DH, DI = 0, 6, 10, 14, 18, 22, 26
DV = DI + 12
DWV = DI + 6 * len(LEVELS)
DST, DO1, DKS, DQS, DWR, DO2 = DWV + 2, DWV + 4, DWV + 6, DWV + 8, DWV + 10, DWV + 12
DN_AUX = DO2 + 2
A_MIX0 = A_DN + 2 * DN_AUX
A_DN2 = A_MIX0 + 4
A_MIX0B = A_DN2 + DN_AUX
A_FN0 = A_MIX0B + 2
A_FFN0 = A_FN0 + 8
A_TN1 = A_FFN0 + 32
A_WS = A_TN1 + 8
A_SG = A_WS + 3
A_ATT1 = A_SG + 6
A_MIX1 = A_ATT1 + 12
A_FN1 = A_MIX1 + 6
A_FFN1 = A_FN1 + 8
A_FFN = (A_FFN0, A_FFN1)
assert DN_AUX % 4 == 0

REFILL = ((), (0,), (1,), (2,), (3,), (4,), (5,), (), (), (6, 7))
REFILL_OUT = ((), (), (0,), (1,), (2,), (3,), (), (4,), (5,), (6, 7))
REFILL_FIRST = ((2,), (3,), (4,), (5,), (6,), (7,))
ALONE = range(16, 26)
MIX_REFILL = ((), (0,), (1,), (2,), (3,), (), (), (), (), (4,), (5,))
N_MEM, N_X, N_FFN0, N_TOK1, N_V, N_FFN1, N_FINAL = range(7)

GN_MEM, GN_TOK, GN_FFN, GN_OUT, GN_BS = 0, 16, 48, 80, 81
N_SMALL = 93


def level_aux(l, direction, what):
    base = DI + 6 * l + 2 * (l > 1)
    if l < len(LEVELS) - 1:
        return base + {("Y", 0): 0, ("Y", 1): 1, ("XY", 0): 2, ("YX", 0): 3, ("XY", 1): 4, ("YX", 1): 5}[what, direction]
    return base + {("Y", 0): 0, ("Y", 1): 1, ("YX", 0): 2, ("XY", 1): 3}[what, direction]


def encoder_trunk(nc, x, mem, consts, mem_norm_g, tok_norm_g, dn_w_in, dn_conv_w, dn_a_log, dn_dt_bias,
                  dn_out_norm_g, gm_w_in, gm_v_norm_g, gm_w_s, gm_b_s, mem_w_kv, tok_w_out, ffn_norm_g,
                  ffn_w1, ffn_w2, final_norm_g, out):
    ctx = ExitStack()
    sem_of = {}

    def sem(name):
        if name not in sem_of:
            sem_of[name] = ctx.enter_context(nc.semaphore(name))
        return sem_of[name]

    def sb(stack, name, shape, dt=F32):
        return stack.enter_context(nc.sbuf_tensor(name, shape, dt))

    with ctx:
        cst = sb(ctx, "cst", [P, C_ALL])
        raw = sb(ctx, "raw", [P, 4, 2, NB])
        w_hi = sb(ctx, "w_hi", [P, 2, 2, NB], F32R)
        w_lo = sb(ctx, "w_lo", [P, 2, 2, NB], F32R)
        xT_hi = sb(ctx, "xT_hi", [P, KT, SEQ], F32R)
        xT_lo = sb(ctx, "xT_lo", [P, KT, SEQ], F32R)
        h = sb(ctx, "h", [P, 2, D])
        memKT = sb(ctx, "memKT", [P, 2, 4, SEQ])
        memV = sb(ctx, "memV", [P, 2, 2, NB])
        mix = sb(ctx, "mix", [P, 2, MIX])
        gains = sb(ctx, "gains", [P, N_SMALL])
        conv_w = sb(ctx, "conv_w", [P, 180])
        stat = sb(ctx, "stat", [P, 2, 2])
        rstd = sb(ctx, "rstd", [P, 2, 2])
        parts = sb(ctx, "parts", [P, 2, 4])
        neg_half = sb(ctx, "neg_half", [P, 8])
        amax = sb(ctx, "amax", [P, 8])
        nmax = sb(ctx, "nmax", [P, 8])
        asum = sb(ctx, "asum", [P, 8])
        arec = sb(ctx, "arec", [P, 8])
        zeros = sb(ctx, "zeros", [P, HALF])
        banks = [ctx.enter_context(nc.psum_tensor(f"pair{i}", [P, NB], F32)) for i in range(4)]
        aux = [ctx.enter_context(nc.psum_tensor(f"aux{i}", [P, NB], F32)) for i in range(4)]

        dn = ExitStack()
        r1 = sb(dn, "r1", [P, 6192])
        tok = sb(dn, "tok", [P, 3, 2, NB])
        kqT = sb(dn, "kqT", [P, 2, 4, SEQ])
        Y = sb(dn, "Y", [P, 2, 8, P])
        attnT = sb(dn, "attnT", [P, 2, 2, 4, P])
        state_out = sb(dn, "state_out", [P, 2, 2, NB])
        gall = sb(dn, "gall", [P, 2 * G_ROWS, NH])
        gs = sb(dn, "gs", [P, 2 * G_ROWS, 4])
        gx = sb(dn, "gx", [P, 96])
        gt = sb(dn, "gt", [P, 2, 48])
        gtmp = sb(dn, "gtmp", [P, 5, 2, 24])
        rows24 = sb(dn, "rows24", [P, 2, 24])
        ss = sb(dn, "ss", [P, 3, 2, 4])
        rs = sb(dn, "rs", [P, 3, 2, 4])
        before = ExitStack()
        wg_hi = sb(before, "wg_hi", [P, KT, 48], F32R)
        wg_lo = sb(before, "wg_lo", [P, KT, 48], F32R)
        before.close()
        projections = sb(dn, "projections", [P, 3 * 2 * NB + 16])
        dn.close()
        small_rows = tok[0:N_SMALL, 0, 0, 0:P]
        conv_rows = tok[0:90, 1, 0, 0:256].rearrange("p (a c) -> p a c", a=2)
        wg = kqT[:].rearrange("p a h t -> p (a h t)")[:, 0:KT * 48].rearrange("p (k n) -> p k n", n=48)
        ktok = Y[:].rearrange("p d (m h) i -> p d m (h i)", m=2)
        proj = projections[:, 0:3 * 2 * NB].rearrange("p (x m c) -> p x m c", x=3, m=2)
        padded = SEQ + CONV - 1
        qk_pad = r1[:, 0:8 * padded].rearrange("p (x c t) -> p x c t", x=2, c=4)
        qk_conv = r1[:, 8 * padded:8 * padded + 8 * SEQ].rearrange("p (x c t) -> p x c t", x=2, c=4)
        v_pad = projections[:, 4 * NB:4 * NB + 4 * padded].rearrange("p (c t) -> p c t", c=4)
        xpad = [qk_pad[:, 0], qk_pad[:, 1], v_pad]
        conv = [qk_conv[:, 0], qk_conv[:, 1], projections[:, 2 * NB:4 * NB].rearrange("p (c t) -> p c t", c=4)]
        NT = r1[:, 0:2048].rearrange("p (d m h i) -> p d m h i", d=2, m=2, h=4)
        XL = r1[:, 2048:4096].rearrange("p (d m h i) -> p d m h i", d=2, m=2, h=4)
        XT = r1[:, 4096:6144].rearrange("p (d m h i) -> p d m h i", d=2, m=2, h=4)
        Wmat = [XT[:, 0], XL[:, 1]]
        S = state_out[:, 0].rearrange("p d (h i) -> p d h i", h=4)
        o = state_out[:, 1]
        g_up = Y[:].rearrange("p d (b h) i -> p (d b) h i", b=2)
        g_big = state_out[:].rearrange("p a b (h i) -> p (a b) h i", h=4)
        sq = attnT[:].rearrange("p a b h i -> p (a b) h i")
        by_head = lambda t: t.rearrange("p (h i) -> p h i", h=4)
        v_new = [by_head(tok[:, 0, d]) for d in range(2)]
        kdec = [by_head(tok[:, 1, d]) for d in range(2)]
        v_tok = [by_head(tok[:, 2, m]) for m in range(2)]
        mem_tok = r1[:, 0:4096].rearrange("p (m d) -> p m d", m=2)
        junk_early = [attnT[:].rearrange("p a b h i -> p (a b h i)"), state_out[:].rearrange("p a b n -> p (a b n)")]
        early = dict(q=r1[:, 4096:5120].rearrange("p (m c) -> p m c", m=2),
                     qT=r1[:, 5120:6144].rearrange("p (h t) -> p h t", h=4),
                     prob=r1[:, 0:2048].rearrange("p (m h t) -> p m h t", m=2, h=4),
                     probT=r1[:, 2048:4096].rearrange("p (m h t) -> p m h t", m=2, h=4))
        moT = [memKT[:, layer] for layer in range(2)]

        late = ExitStack()
        xn_late = sb(late, "xn_late", [P, 2, D])
        relu = sb(late, "relu", [P, 2, 2, NB])
        mixers = ExitStack()
        q_mem = sb(mixers, "q_mem", [P, 2, NB])
        q_memT = sb(mixers, "q_memT", [P, 4, SEQ])
        vg = sb(mixers, "vg", [P, 2, MIX])
        ug = sb(mixers, "ug", [P, 2, MIX])
        ws = sb(mixers, "ws", [P, NH, P])
        wsT = sb(mixers, "wsT", [P, NH, P])
        vgain = sb(mixers, "vgain", [P, MIX])
        mixers.close()
        hid_hi = sb(late, "hid_hi", [P, 32, SEQ], F32R)
        hid_lo = sb(late, "hid_lo", [P, 32, SEQ], F32R)
        late.close()
        late_heads = xn_late[:].rearrange("p m (h t) -> p m h t", h=8)
        buffers = (early, dict(q=q_mem[:], qT=q_memT[:], prob=late_heads[:, :, 0:4, :], probT=late_heads[:, :, 4:8, :]))
        final_gain = memV[:].rearrange("p a b n -> p (a b n)")

        ident = cst[:, C_ID:C_ID + P]
        ones = cst[:, C_ONE:C_ONE + P]

        landed = [sem(f"raw_landed{i}") for i in range(4)]
        hi_ready = sem("hi_ready")
        slabs_split = sem("slabs_split")
        slab_used = sem("slab_used")
        result_drained = [sem("result_drained0"), sem("result_drained1")]
        aux_filled = [sem(f"aux_filled{i}") for i in range(4)]
        aux_drained = [sem(f"aux_drained{i}") for i in range(4)]
        mem_fill = [A_MEMN + p for p in range(8)]
        x_fill = [A_XN + p for p in range(8)]
        mix_fill = [[A_MIX0 + p for p in range(4)] + [A_MIX0B, A_MIX0B + 1],
                    [A_MIX1 + p for p in range(6)]]
        ffn_fill = [[a + p for p in range(8)] for a in (A_FN0, A_FN1)]
        tok1_fill = [A_TN1 + p for p in range(8)]

        def filled(e, n, rounds=0):
            e.wait_ge(aux_filled[n % 4], rounds + (n // 4 + 1))

        def drained(e, n, rounds=0):
            e.wait_ge(aux_drained[n % 4], rounds + (n // 4 + 2))

        def may_fill(e, n, rounds=0):
            e.wait_ge(aux_drained[n % 4], rounds + (n // 4 + 1))

        def result(e, B):
            e.wait_ge(slab_used, B * 8 + 10)

        def norm_known(e, r):
            e.wait_ge(sem("rstd_ready"), 2 * r + 2)

        def slab_done(e, t):
            e.wait_ge(slab_used, t + 3)

        def residual(e, R):
            for m in range(2):
                e.wait_ge(result_drained[m], R + 2)

        def freed(ins, n):
            return ins.then_inc(aux_drained[n % 4], 1)

        def free_result(ins, m):
            return ins.then_inc(result_drained[m], 1)

        def beside(stages, steps, alone=()):
            n = 0
            for _ in steps:
                next(stages, None)
                n += 1
                while n in alone:
                    next(stages, None)
                    n += 1
            finish(stages)

        def finish(stages):
            for _ in stages:
                pass

        block = ctx.enter_context(nc.Block())

        @block.sync
        def _(sp):
            def load(w, k0, n0, B, s):
                if isinstance(k0, int):
                    rows = w[k0 + s * 256:k0 + (s + 1) * 256]
                else:
                    rows = w[bass.ds(k0 + s * 256, 256)]
                src = rows[:, bass.ds(n0, NB)].rearrange("(k p) n -> p k n", p=P)
                if not (isinstance(B, int) and 8 * B + s < 4):
                    sp.wait_ge(slabs_split, B * 8 + (s + 1))
                sp.dma_start(raw[:, s % 4], src).then_inc(landed[s % 4], 16)

            def stream(w, n0, B, count):
                if count == 1:
                    for s in range(SLABS):
                        load(w, 0, n0, B, s)
                    return
                with sp.Fori(0, count) as i:
                    for s in range(SLABS):
                        load(w, 0, i * NB + n0, i + B, s)

            def stream_ffn(layer):
                with sp.Fori(0, 2) as half:
                    with sp.Fori(0, 8) as i:
                        for s in range(SLABS):
                            load(ffn_w1[layer], 0, half * (HID // 2) + i * NB, half * 16 + i + B_FFN[layer], s)
                    with sp.Fori(0, 4) as i:
                        for s in range(2 * SLABS):
                            B = half * 16 + i * 2 + (B_FFN[layer] + 8 + s // 8)
                            load(ffn_w2[layer], half * (HID // 2) + (s // 8) * D, i * NB, B, s % 8)

            sp.dma_start(cst[:, 0:P], consts[:, 0:P]).then_inc(sem("identity_loaded"), 16)
            for rows, k in ((mem_norm_g.rearrange("(k p) -> k p", p=P), GN_MEM),
                            (tok_norm_g.rearrange("l (k p) -> (l k) p", p=P), GN_TOK),
                            (ffn_norm_g.rearrange("l (k p) -> (l k) p", p=P), GN_FFN),
                            (dn_out_norm_g, GN_OUT), (gm_b_s[0], GN_BS)):
                n = rows.shape[0]
                sp.dma_start(small_rows[k:k + n, :], rows).then_inc(sem("rows_loaded"), 16)
            sp.dma_start(conv_rows, dn_conv_w[0].rearrange("t (c p) -> (t c) p", p=P)
                         .rearrange("(a r) p -> r a p", a=2)).then_inc(sem("rows_loaded"), 16)
            mem_rows = mem[0].rearrange("(m p) d -> p m d", p=P)
            for half in range(2):
                cols = slice(half * (D // 2), (half + 1) * (D // 2))
                sp.dma_start(mem_tok[:, :, cols], mem_rows[:, :, cols]).then_inc(sem(f"mem_loaded{half}"), 16)
            stream(mem_w_kv[0], 0, 0, 1)
            x_rows = x[0].rearrange("(m p) d -> p m d", p=P)
            sp.dma_start(h[:, :, 0:D // 2], x_rows[:, :, 0:D // 2]).then_inc(sem("x_loaded"), 16)
            for n, row in enumerate((dn_a_log, dn_dt_bias)):
                sp.dma_start(rows24[:, n], row[0:1].rearrange("l a b -> l (a b)").broadcast_to([P, 24])
                             ).then_inc(sem("gate_rows_loaded"), 16)
            sp.dma_start(wg, dn_w_in[0][:, 4 * MIX:4 * MIX + 48].rearrange("(k p) n -> p k n", p=P)
                         ).then_inc(sem("gate_weights_loaded"), 16)
            stream(mem_w_kv[0], NB, 1, 1)
            sp.dma_start(h[:, :, D // 2:], x_rows[:, :, D // 2:]).then_inc(sem("x_loaded"), 16)
            sp.dma_start(cst[:, P:], consts[:, P:]).then_inc(sem("consts_loaded"), 16)
            stream(mem_w_kv[1], 0, 2, 2)
            stream(dn_w_in[0], 4 * MIX + 48, B_QM, 1)
            with sp.Fori(1, 4) as g:
                for c, X in enumerate((3, 0, 1, 2)):
                    for s in range(SLABS):
                        load(dn_w_in[0], 0, g * NB + (X * MIX - NB), g * 4 + (B_DN - 4 + c), s)
            t = 8 * B_OUT[0]
            for part in (PART_A, PART_B):
                for n in range(4):
                    for p in part:
                        sp.wait_ge(slabs_split, t + 1)
                        sp.dma_start(raw[:, t % 4], tok_w_out[0][p * 256:(p + 1) * 256, n * NB:(n + 1) * NB]
                                     .rearrange("(k p) n -> p k n", p=P)).then_inc(landed[t % 4], 16)
                        t += 1
            stream_ffn(0)
            stream(gm_w_in[0], MIX, B_GM, 1)
            result(sp, B_GM - 1)
            sp.dma_start(ws[:], gm_w_s[0].rearrange("g i j -> i g j")).then_inc(sem("ws_loaded"), 16)
            sp.dma_start(vgain[:], gm_v_norm_g[0:1].broadcast_to([P, MIX])).then_inc(sem("vgain_loaded"), 16)
            stream(gm_w_in[0], MIX + NB, B_GM + 1, 2)
            stream(gm_w_in[0], 2 * MIX, B_GM + 3, 1)
            stream(gm_w_in[0], 0, B_GM + 4, 3)
            stream(tok_w_out[1], 0, B_OUT[1], 4)
            sp.wait_ge(sem("attention_split"), 2)
            sp.dma_start(final_gain, final_norm_g.rearrange("(a d) -> a d", a=1)
                         .broadcast_to([P, D])).then_inc(sem("final_gain_loaded"), 16)
            stream_ffn(1)
            for half in range(2):
                for m in range(2):
                    sp.wait_ge(sem(f"output_ready{m}"), half + 1)
                    cols = slice(half * (D // 2), (half + 1) * (D // 2))
                    sp.dma_start(out[0, m * P:(m + 1) * P, cols], xn_late[:, m, cols]).then_inc(sem("stored"), 16)
            sp.wait_ge(sem("stored"), 64)

        @block.tensor
        def _(pe):
            pe.sem_inc(slab_used, 2)

            def slab(B, s, R, parity, kt0, act_hi, act_lo, first, last):
                pe.wait_ge(slabs_split, B * 8 + (s + 5))
                for k in range(2):
                    kt = kt0 + k
                    start = first and k == 0
                    for m in range(2):
                        if start:
                            pe.wait_ge(result_drained[m], R + 1)
                        acc = banks[2 * parity + m][:]
                        tokens = slice(m * P, (m + 1) * P)
                        pe.matmul(acc, act_hi[:, kt, tokens], w_hi[:, s % 2, k], start=start, stop=False)
                        pe.matmul(acc, act_hi[:, kt, tokens], w_lo[:, s % 2, k], start=False, stop=False)
                        mm = pe.matmul(acc, act_lo[:, kt, tokens], w_hi[:, s % 2, k], start=False,
                                       stop=last and k == 1)
                mm.then_inc(slab_used, 1)

            def proj_block(B, R, parity, fill=None, between=None):
                for s in range(SLABS):
                    if fill is not None:
                        drained(pe, fill[s])
                    if s == 4 and between is not None:
                        between()
                    slab(B, s, R, parity, 2 * s, xT_hi, xT_lo, s == 0, s == SLABS - 1)

            def transposes(n, pieces, rounds=0):
                may_fill(pe, n, rounds)
                for col, src in pieces:
                    w = src.shape[0]
                    t = pe.transpose(aux[n % 4][0:src.shape[1], col:col + w], src, cst[0:w, C_ID:C_ID + w])
                t.then_inc(aux_filled[n % 4], 1)

            def pair_transposes(n, src, p, rounds=0):
                transposes(n, [((k * 2 + m) * P, src[:, m, (2 * p + k) * P:(2 * p + k + 1) * P])
                               for k in range(2) for m in range(2)], rounds)

            def block_steps(B, R, fill=None):
                for s in range(SLABS):
                    if fill is not None:
                        drained(pe, fill[s])
                    slab(B, s, R, R % 2, 2 * s, xT_hi, xT_lo, s == 0, s == SLABS - 1)
                    yield

            def refill(fill, src, plan, R=None):
                for pairs in plan:
                    for p in pairs:
                        if R is not None:
                            for m in range(2):
                                pe.wait_ge(result_drained[m], R + p // 2 + 3)
                        pair_transposes(fill[p], src, p)
                    yield

            def keys():
                for layer in range(2):
                    for m in range(2):
                        pe.wait_ge(result_drained[m], R_KV + 2 * layer + 3)
                    for hp in range(2):
                        pair_transposes(A_KT + 2 * layer + hp, ktok[:, layer], hp)
                yield

            pe.wait_ge(sem("identity_loaded"), 16)
            pe.wait_ge(sem("rows_loaded"), 96)
            transposes(A_SMALL, [(0, small_rows)])
            transposes(A_SMALL + 1, [(0, conv_rows[:, 0, :]), (90, conv_rows[:, 1, :])])
            pe.wait_ge(sem("mem_loaded0"), 16)
            for p in (0, 1):
                pair_transposes(mem_fill[p], mem_tok, p)

            def first_refill():
                for p in range(2, 8):
                    if p == 4:
                        pe.wait_ge(sem("mem_loaded1"), 16)
                    pair_transposes(mem_fill[p], mem_tok, p)
                    yield

            beside(first_refill(), block_steps(0, 0, mem_fill))
            for b in (1, 2):
                finish(block_steps(b, b, mem_fill))
            pe.wait_ge(sem("x_loaded"), 32)
            beside(chain(keys(), refill(x_fill, h, REFILL[1:])),
                   chain(block_steps(3, 3, mem_fill), block_steps(B_QM, R_QM, x_fill)))

            def gates():
                n = A_GATE
                may_fill(pe, n)
                pe.wait_ge(sem("gate_weights_split"), 1)
                for m in range(2):
                    for kt in range(KT):
                        for j, (a, b) in enumerate(((xT_hi, wg_hi), (xT_hi, wg_lo), (xT_lo, wg_hi))):
                            mm = pe.matmul(aux[n % 4][:, m * 48:(m + 1) * 48], a[:, kt, m * P:(m + 1) * P], b[:, kt],
                                           start=kt == 0 and j == 0, stop=kt == KT - 1 and j == 2)
                mm.then_inc(aux_filled[n % 4], 1)
                yield
                yield
                n = A_GATE + 1
                may_fill(pe, n)
                pe.wait_ge(sem("consts_loaded"), 16)
                pe.wait_ge(sem("gate_steps"), 9)
                b = aux[n % 4]
                for m in range(2):
                    row = 2 * (G_G + m)
                    for d, c in ((0, C_UP), (1, C_LO)):
                        pe.matmul(b[:, m * 24 + d * 12:m * 24 + d * 12 + 12], cst[:, c:c + P],
                                  gall[:, row + d, :], start=True, stop=True)
                    mm = pe.matmul(b[:, 48 + m * 24:72 + m * 24], ones, gall[:, row:row + 2, :], start=True, stop=True)
                mm.then_inc(aux_filled[n % 4], 1)
                yield

            def attention(layer, n0, R):
                q, qT, prob, probT = (buffers[layer][k] for k in ("q", "qT", "prob", "probT"))
                for m in range(2):
                    pe.wait_ge(result_drained[m], R + 3)
                for hp in range(2):
                    pair_transposes(n0 + hp, q, hp)
                yield
                for m in range(2):
                    for hp in range(2):
                        n = n0 + 2 + 2 * m + hp
                        drained(pe, n0 + hp)
                        may_fill(pe, n)
                        for k in range(2):
                            mm = pe.matmul(aux[n % 4][:, k * 256:(k + 1) * 256], qT[:, 2 * hp + k, m * P:(m + 1) * P],
                                           memKT[:, layer, 2 * hp + k, :], start=True, stop=True)
                        mm.then_inc(aux_filled[n % 4], 1)
                    yield
                yield
                pe.wait_ge(sem("prob_ready"), 4 * layer + 4)
                for i in range(4):
                    transposes(n0 + 6 + i, [((mt * 2 + m) * P, prob[:, m, i, mt * P:(mt + 1) * P])
                                            for mt in range(2) for m in range(2)])
                yield
                for hp in range(2):
                    n = n0 + 10 + hp
                    drained(pe, n0 + 6 + 2 * hp)
                    drained(pe, n0 + 7 + 2 * hp)
                    may_fill(pe, n)
                    for k in range(2):
                        for mt in range(2):
                            mm = pe.matmul(aux[n % 4][:, k * 256:(k + 1) * 256],
                                           memV[:, layer, mt, (2 * hp + k) * P:(2 * hp + k + 1) * P],
                                           probT[:, mt, 2 * hp + k, :], start=mt == 0, stop=mt == 1)
                    mm.then_inc(aux_filled[n % 4], 1)
                yield

            def deltanet(g, base, rnd):
                bank = lambda n: aux[(base + n) % 4]
                fill = lambda n: may_fill(pe, base + n, rnd)
                have = lambda n: drained(pe, base + n, rnd)
                done = lambda mm, n: mm.then_inc(aux_filled[(base + n) % 4], 1)

                def product(n, lhs, rhs, width, mats):
                    fill(n)
                    for i in range(mats):
                        mm = pe.matmul(bank(n)[:, i * width:(i + 1) * width], lhs(i), rhs(i), start=True, stop=True)
                    done(mm, n)

                def by_tokens(X, n0):
                    pe.wait_ge(sem("silu_done"), g * 3 + (X + 1))
                    for m in range(2):
                        transposes(base + n0 + m,
                                   [(k * P, conv[X][:, k, m * P:(m + 1) * P]) for k in range(4)], rnd)

                for X in range(3):
                    for m in range(2):
                        pe.wait_ge(result_drained[m], g * 4 + (R_DN + X + 4))
                    for hp in range(2):
                        pair_transposes(base + DA + 2 * X + hp, proj[:, X], hp, rnd)
                    yield
                by_tokens(0, DD)
                yield
                yield
                yield
                by_tokens(1, DD + 2)
                yield
                yield
                for X in range(2):
                    for m in range(2):
                        have(DD + 2 * X + m)
                    for hp in range(2):
                        pair_transposes(base + DE + 2 * X + hp, tok[:, X], hp, rnd)
                yield
                for f in range(4):
                    fill(DF + f)
                    pe.wait_ge(sem("decay_operands"), g * 8 + (2 * f + 1))
                    done(pe.matmul(bank(DF + f)[:], ones, g_up[:, f].rearrange("p h i -> p (h i)"),
                                   start=True, stop=True), DF + f)
                yield
                for n in range(4):
                    have(DE + n)
                for m in range(2):
                    for hp in range(2):
                        n = DG + 2 * m + hp
                        fill(n)
                        for k in range(2):
                            hh = 2 * hp + k
                            mm = pe.matmul(bank(n)[:, k * 256:(k + 1) * 256], kqT[:, 1, hh, m * P:(m + 1) * P],
                                           kqT[:, 0:2, hh, m * P:(m + 1) * P], start=True, stop=True)
                        done(mm, n)
                yield
                yield
                for d in range(2):
                    for m in range(2):
                        have(DG + 2 * m)
                        have(DG + 2 * m + 1)
                        transposes(base + DH + 2 * d + m, [(k * P, NT[:, d, m, k, :]) for k in range(4)], rnd)
                yield
                for l, s in enumerate(LEVELS):
                    last = l == len(LEVELS) - 1
                    halves = lambda t: t.rearrange("p (b two s) -> p b two s", two=2, s=s)
                    for d in range(2):
                        if l == 0:
                            if d == 0:
                                pe.wait_ge(sem("x0_vector"), g * 6 + 2)
                            pe.wait_ge(sem("x0_pool"), g * 8 + 4 * (d + 1))
                            for m in range(2):
                                have(DH + 2 * d + m)
                        else:
                            have(level_aux(l - 1, d, "XY"))
                        product(level_aux(l, d, "Y"), lambda i: NT[:, d, i // 4, i % 4, :],
                                lambda i: halves(XL[:, d, i // 4, i % 4, :])[:, :, 0, :], HALF, 8)
                    yield
                    for d in range(2):
                        if l == 0 and d == 1:
                            pe.wait_ge(sem("x0_vector"), g * 6 + 6)
                        if l > 0:
                            have(level_aux(l - 1, d, "YX"))
                        have(level_aux(l, d, "Y"))
                        if not (last and d == 0):
                            product(level_aux(l, d, "XY"), lambda i: XT[:, d, i // 4, i % 4, :],
                                    lambda i: halves(Y[:, d, i, :])[:, :, 0, :], HALF, 8)
                        if not (last and d == 1):
                            product(level_aux(l, d, "YX"), lambda i: Y[:, d, i, :],
                                    lambda i: halves(XT[:, d, i // 4, i % 4, :])[:, :, 1, :], HALF, 8)
                    if l == 1:
                        by_tokens(2, DV)
                    yield
                have(level_aux(len(LEVELS) - 1, 0, "YX"))
                have(level_aux(len(LEVELS) - 1, 1, "XY"))
                for m in range(2):
                    have(DV + m)
                for d in range(2):
                    product(DWV + d, lambda i: Wmat[d][:, d, i, :], lambda i: v_tok[d][:, i, :], P, 4)
                yield
                for d in range(2):
                    have(DWV + d)
                    pe.wait_ge(sem("kdec_done"), g * 2 + (d + 1))
                    product(DST + d, lambda i: kdec[d][:, i, :], lambda i: v_new[d][:, i, :], P, 4)
                for d in range(2):
                    product(DO1 + d, lambda i: attnT[:, d, d, i, :], lambda i: v_new[d][:, i, :], P, 4)
                yield
                for X, n in ((1, DKS), (0, DQS)):
                    for d in range(2):
                        if X == 1:
                            have(DST + d)
                        product(n + d, lambda i: kqT[:, X, i, (1 - d) * P:(2 - d) * P], lambda i: S[:, d, i, :], P, 4)
                yield
                for d in range(2):
                    have(DKS + d)
                    product(DWR + d, lambda i: Wmat[d][:, 1 - d, i, :], lambda i: v_tok[1 - d][:, i, :], P, 4)
                yield
                for d in range(2):
                    have(DWR + d)
                    product(DO2 + d, lambda i: attnT[:, d, 1 - d, i, :], lambda i: v_new[d][:, i, :], P, 4)
                yield
                yield
                yield

            def heads_stream(g):
                for c in range(4):
                    for s in range(SLABS):
                        slab(g * 4 + (B_DN + c), s, g * 4 + (R_DN + c), (R_DN + c) % 2, 2 * s, xT_hi, xT_lo,
                             s == 0, s == SLABS - 1)
                        yield

            beside(chain(gates(), attention(0, A_ATT0, R_QM)), heads_stream(0))
            with pe.Fori(0, 2) as g:
                beside(deltanet(g, A_DN, g * (DN_AUX // 4)), heads_stream(g + 1))

            def projection_part(part, t, R):
                for n in range(4):
                    for j, p in enumerate(part):
                        if p < 6:
                            drained(pe, mix_fill[0][p])
                        else:
                            pe.wait_ge(sem("attention_split"), 1)
                        slab(t // 8, t % 8, R + n, (R + n) % 2, 2 * p, xT_hi, xT_lo, j == 0, j == len(part) - 1)
                        t += 1
                        yield

            pe.wait_ge(sem("mixed"), 4)
            for p in range(4):
                pair_transposes(A_MIX0 + p, mix, p)
            beside(deltanet(2, A_DN2, 0), projection_part(PART_A, 8 * B_OUT[0], R_OUT[0]), ALONE)
            pe.wait_ge(sem("mixed"), 6)
            for p in range(4, 6):
                pair_transposes(mix_fill[0][p], mix, p)
            beside(refill(ffn_fill[0], h, REFILL_OUT, R_OUT[0] + 4),
                   chain(projection_part(PART_B, 8 * B_OUT[0] + 24, R_OUT[0] + 4),
                         block_steps(B_FFN[0], R_FFN[0], ffn_fill[0])))

            def hidden_transposes(layer, half, it, j):
                pe.wait_ge(sem("squared"), half * 8 + it * 2 + (16 * layer + j + 1))
                for q in range(2):
                    pair_transposes(A_FFN[layer] + 2 * j + q, relu[:, j], q, half * 4 + it)

            def ffn(layer, next_steps, next_fill=None):
                for half in range(2):
                    def up(it, j, between):
                        b = it * 2 + j
                        proj_block(half * 16 + b + B_FFN[layer], half * 12 + b + R_FFN[layer],
                                   (R_FFN[layer] + j) % 2, fill=ffn_fill[layer], between=between)
                    if half == 1:
                        up(0, 0, None)
                    with pe.Fori(0, 3) as it:
                        up(it, 1, lambda: hidden_transposes(layer, half, it, 0))
                        up(it + 1, 0, lambda: hidden_transposes(layer, half, it, 1))
                    up(3, 1, lambda: hidden_transposes(layer, half, 3, 0))

                    def down(i, c, between):
                        for s in range(16):
                            if s == 4 and between is not None:
                                between()
                            drained(pe, A_FFN[layer] + s, half * 4)
                            slab(half * 16 + i * 2 + (B_FFN[layer] + 8 + 2 * c + s // 8), s % 8,
                                 half * 12 + i + (R_FFN[layer] + 8 + c), (R_FFN[layer] + c) % 2, 2 * s,
                                 hid_hi, hid_lo, s == 0, s == 15)
                            yield
                    finish(down(0, 0, lambda: hidden_transposes(layer, half, 3, 1)))
                    finish(down(0, 1, None))
                    finish(down(2, 0, None))
                    if half == 0 or next_fill is None:
                        finish(down(2, 1, None))
                beside(refill(next_fill, h, 8 * ((),) + REFILL, R_FFN[layer] + 20) if next_fill else iter(()),
                       chain(down(2, 1, None), next_steps) if next_fill else iter(()))

            ffn(0, block_steps(B_GM, R_GM, tok1_fill), tok1_fill)

            def mixing():
                pe.wait_ge(sem("ws_loaded"), 16)
                for q in range(3):
                    transposes(A_WS + q, [(k * P, ws[:, 4 * q + k, :]) for k in range(4)])
                for _ in range(5):
                    yield
                for q in range(3):
                    drained(pe, A_WS + q)
                for m in range(2):
                    pe.wait_ge(sem("v_normalised"), m + 1)
                    for q in range(3):
                        n = A_SG + 3 * m + q
                        may_fill(pe, n)
                        for k in range(4):
                            i = 4 * q + k
                            mm = pe.matmul(aux[n % 4][:, k * P:(k + 1) * P], wsT[:, i, :], vg[:, m, i * P:(i + 1) * P],
                                           start=True, stop=True)
                        mm.then_inc(aux_filled[n % 4], 1)
                    yield
                yield

            def mix_refill(plan):
                for pairs in plan:
                    for p in pairs:
                        pe.wait_ge(sem("gated"), 2 * (p // 2) + 2)
                        pair_transposes(mix_fill[1][p], mix, p)
                    yield

            def out_block(n):
                for s in range(SLABS):
                    if s < 6:
                        drained(pe, mix_fill[1][s])
                    else:
                        pe.wait_ge(sem("attention_split"), 2)
                    slab(B_OUT[1] + n, s, R_OUT[1] + n, (R_OUT[1] + n) % 2, 2 * s, xT_hi, xT_lo, s == 0, s == 7)
                    yield

            for b in (1, 2):
                finish(block_steps(B_GM + b, R_GM + b, tok1_fill))
            beside(mixing(), block_steps(B_GM + 3, R_GM + 3, tok1_fill))
            beside(attention(1, A_ATT1, R_GM + 3), block_steps(B_GM + 4, R_GM + 4, tok1_fill))
            finish(block_steps(B_GM + 5, R_GM + 5, tok1_fill))
            beside(mix_refill(MIX_REFILL), chain(block_steps(B_GM + 6, R_GM + 6, tok1_fill), out_block(0)))
            for n in (1, 2):
                finish(out_block(n))
            beside(refill(ffn_fill[1], h, REFILL, R_OUT[1]),
                   chain(out_block(3), block_steps(B_FFN[1], R_FFN[1], ffn_fill[1])))
            ffn(1, None)

        @block.scalar
        def _(act):
            def split(B, s):
                act.wait_ge(landed[s % 4], B * 32 + 16 * (s // 4 + 1))
                act.wait_ge(slab_used, B * 8 + (s + 1))
                act.activation(w_hi[:, s % 2], raw[:, s % 4], ACT.Copy).then_inc(hi_ready, 1)

            def head(B):
                for s in range(2):
                    split(B, s)

            def tail(B, between=None, at=5):
                for s in range(2, SLABS):
                    split(B, s)
                    if s == at and between is not None:
                        between()

            def block_steps(B, drain=None):
                for t in range(8 * B, 8 * B + SLABS):
                    split((t + 2) // 8, (t + 2) % 8)
                    if t % 8 == SLABS - 1 and drain is not None:
                        drain()
                    yield

            def copy_result(B, parity, m, dst, func=ACT.Copy, norm=None):
                norm_known(act, norm)
                result(act, B)
                k = norm in (N_MEM, N_V)
                free_result(act.activation(dst, banks[2 * parity + m][:], func, scale=rstd[:, k, m:m + 1]), m)

            def sum_squares(src, junk, m, k=0):
                act.activation(junk, src, ACT.Square, accum_out=stat[:, k, m:m + 1]
                               ).then_inc(sem(f"squares_summed{m}"), 1)

            def operand_hi(n, p, gain):
                filled(act, n)
                if gain is None:
                    act.activation(xT_hi[:, 2 * p:2 * p + 2, :], pair(n), ACT.Copy).then_inc(sem("xT_hi_ready"), 2)
                else:
                    for k in range(2):
                        c = gain + (2 * p + k) * (gain != GN_OUT)
                        act.activation(xT_hi[:, 2 * p + k, :], aux[n % 4][:, k * SEQ:(k + 1) * SEQ], ACT.Copy,
                                       scale=gains[:, c:c + 1]).then_inc(sem("xT_hi_ready"), 1)

            def copy_aux(n, dst, src):
                filled(act, n)
                freed(act.activation(dst, src, ACT.Copy), n)

            pair = lambda n: aux[n % 4][:].rearrange("p (k t) -> p k t", k=2)

            def refill(fill, gain, plan, ends=None):
                for pairs in plan:
                    for p in pairs:
                        operand_hi(fill[p], p, gain)
                    yield
                if ends is not None:
                    residual(act, ends)
                    sum_squares(h[:, 0], xn_late[:, 0], 0)
                yield

            copy_aux(A_SMALL, gains[:], src=aux[A_SMALL % 4][:, 0:N_SMALL])
            copy_aux(A_SMALL + 1, conv_w[:], src=aux[(A_SMALL + 1) % 4][:, 0:180])
            drained(act, A_SMALL)
            for p in (0, 1):
                operand_hi(mem_fill[p], p, GN_MEM)
            head(0)

            def first_refill():
                for (p,) in REFILL_FIRST:
                    operand_hi(mem_fill[p], p, GN_MEM)
                    yield
                sum_squares(mem_tok[:, 0], junk_early[0], 0, 1)

            def memory_result(b):
                dst = ktok[:, b // 2, 0, :] if b % 2 == 0 else memV[:, b // 2, 0, :]
                return lambda: copy_result(b, b % 2, 0, dst, norm=N_MEM)

            def keys():
                for layer in range(2):
                    for hp in range(2):
                        n = A_KT + 2 * layer + hp
                        copy_aux(n, memKT[:, layer, 2 * hp:2 * hp + 2, :], src=pair(n))
                yield

            beside(first_refill(), block_steps(0, memory_result(0)))
            act.wait_ge(sem("gate_weights_loaded"), 16)
            act.activation(wg_hi[:], wg, ACT.Copy).then_inc(sem("gate_hi"), 1)
            finish(block_steps(1, memory_result(1)))
            finish(block_steps(2, memory_result(2)))
            act.wait_ge(sem("x_loaded"), 32)
            sum_squares(h[:, 0], junk_early[0], 0)
            beside(chain(keys(), refill(x_fill, GN_TOK, REFILL[1:])), chain(block_steps(3, memory_result(3)),
                   block_steps(B_QM, lambda: copy_result(B_QM, R_QM % 2, 0, early["q"][:, 0], norm=N_X))))

            def gates():
                act.wait_ge(sem("gate_rows_loaded"), 32)
                act.activation(rows24[:, 0], rows24[:, 0], ACT.Exp).then_inc(sem("gate_exps"), 1)
                act.wait_ge(sem("gate_steps"), 4)
                act.activation(gtmp[:, 2], gtmp[:, 1], ACT.Exp).then_inc(sem("gate_exps"), 1)
                act.activation(gtmp[:, 3], gt[:, :, 24:48], ACT.Exp, scale=-1.0).then_inc(sem("gate_exps"), 1)
                act.wait_ge(sem("gate_exps"), 2)
                act.activation(gtmp[:, 4], gtmp[:, 2], ACT.Ln, bias=1.0).then_inc(sem("gate_exps"), 1)
                yield
                yield
                act.wait_ge(sem("gate_steps"), 12)
                act.activation(gall[:, 2 * G_EGC:2 * G_EGC + 4, :].rearrange("p r h -> p (r h)"),
                               gx[:, 0:48], ACT.Exp).then_inc(sem("gate_exps"), 1)
                act.activation(gall[:, 2 * G_EKD:2 * G_EKD + 4, :].rearrange("p r h -> p (r h)"),
                               gtmp[:, 0].rearrange("p m c -> p (m c)"), ACT.Exp).then_inc(sem("gate_exps"), 1)
                yield

            def attention(layer, n0):
                qT, prob, probT = (buffers[layer][k] for k in ("qT", "prob", "probT"))
                for hp in range(2):
                    copy_aux(n0 + hp, qT[:, 2 * hp:2 * hp + 2, :], src=pair(n0 + hp))
                yield
                for j in range(4):
                    n = n0 + 2 + j
                    act.wait_ge(sem("score_max"), 8 * layer + 2 * (j + 1))
                    for k in range(2):
                        c = 2 * j + k
                        e = act.activation(prob[:, j // 2, 2 * (j % 2) + k, :], aux[n % 4][:, k * SEQ:(k + 1) * SEQ],
                                           ACT.Exp, bias=nmax[:, c:c + 1], scale=HD ** -0.5, accum_out=asum[:, c:c + 1])
                        if k == 0:
                            e.then_inc(sem("exp_half"), 1)
                        else:
                            freed(e, n)
                    if j % 2:
                        yield
                yield
                for i in range(4):
                    n = n0 + 6 + i
                    copy_aux(n, probT[:, :, i, :], src=pair(n))
                yield
                for hp in range(2):
                    copy_aux(n0 + 10 + hp, moT[layer][:, 2 * hp:2 * hp + 2, :], src=pair(n0 + 10 + hp))
                yield

            def deltanet(g, base, rnd):
                fil = lambda n: filled(act, base + n, rnd)
                bank = lambda n: aux[(base + n) % 4]
                halves = lambda n: bank(n)[:].rearrange("p (k t) -> p k t", k=2)
                free = lambda ins, n: freed(ins, base + n)

                def silu(X):
                    act.wait_ge(sem("conv_tap"), g * 48 + 16 * (X + 1))
                    act.activation(conv[X], conv[X], ACT.Silu).then_inc(sem("silu_done"), 1)

                def squares(X):
                    for m in range(2):
                        n = DD + 2 * X + m
                        fil(n)
                        act.activation(sq[:, 2 * X + m], bank(n)[:].rearrange("p (h i) -> p h i", h=4), ACT.Square
                                       ).then_inc(sem("head_squares"), 1)

                for X in range(3):
                    if X == 2:
                        fil(DA + 5)
                    for n in (2 * X, 2 * X + 1):
                        fil(DA + n)
                        c = 2 * (n % 2)
                        for k in range(2):
                            w = conv_w[:, bass.ds(g * 4 + (CONV // 2 * 36 + X * 12 + c + k), 1)]
                            act.activation(conv[X][:, c + k], halves(DA + n)[:, k], ACT.Copy, scale=w
                                           ).then_inc(sem("centre_tap"), 1)
                        free(act.activation(xpad[X][:, c:c + 2, 2:2 + SEQ], halves(DA + n), ACT.Copy), DA + n)
                    if X == 2:
                        silu(0)
                    yield
                squares(0)
                yield
                yield
                silu(1)
                yield
                squares(1)
                yield
                yield
                for X in range(2):
                    for hp in range(2):
                        n = DE + 2 * X + hp
                        fil(n)
                        free(act.activation(kqT[:, X, 2 * hp:2 * hp + 2, :], halves(n), ACT.Copy), n)
                yield
                for f in range(4):
                    drained(act, base + DF + f, rnd)
                    act.activation(NT[:, f // 2, f % 2], NT[:, f // 2, f % 2], ACT.Exp).then_inc(sem("decay_ready"), 1)
                yield
                yield
                yield
                for m in range(2):
                    n = DH + 2 + m
                    act.wait_ge(sem("x0_vector"), g * 6 + (3 + 2 * m))
                    act.wait_ge(sem("x0_pool"), g * 8 + (6 + 2 * m))
                    free(act.activation(NT[:, 1, m].rearrange("p h i -> p (h i)"), bank(n)[:], ACT.Copy), n)
                yield
                yield
                yield
                silu(2)
                yield
                for m in range(2):
                    fil(DV + m)
                    free(act.activation(tok[:, 2, m], bank(DV + m)[:], ACT.Copy), DV + m)
                yield
                for _ in range(2 * len(LEVELS) - 3):
                    yield
                for d in range(2):
                    fil(DST + d)
                    free(act.activation(S[:, d], by_head(bank(DST + d)[:]), ACT.Copy), DST + d)
                yield
                yield
                yield
                yield
                for d in range(2):
                    drained(act, base + DO2 + d, rnd)
                for m in range(2):
                    act.activation(sq[:, m], by_head(o[:, m]), ACT.Square).then_inc(sem("out_squares"), 1)
                yield
                yield

            def heads_stream(g):
                for c in range(4):
                    for s in range(SLABS):
                        B = g * 4 + (B_DN + c + (s + 2) // 8)
                        split(B, (s + 2) % 8)
                        if s == SLABS - 1:
                            B = g * 4 + (B_DN + c)
                            parity = (R_DN + c) % 2
                            if c == 0:
                                for m in range(2):
                                    copy_result(B, parity, m, mix[:, m, bass.ds(g * NB, NB)], ACT.Silu, N_X)
                            else:
                                copy_result(B, parity, 0, proj[:, c - 1, 0, :], norm=N_X)
                        yield

            beside(chain(gates(), attention(0, A_ATT0)), heads_stream(0))
            with act.Fori(0, 2) as g:
                beside(deltanet(g, A_DN, g * (DN_AUX // 4)), heads_stream(g + 1))

            def out_part(t, count):
                for t in range(t, t + count):
                    split((t + 2) // 8, (t + 2) % 8)
                    yield

            for p in range(4):
                operand_hi(A_MIX0 + p, p, GN_OUT)
            act.activation(xT_hi[:, 12:16, :], moT[0], ACT.Copy).then_inc(sem("xT_hi_ready"), 4)
            beside(deltanet(2, A_DN2, 0), out_part(8 * B_OUT[0], 24), ALONE)
            for p in range(4, 6):
                operand_hi(mix_fill[0][p], p, GN_OUT)

            def first_hidden(layer):
                return lambda: copy_result(B_FFN[layer], R_FFN[layer] % 2, 0, relu[:, 0, 0, :], ACT.Relu,
                                           (N_FFN0, N_FFN1)[layer])

            beside(refill(ffn_fill[0], GN_FFN, REFILL_OUT, R_FFN[0]),
                   chain(out_part(8 * B_OUT[0] + 24, 8), block_steps(B_FFN[0], first_hidden(0))))

            def hidden(layer, half, it, j):
                for q in range(2):
                    n = A_FFN[layer] + 2 * j + q
                    filled(act, n, half * 4 + it)
                    act.activation(hid_hi[:, bass.ds(it * 8 + (4 * j + 2 * q), 2), :], pair(n), ACT.Copy
                                   ).then_inc(sem("hidden_hi"), 1)

            def ffn(layer, stages=None, next_steps=None):
                for half in range(2):
                    def up(it, j, between):
                        tail(half * 16 + it * 2 + (B_FFN[layer] + j), between)
                        head(half * 16 + it * 2 + (B_FFN[layer] + j + 1))
                        copy_result(half * 16 + it * 2 + (B_FFN[layer] + j), (R_FFN[layer] + j) % 2, 0,
                                    relu[:, j, 0, :], ACT.Relu, (N_FFN0, N_FFN1)[layer])
                    if half == 1:
                        up(0, 0, None)
                    with act.Fori(0, 3) as it:
                        up(it, 1, lambda: hidden(layer, half, it, 0))
                        up(it + 1, 0, lambda: hidden(layer, half, it, 1))
                    up(3, 1, lambda: hidden(layer, half, 3, 0))
                    B = half * 16 + B_FFN[layer] + 8
                    tail(B, lambda: hidden(layer, half, 3, 1))
                    if half == 0:
                        with act.Fori(0, 7) as i:
                            head(i + (B + 1))
                            tail(i + (B + 1))
                        head(B + 8)
                for i in range(3):
                    head(B + 1)
                    tail(B + 1)
                    head(B + 2)
                    if i < 2:
                        tail(B + 2, lambda: final_stage(layer, i))
                    B += 2
                if stages is None:
                    tail(B, lambda: final_stage(layer, 2))
                    head(B + 1)
                    tail(B + 1)
                    block_squares(3)
                else:
                    beside(stages, chain(block_steps(B), block_steps(B + 1), next_steps))

            def final_stage(layer, i):
                if layer == 1:
                    block_squares(i)

            def block_squares(i):
                residual(act, R_FFN[1] + 21 + i)
                for m in range(2):
                    if i > 1:
                        act.wait_ge(sem("block_squares"), 2 * i - 3 + m)
                    act.activation(relu[:, i % 2, m], h[:, m, i * NB:(i + 1) * NB], ACT.Square,
                                   accum_out=parts[:, m, i:i + 1]).then_inc(sem("block_squares"), 1)

            def values(b):
                def drain():
                    dst, i = (vg, b) if b < 3 else (ug, b - 4)
                    for m in range(2):
                        copy_result(B_GM + b, (R_GM + b) % 2, m, dst[:, m, i * NB:(i + 1) * NB],
                                    ACT.Gelu_apprx_tanh, N_TOK1)
                return drain

            ffn(0, refill(tok1_fill, GN_TOK + 16, 8 * ((),) + REFILL, R_GM), block_steps(B_GM, values(0)))

            for b in (1, 2):
                finish(block_steps(B_GM + b, values(b)))

            def mixing():
                for m in range(2):
                    act.wait_ge(result_drained[m], R_GM + 5)
                    sum_squares(vg[:, m], xn_late[:, m, 0:MIX], m, 1)
                for q in range(3):
                    copy_aux(A_WS + q, wsT[:, 4 * q:4 * q + 4, :],
                             src=aux[(A_WS + q) % 4][:].rearrange("p (k t) -> p k t", k=4))
                yield

            def out_split():
                for pairs in MIX_REFILL[0:8]:
                    for p in pairs:
                        operand_hi(A_MIX1 + p, p, None)
                    yield
                slab_done(act, 8 * (B_GM + 6) + 7)
                act.activation(xT_hi[:, 12:16, :], moT[1], ACT.Copy).then_inc(sem("xT_hi_ready"), 4)
                for pairs in MIX_REFILL[8:]:
                    for p in pairs:
                        operand_hi(A_MIX1 + p, p, None)
                    yield

            beside(mixing(), block_steps(B_GM + 3, lambda: copy_result(B_GM + 3, (R_GM + 3) % 2, 0, q_mem[:, 0, :],
                                                                      norm=N_TOK1)))
            beside(attention(1, A_ATT1), block_steps(B_GM + 4, values(4)))
            finish(block_steps(B_GM + 5, values(5)))
            beside(out_split(), chain(block_steps(B_GM + 6, values(6)), block_steps(B_OUT[1])))
            for n in (1, 2):
                finish(block_steps(B_OUT[1] + n))
            beside(refill(ffn_fill[1], GN_FFN + 16, REFILL, R_FFN[1]),
                   chain(block_steps(B_OUT[1] + 3), block_steps(B_FFN[1], first_hidden(1))))
            ffn(1)
            act.wait_ge(sem("gained"), 8)
            norm_known(act, N_FINAL)
            for half in range(2):
                t = xn_late[:, 0, half * (D // 2):(half + 1) * (D // 2)]
                act.activation(t, t, ACT.Copy, scale=rstd[:, 0, 0:1]).then_inc(sem("output_ready0"), 1)

        @block.vector
        def _(dve):
            dve.sem_inc(slabs_split, 4)
            for m in range(2):
                dve.sem_inc(result_drained[m], 2)
            for b in range(4):
                dve.sem_inc(aux_drained[b], 1)

            def split(B, s):
                dve.wait_ge(hi_ready, B * 8 + (s + 1))
                dve.wait_ge(slab_used, B * 8 + (s + 1))
                dve.tensor_tensor(w_lo[:, s % 2], raw[:, s % 4], w_hi[:, s % 2].bitcast(F32), ALU.subtract
                                  ).then_inc(slabs_split, 1)

            def head(B):
                for s in range(2):
                    split(B, s)

            def tail(B, between=None, at=5):
                for s in range(2, SLABS):
                    split(B, s)
                    if s == at and between is not None:
                        between()

            def block_steps(B, drain=None):
                for t in range(8 * B, 8 * B + SLABS):
                    split((t + 2) // 8, (t + 2) % 8)
                    if t % 8 == SLABS - 1 and drain is not None:
                        drain()
                    yield

            def copy_result(B, parity, m, dst, norm):
                norm_known(dve, norm)
                result(dve, B)
                k = norm in (N_MEM, N_V)
                free_result(dve.tensor_scalar(dst, banks[2 * parity + m][:], rstd[:, k, m:m + 1], None, ALU.mult), m)

            def sum_squares(src, junk, m, k=0):
                dve.tensor_tensor_reduce(out=junk, in0=src, in1=src, scale=1.0, scalar=0.0, op0=ALU.mult,
                                         op1=ALU.add, accum_out=stat[:, k, m:m + 1]).then_inc(sem(f"squares_summed{m}"), 1)

            def operand_lo(n, p, gain, hi_count):
                dve.wait_ge(sem("xT_hi_ready"), hi_count)
                if gain is None:
                    freed(dve.tensor_tensor(xT_lo[:, 2 * p:2 * p + 2, :], aux[n % 4][:].rearrange("p (k t) -> p k t", k=2),
                                            xT_hi[:, 2 * p:2 * p + 2, :].bitcast(F32), ALU.subtract), n)
                else:
                    for k in range(2):
                        c = gain + (2 * p + k) * (gain != GN_OUT)
                        e = dve.scalar_tensor_tensor(out=xT_lo[:, 2 * p + k, :], in0=aux[n % 4][:, k * SEQ:(k + 1) * SEQ],
                                                     scalar=gains[:, c:c + 1], in1=xT_hi[:, 2 * p + k, :].bitcast(F32),
                                                     op0=ALU.mult, op1=ALU.subtract)
                        if k == 0:
                            e.then_inc(sem("xT_lo_half"), 1)
                    freed(e, n)

            def rows(v, n):
                return v.unsqueeze(2).broadcast_to([P, 4, n])

            def over(v, n):
                return v.unsqueeze(1).broadcast_to([P, n, v.shape[1]])

            def refill(fill, gain, plan, count, ends=None):
                for pairs in plan:
                    for p in pairs:
                        operand_lo(fill[p], p, gain, count + 2 * (p + 1))
                    yield
                if ends is not None:
                    residual(dve, ends)
                    sum_squares(h[:, 1], xn_late[:, 1], 1)
                yield

            drained(dve, A_SMALL)
            for p in (0, 1):
                operand_lo(mem_fill[p], p, GN_MEM, 2 * (p + 1))
            head(0)

            def first_refill():
                for (p,) in REFILL_FIRST:
                    operand_lo(mem_fill[p], p, GN_MEM, 2 * (p + 1))
                    yield
                for half in range(2):
                    dve.wait_ge(sem(f"mem_loaded{half}"), 16)
                sum_squares(mem_tok[:, 1], junk_early[1], 1, 1)

            def memory_result(b):
                dst = ktok[:, b // 2, 1, :] if b % 2 == 0 else memV[:, b // 2, 1, :]
                return lambda: copy_result(b, b % 2, 1, dst, N_MEM)

            beside(first_refill(), block_steps(0, memory_result(0)))
            dve.wait_ge(sem("gate_hi"), 1)
            dve.tensor_tensor(wg_lo[:], wg, wg_hi[:].bitcast(F32), ALU.subtract).then_inc(sem("gate_weights_split"), 1)
            finish(block_steps(1, memory_result(1)))
            finish(block_steps(2, memory_result(2)))
            dve.wait_ge(sem("x_loaded"), 32)
            sum_squares(h[:, 1], junk_early[1], 1)
            beside(refill(x_fill, GN_TOK, REFILL, 16), chain(block_steps(3, memory_result(3)),
                   block_steps(B_QM, lambda: copy_result(B_QM, R_QM % 2, 1, early["q"][:, 1], N_X))))

            def gates():
                steps = sem("gate_steps")
                n = A_GATE
                filled(dve, n)
                norm_known(dve, N_X)
                dve.tensor_scalar(gt[:, 0], aux[n % 4][:, 0:48], rstd[:, 0, 0:1], None, ALU.mult
                                  ).then_inc(sem("gate_scaled"), 1)
                freed(dve.tensor_scalar(gt[:, 1], aux[n % 4][:, 48:96], rstd[:, 0, 1:2], None, ALU.mult), n)
                drained(dve, n)
                dve.wait_ge(sem("gate_rows_loaded"), 32)
                dve.tensor_tensor(gtmp[:, 0], gt[:, :, 0:24], over(rows24[:, 1], 2), ALU.add).then_inc(steps, 1)
                dve.wait_ge(steps, 1)
                dve.tensor_scalar(gtmp[:, 1], gtmp[:, 0], -1.0, None, ALU.mult).then_inc(steps, 1)
                dve.wait_ge(steps, 2)
                dve.tensor_tensor(gtmp[:, 1], gtmp[:, 1], gtmp[:, 0], ALU.min).then_inc(steps, 1)
                dve.wait_ge(steps, 3)
                dve.tensor_scalar(gtmp[:, 0], gtmp[:, 0], 0.0, None, ALU.max).then_inc(steps, 1)
                yield
                dve.wait_ge(sem("gate_exps"), 4)
                dve.tensor_tensor(gtmp[:, 0], gtmp[:, 0], gtmp[:, 4], ALU.add).then_inc(steps, 1)
                dve.wait_ge(steps, 5)
                dve.tensor_tensor(gtmp[:, 0], gtmp[:, 0], over(rows24[:, 0], 2), ALU.mult).then_inc(steps, 1)
                dve.wait_ge(steps, 6)
                gm = lambda a: gall[:, 2 * a:2 * a + 4, :].rearrange("p (m d) h -> p m (d h)", m=2)
                dve.tensor_scalar(gm(G_G), gtmp[:, 0], -1.0, None, ALU.mult).then_inc(steps, 1)
                dve.tensor_scalar(gtmp[:, 3], gtmp[:, 3], 1.0, None, ALU.add).then_inc(steps, 1)
                dve.wait_ge(steps, 8)
                dve.reciprocal(gm(G_BETA), gtmp[:, 3]).then_inc(steps, 1)
                yield
                n = A_GATE + 1
                filled(dve, n)
                freed(dve.tensor_copy(gx[:], aux[n % 4][:, 0:96]), n)
                drained(dve, n)
                dve.tensor_copy(gm(G_GC), gx[:, 0:48].rearrange("p (m c) -> p m c", m=2)).then_inc(steps, 1)
                dve.tensor_tensor(gtmp[:, 0].rearrange("p m c -> p (m c)"), gx[:, 48:96], gx[:, 0:48], ALU.subtract
                                  ).then_inc(steps, 1)
                dve.tensor_copy(gtmp[:, 1].rearrange("p m c -> p (m c)"), gx[:, 0:48]).then_inc(steps, 1)
                dve.wait_ge(sem("gate_exps"), 5)
                dve.tensor_scalar(gm(G_NEG), gm(G_EGC), -1.0, None, ALU.mult).then_inc(steps, 1)
                yield

            def attention(layer, n0):
                prob = buffers[layer]["prob"]
                yield
                for j in range(4):
                    n = n0 + 2 + j
                    filled(dve, n)
                    dve.tensor_reduce(amax[:, 2 * j:2 * j + 2], aux[n % 4][:].rearrange("p (k t) -> p k t", k=2),
                                      AX.X, ALU.max).then_inc(sem("score_max"), 1)
                    dve.wait_ge(sem("score_max"), 8 * layer + 2 * j + 1)
                    dve.tensor_scalar(nmax[:, 2 * j:2 * j + 2], amax[:, 2 * j:2 * j + 2], -(HD ** -0.5), None, ALU.mult
                                      ).then_inc(sem("score_max"), 1)
                    if j == 1:
                        yield
                for j in range(4):
                    drained(dve, n0 + 2 + j)
                dve.reciprocal(arec[:], asum[:]).then_inc(sem("sum_inverse"), 1)
                dve.wait_ge(sem("sum_inverse"), layer + 1)
                for j in range(4):
                    t = prob[:, j // 2, 2 * (j % 2):2 * (j % 2) + 2, :]
                    dve.tensor_tensor(t, t, arec[:, 2 * j:2 * j + 2].unsqueeze(2).broadcast_to([P, 2, SEQ]), ALU.mult
                                      ).then_inc(sem("prob_ready"), 1)
                yield
                yield
                yield
                yield

            def deltanet(g, base, rnd):
                fil = lambda n: filled(dve, base + n, rnd)
                have = lambda n: drained(dve, base + n, rnd)
                bank = lambda n: aux[(base + n) % 4]
                heads = lambda n: by_head(bank(n)[:])
                free = lambda ins, n: freed(ins, base + n)
                beta = lambda m, d, hh: gs[:, 2 * (G_BETA + m) + d, hh:hh + 1]
                taps = sem("conv_tap")

                def convolve(X, *steps):
                    for i in steps:
                        tap = (0, 1, 3, 4)[i]
                        if i == 0:
                            have(DA + 2 * X)
                            have(DA + 2 * X + 1)
                        for c in range(4):
                            w = conv_w[:, bass.ds(g * 4 + (tap * 36 + X * 12 + c), 1)]
                            if i > 0:
                                dve.wait_ge(taps, g * 48 + (16 * X + 4 * (i - 1) + c + 1))
                            dve.scalar_tensor_tensor(out=conv[X][:, c], in0=xpad[X][:, c, tap:tap + SEQ], scalar=w,
                                                     in1=conv[X][:, c], op0=ALU.mult, op1=ALU.add).then_inc(taps, 1)

                def square_sums(X):
                    for m in range(2):
                        dve.wait_ge(sem("head_squares"), g * 4 + (2 * X + m + 1))
                        dve.tensor_reduce(ss[:, X, m], sq[:, 2 * X + m], AX.X, ALU.add).then_inc(sem("head_sums"), 1)
                    f = float(HD) if X == 0 else 1.0
                    dve.wait_ge(sem("head_sums"), g * 6 + (3 * X + 2))
                    dve.tensor_scalar(ss[:, X], ss[:, X], f, f * EPS, ALU.mult, ALU.add).then_inc(sem("head_sums"), 1)

                def normalise(X):
                    for m in range(2):
                        n = DD + 2 * X + m
                        dve.wait_ge(sem("head_rstd"), g * 2 + (X + 1))
                        free(dve.tensor_tensor(by_head(tok[:, X, m]), heads(n), rows(rs[:, X, m], P), ALU.mult), n)

                dve.wait_ge(sem("padded"), g * 2 + 2)
                convolve(0, 0, 1)
                yield
                convolve(0, 2, 3)
                yield
                convolve(1, 0, 1)
                yield
                convolve(1, 2)
                square_sums(0)
                yield
                normalise(0)
                convolve(1, 3)
                yield
                dve.wait_ge(sem("v_padded"), g * 2 + 2)
                convolve(2, 0)
                yield
                square_sums(1)
                yield
                normalise(1)
                yield
                convolve(2, 1)
                yield
                for f in range(4):
                    fil(DF + f)
                    dve.wait_ge(sem("decay_operands"), g * 8 + (2 * f + 2))
                    free(dve.tensor_tensor(NT[:, f // 2, f % 2], heads(DF + f), g_big[:, f], ALU.subtract), DF + f)
                yield
                dve.wait_ge(sem("decay_ready"), g * 4 + 4)
                dve.wait_ge(sem("head_sums"), g * 6 + 6)
                for m in range(2):
                    for hp in range(2):
                        n = DG + 2 * m + hp
                        fil(n)
                        view = bank(n)[:].rearrange("p (k two i) -> p k two i", k=2, two=2)
                        for d in range(2):
                            dve.tensor_tensor(attnT[:, d, m, 2 * hp:2 * hp + 2, :], view[:, :, 0, :],
                                              NT[:, d, m, 2 * hp:2 * hp + 2, :], ALU.mult).then_inc(sem("attn_ready"), 1)
                        dve.wait_ge(sem("attn_ready"), g * 8 + (2 * (2 * m + hp) + 2))
                        for d in range(2):
                            for k in range(2):
                                hh = 2 * hp + k
                                e = dve.scalar_tensor_tensor(out=NT[:, d, m, hh, :], in0=view[:, k, 1, :],
                                                             scalar=beta(m, d, hh), in1=NT[:, d, m, hh, :],
                                                             op0=ALU.mult, op1=ALU.mult)
                                if (d, k) != (1, 1):
                                    e.then_inc(sem("n_part"), 1)
                        free(e, n)
                    yield
                x0 = sem("x0_vector")
                for d in range(2):
                    for m in range(2):
                        n = DH + 2 * d + m
                        fil(n)
                        if d == 0:
                            free(dve.tensor_tensor(XL[:, 0, m], heads(n), over(cst[:, C_M1L:C_M1L + P], 4), ALU.mult), n)
                            have(n)
                            dve.tensor_tensor(XL[:, 0, m], XL[:, 0, m], over(ident, 4), ALU.add).then_inc(x0, 1)
                        else:
                            dve.tensor_tensor(XT[:, 1, m], heads(n), over(cst[:, C_M1T:C_M1T + P], 4), ALU.mult
                                              ).then_inc(x0, 1)
                            dve.wait_ge(x0, g * 6 + (3 + 2 * m))
                            dve.tensor_tensor(XT[:, 1, m], XT[:, 1, m], over(ident, 4), ALU.add).then_inc(x0, 1)
                yield
                for l, s in enumerate(LEVELS):
                    last = l == len(LEVELS) - 1
                    halves = lambda t: t.rearrange("p x (b two s) -> p x b two s", two=2, s=s)
                    mats = lambda t: t.rearrange("p m h i -> p (m h) i")
                    got = lambda n: bank(n)[:].rearrange("p (x b s) -> p x b s", x=8, s=s)
                    mask = cst[:, C_LEV + l * HALF:C_LEV + (l + 1) * HALF].rearrange("p (b s) -> p b s", s=s)
                    mask = mask.unsqueeze(1).broadcast_to([P, 8, HALF // s, s])
                    for d in range(2):
                        n = level_aux(l, d, "Y")
                        fil(n)
                        dve.wait_ge(sem("y_zeroed"), g * (2 * len(LEVELS)) + (2 * l + d + 1))
                        free(dve.tensor_tensor(halves(Y[:, d])[:, :, :, 0, :], got(n), mask, ALU.mult), n)
                    if l == 0:
                        convolve(2, 2)
                    yield
                    for d in range(2):
                        if not (last and d == 0):
                            n = level_aux(l, d, "XY")
                            fil(n)
                            t = halves(mats(XL[:, d]))[:, :, :, 0, :]
                            free(dve.tensor_tensor(t, t, got(n), ALU.subtract), n)
                        if not (last and d == 1):
                            n = level_aux(l, d, "YX")
                            fil(n)
                            t = halves(mats(XT[:, d]))[:, :, :, 1, :]
                            free(dve.tensor_tensor(t, t, got(n), ALU.subtract), n)
                    if l == 0:
                        convolve(2, 3)
                    yield

                def new_values(d, m, n):
                    fil(n)
                    free(dve.tensor_tensor(v_new[d], heads(n), rows(gs[:, 2 * (G_BETA + m) + d, :], P), ALU.mult), n)

                for d in range(2):
                    new_values(d, d, DWV + d)
                yield
                for d in range(2):
                    fil(DO1 + d)
                    free(dve.tensor_copy(o[:, d], bank(DO1 + d)[:]), DO1 + d)
                yield
                for n, kind in ((DKS, G_NEG), (DQS, G_EGC)):
                    for d in range(2):
                        m = 1 - d
                        fil(n + d)
                        if n == DQS:
                            have(DO1 + m)
                        dst = v_tok[m] if n == DKS else by_head(o[:, m])
                        for i in range(4):
                            e = dve.scalar_tensor_tensor(out=dst[:, i], in0=heads(n + d)[:, i],
                                                         scalar=gs[:, 2 * (kind + m) + d, i:i + 1],
                                                         in1=dst[:, i], op0=ALU.mult, op1=ALU.add)
                            if i < 3:
                                e.then_inc(sem("head_part"), 1)
                        free(e, n + d)
                yield
                for d in range(2):
                    new_values(d, 1 - d, DWR + d)
                yield
                for d in range(2):
                    m = 1 - d
                    fil(DO2 + d)
                    have(DQS + d)
                    free(dve.tensor_tensor(o[:, m], o[:, m], bank(DO2 + d)[:], ALU.add), DO2 + d)
                yield
                for m in range(2):
                    dve.wait_ge(sem("out_squares"), g * 2 + (m + 1))
                    dve.tensor_reduce(ss[:, 2, m], sq[:, m], AX.X, ALU.add).then_inc(sem("out_sums"), 1)
                dve.wait_ge(sem("out_sums"), g * 3 + 2)
                dve.tensor_scalar(ss[:, 2], ss[:, 2], 1.0 / HD, EPS, ALU.mult, ALU.add).then_inc(sem("out_sums"), 1)
                yield
                dve.wait_ge(sem("out_rstd"), g + 1)
                for m in range(2):
                    om = by_head(o[:, m])
                    dve.tensor_tensor(om, om, rows(rs[:, 2, m], P), ALU.mult).then_inc(sem("out_normed"), 1)
                for m in range(2):
                    dve.wait_ge(result_drained[m], g * 4 + (R_DN + 3))
                for m in range(2):
                    dve.wait_ge(sem("out_normed"), g * 2 + (m + 1))
                    t = mix[:, m, bass.ds(g * NB, NB)]
                    dve.tensor_tensor(t, o[:, m], t, ALU.mult).then_inc(sem("mixed"), 1)
                dve.wait_ge(sem("mixed"), g * 2 + 2)
                yield

            def heads_stream(g):
                for c in range(4):
                    for s in range(SLABS):
                        split(g * 4 + (B_DN + c + (s + 2) // 8), (s + 2) % 8)
                        if s == SLABS - 1 and c > 0:
                            copy_result(g * 4 + (B_DN + c), (R_DN + c) % 2, 1, proj[:, c - 1, 1, :], N_X)
                        yield

            beside(chain(gates(), attention(0, A_ATT0)), heads_stream(0))
            with dve.Fori(0, 2) as g:
                beside(deltanet(g, A_DN, g * (DN_AUX // 4)), heads_stream(g + 1))

            def out_part(part, t, R):
                for n in range(4):
                    for j in range(len(part)):
                        split((t + 2) // 8, (t + 2) % 8)
                        if j == len(part) - 1:
                            slab_done(dve, t)
                            for m in range(2):
                                v = h[:, m, n * NB:(n + 1) * NB]
                                free_result(dve.tensor_tensor(v, v, banks[2 * ((R + n) % 2) + m][:], ALU.add), m)
                        t += 1
                        yield

            for p in range(4):
                operand_lo(A_MIX0 + p, p, GN_OUT, 32 + 2 * (p + 1))
            dve.wait_ge(sem("xT_hi_ready"), 44)
            dve.tensor_tensor(xT_lo[:, 12:16, :], moT[0], xT_hi[:, 12:16, :].bitcast(F32), ALU.subtract
                              ).then_inc(sem("attention_split"), 1)
            beside(deltanet(2, A_DN2, 0), out_part(PART_A, 8 * B_OUT[0], R_OUT[0]), ALONE)
            for p in range(4, 6):
                operand_lo(mix_fill[0][p], p, GN_OUT, 44 + 2 * (p - 3))
            residual(dve, R_OUT[0] + 4)

            def relu_result(layer, B, R, j):
                norm_known(dve, (N_FFN0, N_FFN1)[layer])
                result(dve, B)
                free_result(dve.tensor_scalar(relu[:, j, 1, :], banks[2 * (R % 2) + 1][:], rstd[:, 0, 1:2], 0.0,
                                              ALU.mult, ALU.max), 1)

            beside(refill(ffn_fill[0], GN_FFN, REFILL_OUT, 48, R_FFN[0]),
                   chain(out_part(PART_B, 8 * B_OUT[0] + 24, R_OUT[0] + 4),
                         block_steps(B_FFN[0], lambda: relu_result(0, B_FFN[0], R_FFN[0], 0))))

            def add_result(B, parity, i):
                result(dve, B)
                for m in range(2):
                    t = h[:, m, bass.ds(i * NB, NB)]
                    free_result(dve.tensor_tensor(t, t, banks[2 * parity + m][:], ALU.add), m)

            def hidden(layer, half, it, j):
                for q in range(2):
                    n = A_FFN[layer] + 2 * j + q
                    dve.wait_ge(sem("hidden_hi"), half * 16 + it * 4 + (32 * layer + 2 * j + q + 1))
                    t = bass.ds(it * 8 + (4 * j + 2 * q), 2)
                    freed(dve.tensor_tensor(hid_lo[:, t, :], aux[n % 4][:].rearrange("p (k t) -> p k t", k=2),
                                            hid_hi[:, t, :].bitcast(F32), ALU.subtract), n)

            def final_stage(layer, half, i):
                if layer == 1 and half == 1:
                    final_gains(i)

            def final_gains(i):
                residual(dve, R_FFN[1] + 21 + i)
                dve.wait_ge(sem("final_gain_loaded"), 16)
                cols = slice(i * NB, (i + 1) * NB)
                for m in range(2):
                    dve.tensor_tensor(xn_late[:, m, cols], h[:, m, cols], final_gain[:, cols], ALU.mult
                                      ).then_inc(sem("gained"), 1)

            def ffn(layer, stages=None, next_steps=None):
                for half in range(2):
                    def up(it, j, between):
                        B = half * 16 + it * 2 + (B_FFN[layer] + j)
                        tail(B, between)
                        head(half * 16 + it * 2 + (B_FFN[layer] + j + 1))
                        relu_result(layer, B, R_FFN[layer] + j, j)
                    if half == 1:
                        up(0, 0, None)
                    with dve.Fori(0, 3) as it:
                        up(it, 1, lambda: hidden(layer, half, it, 0))
                        up(it + 1, 0, lambda: hidden(layer, half, it, 1))
                    up(3, 1, lambda: hidden(layer, half, 3, 0))

                    def down(i, between=None):
                        B = half * 16 + B_FFN[layer] + 8 + 2 * i
                        tail(B, between)
                        head(B + 1)
                        tail(B + 1)
                        head(B + 2)
                        add_result(B + 1, (R_FFN[layer] + i) % 2, i)
                    down(0, lambda: hidden(layer, half, 3, 1))
                    for i in (1, 2, 3)[0:3 - half]:
                        down(i, lambda: final_stage(layer, half, i - 1))
                B = B_FFN[layer] + 30
                last_sum = lambda: add_result(B + 1, (R_FFN[layer] + 3) % 2, 3)
                if stages is None:
                    tail(B, lambda: final_stage(layer, 1, 2))
                    head(B + 1)
                    tail(B + 1)
                    last_sum()
                    final_gains(3)
                else:
                    beside(stages, chain(block_steps(B), block_steps(B + 1, last_sum), next_steps))

            ffn(0, refill(tok1_fill, GN_TOK + 16, 8 * ((),) + REFILL, 64, R_GM), block_steps(B_GM))

            for b in (1, 2):
                finish(block_steps(B_GM + b))

            def mixing():
                for _ in range(3):
                    yield
                dve.wait_ge(sem("vgain_loaded"), 16)
                norm_known(dve, N_V)
                for m in range(2):
                    dve.scalar_tensor_tensor(out=vg[:, m], in0=vg[:, m], scalar=rstd[:, 1, m:m + 1], in1=vgain[:],
                                             op0=ALU.mult, op1=ALU.mult).then_inc(sem("v_normalised"), 1)
                    yield
                for m in range(2):
                    for q in range(3):
                        n = A_SG + 3 * m + q
                        filled(dve, n)
                        bias = gains[:, GN_BS + 4 * q:GN_BS + 4 * q + 4]
                        freed(dve.tensor_tensor(by_head(mix[:, m, q * NB:(q + 1) * NB]), by_head(aux[n % 4][:]),
                                                rows(bias, P), ALU.add), n)
                    yield

            def gate(b):
                for m in range(2):
                    dve.wait_ge(result_drained[m], R_GM + 4 + b + 3)
                for m in range(2):
                    if b == 0:
                        for q in range(3):
                            drained(dve, A_SG + 3 * m + q)
                    t = mix[:, m, b * NB:(b + 1) * NB]
                    dve.tensor_tensor(t, t, ug[:, m, b * NB:(b + 1) * NB], ALU.mult).then_inc(sem("gated"), 1)

            def gating(b):
                yield
                gate(b)
                yield

            def out_split():
                for step, pairs in enumerate(MIX_REFILL):
                    if step == 1:
                        gate(1)
                    if step == 8:
                        gate(2)
                        dve.wait_ge(sem("xT_hi_ready"), 92)
                        dve.tensor_tensor(xT_lo[:, 12:16, :], moT[1], xT_hi[:, 12:16, :].bitcast(F32), ALU.subtract
                                          ).then_inc(sem("attention_split"), 1)
                    for p in pairs:
                        operand_lo(A_MIX1 + p, p, None, 80 + 2 * (p + 1) + 4 * (p > 3))
                    yield

            def out_block(n):
                return block_steps(B_OUT[1] + n, lambda: add_result(B_OUT[1] + n, (R_OUT[1] + n) % 2, n))

            beside(mixing(), block_steps(B_GM + 3, lambda: copy_result(B_GM + 3, (R_GM + 3) % 2, 1, q_mem[:, 1, :],
                                                                      N_TOK1)))
            beside(attention(1, A_ATT1), block_steps(B_GM + 4))
            beside(gating(0), block_steps(B_GM + 5))
            beside(out_split(), chain(block_steps(B_GM + 6), out_block(0)))
            for n in (1, 2):
                finish(out_block(n))
            beside(refill(ffn_fill[1], GN_FFN + 16, REFILL, 96, R_FFN[1]),
                   chain(out_block(3), block_steps(B_FFN[1], lambda: relu_result(1, B_FFN[1], R_FFN[1], 0))))
            ffn(1)

            dve.wait_ge(sem("block_squares"), 8)
            dve.tensor_reduce(stat[:, 0], parts[:], AX.X, ALU.add).then_inc(sem("final_sums"), 1)
            dve.wait_ge(sem("gained"), 8)
            norm_known(dve, N_FINAL)
            for half in range(2):
                t = xn_late[:, 1, half * (D // 2):(half + 1) * (D // 2)]
                dve.tensor_scalar(t, t, rstd[:, 0, 1:2], None, ALU.mult).then_inc(sem("output_ready1"), 1)

        @block.gpsimd
        def _(pool):
            def inverse_root(dst, src, width, mult, eps, name, first):
                pool.tensor_scalar(dst, src, mult, eps, ALU.mult, ALU.add).then_inc(sem(name), 1)
                pool.wait_ge(sem(name), first + 1)
                pool.tensor_tensor(dst, dst, neg_half[:, 0:width], ALU.pow).then_inc(sem(name), 1)

            def norm(r, width=D):
                k = r in (N_MEM, N_V)
                for m in range(2):
                    pool.wait_ge(sem(f"squares_summed{m}"), r + 1)
                inverse_root(rstd[:, k], stat[:, k], 2, 1.0 / width, EPS, "rstd_ready", 2 * r)

            pool.memset(neg_half[:], -0.5).then_inc(sem("filled_constants"), 1)
            pool.memset(zeros[:], 0.0).then_inc(sem("filled_constants"), 1)
            pool.wait_ge(sem("filled_constants"), 2)
            norm(N_MEM)
            norm(N_X)
            pool.wait_ge(sem("gate_steps"), 13)
            pool.wait_ge(sem("gate_exps"), 6)
            for hp in range(2):
                drained(pool, A_ATT0 + 10 + hp)

            def deltanet(g, base, rnd):
                fil = lambda n: filled(pool, base + n, rnd)
                have = lambda n: drained(pool, base + n, rnd)
                heads = lambda v: v.unsqueeze(2).broadcast_to([P, 4, P])
                over = lambda v: v.unsqueeze(1).broadcast_to([P, 4, P])
                flat = lambda t: t.rearrange("p m h -> p (m h)")

                def zero(dst):
                    z = zeros[:, 0:dst.shape[2]].unsqueeze(1).broadcast_to([P, dst.shape[1], dst.shape[2]])
                    pool.tensor_tensor(dst, z, z, ALU.add).then_inc(sem("y_zeroed"), 1)

                def decay_operands(f):
                    d, m = f // 2, f % 2
                    c = (C_UP, C_LO)[d]
                    pool.tensor_tensor(g_up[:, f], over(cst[:, c:c + P]), heads(gs[:, 2 * (G_G + m) + d, :]), ALU.mult
                                       ).then_inc(sem("decay_operands"), 1)
                    c = (C_BIGF, C_BIGB)[d]
                    pool.tensor_tensor(g_big[:, f], over(cst[:, c:c + P]), heads(gs[:, 2 * (G_GC + m) + d, :]), ALU.add
                                       ).then_inc(sem("decay_operands"), 1)

                for c in (0, 2 + SEQ):
                    pool.memset(qk_pad[:, :, :, c:c + 2], 0.0).then_inc(sem("padded"), 1)
                pool.tensor_copy(gs[:], gall[:, :, bass.ds(g * 4, 4)]).then_inc(sem("group_gates"), 1)
                pool.wait_ge(sem("group_gates"), g + 1)
                have(DA + 5)
                z = zeros[:, 0:2].unsqueeze(1).broadcast_to([P, 4, 2])
                for c in (0, 2 + SEQ):
                    pool.tensor_tensor(v_pad[:, :, c:c + 2], z, z, ALU.add).then_inc(sem("v_padded"), 1)
                for f in range(4):
                    decay_operands(f)
                for X in range(2):
                    pool.wait_ge(sem("head_sums"), g * 6 + (3 * X + 3))
                    pool.tensor_tensor(flat(rs[:, X]), flat(ss[:, X]), neg_half[:], ALU.pow).then_inc(sem("head_rstd"), 1)
                for d in range(2):
                    for m in range(2):
                        have(DG + 2 * m)
                        have(DG + 2 * m + 1)
                        dst, c = ((XT[:, 0, m], C_M1T), (XL[:, 1, m], C_M1L))[d]
                        n = g * 8 + (4 * d + 2 * m + 1)
                        pool.tensor_tensor(dst, NT[:, d, m], over(cst[:, c:c + P]), ALU.mult).then_inc(sem("x0_pool"), 1)
                        pool.wait_ge(sem("x0_pool"), n)
                        pool.tensor_tensor(dst, dst, over(ident), ALU.add).then_inc(sem("x0_pool"), 1)
                for l, s in enumerate(LEVELS):
                    for d in range(2):
                        if l == 0:
                            zero(Y[:, d].rearrange("p x (two s) -> p (x two) s", s=HALF))
                        else:
                            fil(level_aux(l - 1, d, "YX"))
                            zero(Y[:, d].rearrange("p x (b two s) -> p (x b) two s", two=2, s=s)[:, :, 1, :])
                    if l == 0:
                        for d in range(2):
                            pool.tensor_tensor(kdec[d], kdec[d], heads(gs[:, 2 * (G_EKD + d) + d, :]), ALU.mult
                                               ).then_inc(sem("kdec_done"), 1)
                pool.wait_ge(sem("out_sums"), g * 3 + 3)
                pool.tensor_tensor(flat(rs[:, 2]), flat(ss[:, 2]), neg_half[:], ALU.pow).then_inc(sem("out_rstd"), 1)
                pool.wait_ge(sem("mixed"), g * 2 + 2)

            with pool.Fori(0, 2) as g:
                deltanet(g, A_DN, g * (DN_AUX // 4))
            deltanet(2, A_DN2, 0)

            def square_hidden(layer, half, it, j):
                for m in range(2):
                    pool.wait_ge(result_drained[m], half * 12 + it * 2 + (R_FFN[layer] + j + 3))
                t = relu[:, j].rearrange("p m n -> p (m n)")
                pool.tensor_tensor(t, t, t, ALU.mult).then_inc(sem("squared"), 1)

            def ffn(layer):
                with pool.Fori(0, 2) as half:
                    with pool.Fori(0, 4) as it:
                        for j in range(2):
                            square_hidden(layer, half, it, j)

            norm(N_FFN0)
            ffn(0)
            norm(N_TOK1)
            norm(N_V, MIX)
            norm(N_FFN1)
            ffn(1)
            pool.wait_ge(sem("final_sums"), 1)
            inverse_root(rstd[:, 0], stat[:, 0], 2, 1.0 / D, EPS, "rstd_ready", 2 * N_FINAL)


_INS = ["x", "mem", "mem_norm_g", "tok_norm_g", "dn_w_in", "dn_conv_w", "dn_a_log", "dn_dt_bias", "dn_out_norm_g",
        "gm_w_in", "gm_v_norm_g", "gm_w_s", "gm_b_s", "mem_w_kv", "tok_w_out", "ffn_norm_g", "ffn_w1", "ffn_w2",
        "final_norm_g"]


def kernel(**inputs):
    import concourse.bacc as bacc
    from concourse.bass_utils import run_bass_kernel_spmd

    nc = bacc.Bacc("TRN2", target_bir_lowering=False, num_devices=1)
    arrays, args = {}, {}
    for name in _INS:
        a = np.ascontiguousarray(inputs[name])
        arrays[f"in_{name}"] = a
        args[name] = nc.dram_tensor(f"in_{name}", a.shape, mybir.dt.from_np(a.dtype), kind="ExternalInput").ap()
    arrays["in_consts"] = shape_constants()
    args["consts"] = nc.dram_tensor("in_consts", (P, C_ALL), F32, kind="ExternalInput").ap()
    out = nc.dram_tensor("out_0", (1, SEQ, D), F32, kind="ExternalOutput").ap()
    encoder_trunk(nc, out=out, **args)
    r = run_bass_kernel_spmd(nc, [arrays], core_ids=[0])
    return r.results[0]["out_0"]
```
